# Optimizing a Trainium2 kernel written in Bass

```python
import math
import jax, jax.numpy as jnp
from jax import lax
import numpy as np

D_MODEL = 2048
BATCH = 1
SEQ = 512
DEPTH = 1

GRID_W = 64
ROPE_THETA = 10000.0
Q_BLOCK = 128
EPS = 1e-6

HEAD_DIM = 128
HA = 8
HKV = 2
G_A = HA // HKV

HB = 8
QK_NOPE = 128
QK_ROPE = 64
V_DIM = 128
KV_RANK = 512
QK_B = QK_NOPE + QK_ROPE

W_QA = HA * HEAD_DIM
W_KA = HKV * HEAD_DIM
W_VA = HKV * HEAD_DIM
W_QB = HB * QK_B
W_CKV = KV_RANK
W_KPE = QK_ROPE
W_IN = W_QA + W_KA + W_VA + W_QB + W_CKV + W_KPE

MIX_A = HA * HEAD_DIM
MIX_B = HB * V_DIM
MIX_W = MIX_A + MIX_B

D_FF = 4 * D_MODEL
N_MOD = 6

kernel_name = "hybrid_gqa_mla_axialrope_block"

def rms_norm(x, g):
    xf = x.astype(jnp.float32)
    y = xf * lax.rsqrt(jnp.mean(xf * xf, axis=-1, keepdims=True) + EPS)
    return (y * g.astype(jnp.float32)).astype(x.dtype)

def rope_tables_2d(seq_len, dim):
    rows = seq_len // GRID_W
    r, cl = jnp.meshgrid(jnp.arange(rows), jnp.arange(GRID_W), indexing="ij")
    row = r.reshape(-1).astype(jnp.float32)
    col = cl.reshape(-1).astype(jnp.float32)
    half = dim // 2
    inv = ROPE_THETA ** (-jnp.arange(0, half, 2, dtype=jnp.float32) / half)
    ang_r = row[:, None] * inv[None, :]
    ang_c = col[:, None] * inv[None, :]
    ang = jnp.concatenate([ang_r, ang_r, ang_c, ang_c], axis=-1)
    return jnp.cos(ang), jnp.sin(ang)

def _rotate_half(v):
    h = v.shape[-1] // 2
    return jnp.concatenate([-v[..., h:], v[..., :h]], axis=-1)

def apply_rope_2d(x, cos, sin):
    half = x.shape[-1] // 2
    rot = jnp.concatenate([_rotate_half(x[..., :half]), _rotate_half(x[..., half:])], axis=-1)
    return (x.astype(jnp.float32) * cos + rot.astype(jnp.float32) * sin).astype(x.dtype)

def gqa_blocked(q, k, v):
    B, _, _, S, D = q.shape
    scale = 1.0 / math.sqrt(D)

    def block(i):
        qb = lax.dynamic_slice_in_dim(q, i * Q_BLOCK, Q_BLOCK, axis=3)
        s = jnp.einsum("bkgqd,bksd->bkgqs", qb, k).astype(jnp.float32) * scale
        p = jax.nn.softmax(s, axis=-1).astype(v.dtype)
        return jnp.einsum("bkgqs,bksd->bkgqd", p, v)

    o = lax.map(block, jnp.arange(S // Q_BLOCK))
    o = jnp.transpose(o, (1, 0, 4, 2, 3, 5))
    return o.reshape(B, S, HA * D)

def mla_blocked(q_nope, q_pe, k_nope, k_pe, v):
    B, H, S, _ = q_nope.shape
    scale = 1.0 / math.sqrt(QK_B)

    def block(i):
        qn = lax.dynamic_slice_in_dim(q_nope, i * Q_BLOCK, Q_BLOCK, axis=2)
        qp = lax.dynamic_slice_in_dim(q_pe, i * Q_BLOCK, Q_BLOCK, axis=2)
        s = (jnp.einsum("bhqd,bhsd->bhqs", qn, k_nope)
             + jnp.einsum("bhqr,bsr->bhqs", qp, k_pe)).astype(jnp.float32) * scale
        p = jax.nn.softmax(s, axis=-1).astype(v.dtype)
        return jnp.einsum("bhqs,bhsd->bhqd", p, v)

    o = lax.map(block, jnp.arange(S // Q_BLOCK))
    o = jnp.transpose(o, (1, 0, 3, 2, 4))
    return o.reshape(B, S, H * V_DIM)

def setup_inputs(seed: int = 0) -> dict:
    key = jax.random.key(seed)
    ks = jax.random.split(key, 20)
    f = jnp.float32

    def w(k, shape, fan_in):
        return jax.random.normal(k, shape, f) * (fan_in ** -0.5)

    def gain(k, shape):
        return 1.0 + 0.05 * jax.random.normal(k, shape, f)

    L = DEPTH
    return {
        "x": jax.random.normal(ks[0], (BATCH, SEQ, D_MODEL), f),
        "c": jax.random.normal(ks[1], (BATCH, D_MODEL), f),
        "w_ada": w(ks[2], (L, D_MODEL, N_MOD * D_MODEL), D_MODEL),
        "b_ada": 0.02 * jax.random.normal(ks[3], (L, N_MOD * D_MODEL), f),
        "g_pre_attn": gain(ks[4], (L, D_MODEL)),
        "w_in": w(ks[5], (L, D_MODEL, W_IN), D_MODEL),
        "g_q_a": gain(ks[6], (L, HEAD_DIM)),
        "g_k_a": gain(ks[7], (L, HEAD_DIM)),
        "g_ckv": gain(ks[8], (L, KV_RANK)),
        "w_kv_b": w(ks[9], (L, KV_RANK, HB * (QK_NOPE + V_DIM)), KV_RANK),
        "g_out_a": gain(ks[10], (L, MIX_A)),
        "g_out_b": gain(ks[11], (L, MIX_B)),
        "w_out": w(ks[12], (L, MIX_W, D_MODEL), MIX_W),
        "g_post_attn": gain(ks[13], (L, D_MODEL)),
        "g_pre_mlp": gain(ks[14], (L, D_MODEL)),
        "w_mlp_in": w(ks[15], (L, D_MODEL, D_FF), D_MODEL),
        "w_mlp_out": w(ks[16], (L, D_FF, D_MODEL), D_FF),
        "g_post_mlp": gain(ks[17], (L, D_MODEL)),
    }

def reference(x, c, w_ada, b_ada, g_pre_attn, w_in, g_q_a, g_k_a, g_ckv, w_kv_b,
              g_out_a, g_out_b, w_out, g_post_attn, g_pre_mlp, w_mlp_in, w_mlp_out,
              g_post_mlp):
    B, S, _ = x.shape
    cos_a, sin_a = rope_tables_2d(S, HEAD_DIM)
    cos_b, sin_b = rope_tables_2d(S, QK_ROPE)
    c_act = jax.nn.silu(c)

    offs = np.cumsum([0, W_QA, W_KA, W_VA, W_QB, W_CKV, W_KPE])

    for l in range(DEPTH):
        mod = c_act @ w_ada[l] + b_ada[l]
        sh_a, sc_a, gt_a, sh_m, sc_m, gt_m = [m[:, None, :] for m in jnp.split(mod, N_MOD, axis=-1)]

        h = rms_norm(x, g_pre_attn[l]) * (1.0 + sc_a) + sh_a
        proj = h @ w_in[l]
        q_a, k_a, v_a, q_b, ckv, k_pe = [proj[..., offs[i]:offs[i + 1]] for i in range(6)]

        q_a = rms_norm(q_a.reshape(B, S, HA, HEAD_DIM), g_q_a[l]).transpose(0, 2, 1, 3)
        k_a = rms_norm(k_a.reshape(B, S, HKV, HEAD_DIM), g_k_a[l]).transpose(0, 2, 1, 3)
        v_a = v_a.reshape(B, S, HKV, HEAD_DIM).transpose(0, 2, 1, 3)
        q_a = apply_rope_2d(q_a, cos_a, sin_a).reshape(B, HKV, G_A, S, HEAD_DIM)
        k_a = apply_rope_2d(k_a, cos_a, sin_a)
        o_a = gqa_blocked(q_a, k_a, v_a)

        q_b = q_b.reshape(B, S, HB, QK_B).transpose(0, 2, 1, 3)
        q_nope = q_b[..., :QK_NOPE]
        q_pe = apply_rope_2d(q_b[..., QK_NOPE:], cos_b, sin_b)
        kv = rms_norm(ckv, g_ckv[l]) @ w_kv_b[l]
        kv = kv.reshape(B, S, HB, QK_NOPE + V_DIM).transpose(0, 2, 1, 3)
        k_nope, v_b = kv[..., :QK_NOPE], kv[..., QK_NOPE:]
        k_pe = apply_rope_2d(k_pe, cos_b, sin_b)
        o_b = mla_blocked(q_nope, q_pe, k_nope, k_pe, v_b)

        o = jnp.concatenate([rms_norm(o_a, g_out_a[l]), rms_norm(o_b, g_out_b[l])], axis=-1)
        o = o @ w_out[l]
        x = x + gt_a * rms_norm(o, g_post_attn[l])

        h = rms_norm(x, g_pre_mlp[l]) * (1.0 + sc_m) + sh_m
        y = jnp.square(jax.nn.relu(h @ w_mlp_in[l])) @ w_mlp_out[l]
        x = x + gt_m * rms_norm(y, g_post_mlp[l])

    return x


_drawn_inputs = setup_inputs


def setup_inputs(seed=0):
    import zlib

    import numpy as np

    out = dict(_drawn_inputs(seed))
    spreads = {}
    factors = {'g_pre_attn': 7.518,
     'g_q_a': 8.0,
     'g_k_a': 8.0,
     'g_ckv': 3.505,
     'g_out_a': 3.224,
     'g_out_b': 3.352}
    for name, (base, spread) in spreads.items():
        noise = np.random.default_rng([zlib.crc32(name.encode()), seed]).standard_normal(out[name].shape)
        drawn = base * np.exp(spread * noise) if base else spread * noise
        out[name] = __import__('jax').numpy.asarray(drawn.astype(out[name].dtype))
    for name, factor in factors.items():
        out[name] = (out[name] * factor).astype(out[name].dtype)
    return out
```

```python
import math
from contextlib import ExitStack

import numpy as np

import concourse.bass as bass
from concourse import mybir

F32, F32R = mybir.dt.float32, mybir.dt.float32r
ACT, ALU, AX = mybir.ActivationFunctionType, mybir.AluOpType, mybir.AxisListType

P = 128
T = 512
NT = T // P
D = 2048
KD = D // P
COLS = 512
NB = D // COLS
QROWS = 2
RING = 4
HEADS = 8
RANK = 512
KR = RANK // P
ROPE_B = 64
D_FF = 4 * D
GROUPS = 8
FCH = D_FF // GROUPS // P
EPS = 1e-6
SCALE_A = 1.0 / math.sqrt(128)
SCALE_B = 1.0 / math.sqrt(128 + ROPE_B)
SH_A, SC_A, GT_A, SH_M, SC_M, GT_M = [i * D for i in range(6)]

UNITS_D = KD // QROWS
START_RAW, START_W = 2 * UNITS_D + 3, 3
PROJ_RAW = NB * START_RAW
PROJ_W = NB * START_W
PROJ_BLOCKS = 6
KV_RAW = PROJ_RAW + PROJ_BLOCKS * 2 * UNITS_D
KV_W = PROJ_W + PROJ_BLOCKS * UNITS_D
KV_UNITS = 8
OUT_RAW = KV_RAW + 3 * KV_UNITS
OUT_W = KV_W + KV_UNITS
OUT_RAW_N, OUT_W_N = 3 * UNITS_D, UNITS_D
MLP_RAW = OUT_RAW + NB * OUT_RAW_N
MLP_W = OUT_W + NB * OUT_W_N
UP_UNITS, DOWN_UNITS = 2 * UNITS_D, NB * FCH // QROWS
MLP_N = UP_UNITS + DOWN_UNITS
DN_U = FCH // QROWS


class At:

    def __init__(self, const, i=None, per=0):
        assert per % RING == 0
        self.const, self.i, self.per = const, i, per

    def slot(self):
        return self.const % RING

    def count(self, times=1, more=0, each=1):
        fixed = times * (self.const // each) + more
        return fixed if self.i is None else self.i * (times * self.per // each) + fixed

    def plus(self, n):
        return At(self.const + n, self.i, self.per)


class Chain:

    def __init__(self, engine, sem):
        self.engine, self.sem, self.n, self.loop = engine, sem, 0, 0

    def step(self, instruction):
        instruction.then_inc(self.sem, 1)
        self.n += 1
        self.engine.wait_ge(self.sem, self.loop + self.n)

    def enter(self, i, per):
        self.loop, self.at, self.per = i * per, self.n, per

    def leave(self, times):
        assert self.n - self.at == self.per, (self.n - self.at, self.per)
        self.loop, self.n = 0, self.at + times * self.per


def build(nc, a, out, x1_dram):
    with ExitStack() as ctx:
        sem = lambda name: ctx.enter_context(nc.semaphore(name))
        base = 16512
        KB = 1024
        room = ctx.enter_context(nc.sbuf_tensor("room", [P, 53000], F32))

        def sb(name, kb, shape, dtype=F32):
            size = int(np.prod(shape)) * 4
            assert base + int(kb * KB) + size <= 229344, name
            return nc.alloc_sbuf_tensor_at(name, [P] + list(shape), dtype, offset=base + int(kb * KB))

        place = [0.0]

        def small(name, shape):
            t = sb(name, place[0], shape)
            place[0] += math.ceil(int(np.prod(shape)) * 4 / 32) * 32 / KB
            assert place[0] <= 4
            return t

        ident = small("ident", [P])
        rot = small("rot", [P])
        ones = small("ones", [P])
        gains = small("gains", [KD * 3 + 2 * HEADS + KR])
        bias = small("bias", [6 * KD])
        g_q, g_k = sb("g_q", 206, [P]), sb("g_k", 206.5, [P])
        silu_c = small("silu_c", [KD])
        silu_t = small("silu_t", [KD])
        gsc_a = small("gsc_a", [2, 4])
        shf_a = small("shf_a", [2, 4])
        mod_m = small("mod_m", [2 * KD])
        gsc_m = small("gsc_m", [KD])
        shf_m = small("shf_m", [KD])
        stat = small("stat", [NT, 4])
        stat_v = small("stat_v", [NT, 4])
        stat_s = small("stat_s", [NT, 4])
        rstd = small("rstd", [NT, 4])
        top = small("top", [NT])
        nbias = small("nbias", [NT])
        total = small("total", [NT])
        rtotal = small("rtotal", [NT])
        r_out = small("r_out", [2, NT])
        row_sq = small("row_sq", [NT, NB])
        raw = [sb(f"raw{i}", 4 + 4 * i, [QROWS, COLS]) for i in range(RING)]
        hi = [sb(f"hi{i}", 20 + 4 * i, [QROWS, COLS], F32R) for i in range(RING)]
        lo = [sb(f"lo{i}", 36 + 4 * i, [QROWS, COLS], F32R) for i in range(RING)]
        x_tok = sb("x_tok", 52, [NT, D])
        h_hi, h_lo = sb("h_hi", 52, [KD, T], F32R), sb("h_lo", 84, [KD, T], F32R)
        prob = sb("prob", 52, [NT, T])
        head_raw = {n: sb(f"{n}_raw", kb, [T]) for n, kb in (("k", 60), ("v", 62), ("o", 178))}
        k_nope = sb("k_nope", 68, [HEADS, T])
        v_lat = sb("v_lat", 84, [NT, HEADS, P])
        stage = {}
        for n, name in enumerate(("q", "k", "v", "qr")):
            stage[name] = (sb(f"{name}_hi", 100 + 4 * n, [T], F32R), sb(f"{name}_lo", 102 + 4 * n, [T], F32R))
        o_hi, o_lo = sb("o_hi", 52, [KD, T], F32R), sb("o_lo", 84, [KD, T], F32R)
        h2_hi, h2_lo = sb("h2_hi", 52, [KD, T], F32R), sb("h2_lo", 84, [KD, T], F32R)
        x1_back = sb("x1_back", 52, [NT, D])
        y_junk = sb("y_junk", 84, [D])
        x_t = sb("x_t", 116, [KD, T])
        q_o = sb("q_o", 116, [2 * HEADS, T])
        z_tok = sb("z_tok", 116, [NT, D])
        y_acc = sb("y_acc", 116, [NT, D])
        q_rot = sb("q_rot", 148, [HEADS // 2, T])
        k_gqa = sb("k_gqa", 156, [2, T])
        v_gqa = sb("v_gqa", 160, [NT, 2, P])
        kr_hi, kr_lo = sb("kr_hi", 164, [2, T], F32R), sb("kr_lo", 168, [2, T], F32R)
        ckv = sb("ckv", 172, [KR, T])
        sq = sb("sq", 172, [T])
        sq_sum = sb("sq_sum", 174, [2, T])
        x_res = sb("x_res", 148, [NT, D])
        y_hi, y_lo = sb("y_hi", 148, [FCH, T], F32R), sb("y_lo", 164, [FCH, T], F32R)
        mod_acc = [sb(f"mod_acc{i}", 180 + 2 * i, [COLS]) for i in range(3)]
        tab_b = sb("tab_b", 184, [2, NT, ROPE_B])
        tab_a = sb("tab_a", 186, [2, NT, P])
        tab_g = sb("tab_g", 190, [2, NT, P])
        tab_t = sb("tab_t", 190, [2, T])
        tok = sb("tok", 194, [NT, COLS])
        vec_rows = sb("vec_rows", 194, [2, P])
        tmp = [sb(f"tmp{i}", 202 + 2 * i, [COLS]) for i in range(2)]
        c_hi, c_lo = sb("c_hi", 186, [KR, T], F32R), sb("c_lo", 194, [KR, T], F32R)
        pt_hi, pt_lo = sb("pt_hi", 186, [NT, T], F32R), sb("pt_lo", 194, [NT, T], F32R)
        ga_acc = sb("ga_acc", 202, [2, COLS])
        gm_acc = sb("gm_acc", 180, [D])
        part = sb("part", 188, [NT, COLS])
        comb = sb("comb", 196, [COLS])
        rows = sb("rows", 198, [2, COLS])
        tmp_u = [sb(f"tmp_u{i}", 188 + 2 * i, [T]) for i in range(2)]
        tmp_y = [sb(f"tmp_y{i}", 192 + 2 * i, [T]) for i in range(2)]

        bank = [ctx.enter_context(nc.psum_tensor(f"bank{i}", [P, COLS], F32)) for i in range(8)]
        sets = (bank[0:4], bank[4:8])

        w_ada = a["w_ada"].rearrange("l (u q p) n -> (l u) p q n", q=QROWS, p=P)
        w_in = a["w_in"].rearrange("l (u q p) n -> (l u) p q n", q=QROWS, p=P)
        w_in4 = a["w_in"].rearrange("l (u q p) n -> (l u) p q n", q=4, p=P)
        w_kv = a["w_kv_b"].rearrange("l (u q p) (h e) -> (l u) p q h e", q=QROWS, p=P, h=HEADS)
        w_out = a["w_out"].rearrange("l (u q p) n -> (l u) p q n", q=QROWS, p=P)
        w_up = a["w_mlp_in"].rearrange("l (u q p) n -> (l u) p q n", q=QROWS, p=P)
        w_dn = a["w_mlp_out"].rearrange("l (u q p) n -> (l u) p q n", q=QROWS, p=P)
        x_d = a["x"].rearrange("b (t p) d -> (b t) p d", p=P)
        out_d = out.rearrange("b (t p) d -> (b t) p d", p=P)
        x1_d = x1_dram.rearrange("(t p) d -> t p d", p=P)
        b_rows = a["b_ada"]

        raw_landed = [sem(f"raw_landed{i}") for i in range(RING)]
        raw_used = sem("raw_used")
        hi_ready = sem("hi_ready")
        w_used = sem("w_used")
        x_landed = [sem(f"x_landed{i}") for i in range(NT)]
        vec_landed, const_landed, tab_landed = sem("vec_landed"), sem("const_landed"), sem("tab_landed")
        ones_ready = sem("ones_ready")
        dve_own, act_own, pool_own, pe_own = sem("dve_own"), sem("act_own"), sem("pool_own"), sem("pe_own")
        vec_turned, vec_ready, exp_c, silu_ready = sem("vec_turned"), sem("vec_ready"), sem("exp_c"), sem("silu_ready")
        x_sq, x_var, x_sqrt, x_normed, x_turned, x_t_ready = [sem(f"x_{n}") for n in ("sq", "var", "sqrt", "normed", "turned", "t_ready")]
        mod_summed, mod_reduced, mod_read = sem("mod_summed"), sem("mod_reduced"), sem("mod_read")
        h_tmp, h_hi_ready, h_ready = sem("h_tmp"), sem("h_hi_ready"), sem("h_ready")
        copied = sem("copied")
        c_sq, kr_copied, kr_turned, kr_sum, kr_hi_done, kr_ready = [sem(n) for n in ("c_sq", "kr_copied", "kr_turned", "kr_sum", "kr_hi_done", "kr_ready")]
        var_ready, sqrt_ready, rstd_ready, tok_ready = sem("var_ready"), sem("sqrt_ready"), sem("rstd_ready"), sem("tok_ready")
        turned, turned_out = sem("turned"), sem("turned_out")
        c_hi_done, c_ready = sem("c_hi_done"), sem("c_ready")
        q_hi_done, q_ready, k_ready, v_ready = sem("q_hi_done"), sem("q_ready"), sem("k_ready"), sem("v_ready")
        s_done, nb_ready, exp_done, p_ready, p_turned, pt_hi_done, pt_done, pv_done, o_done = [
            sem(n) for n in ("s_done", "nb_ready", "exp_done", "p_ready", "p_turned", "pt_hi_done", "pt_done", "pv_done", "o_done")]
        sq_ready, sq_reduced, r_var, r_sqrt, r_ready, r_free = [sem(n) for n in ("sq_ready", "sq_reduced", "r_var", "r_sqrt", "r_ready", "r_free")]
        o_hi_done, o_ready = sem("o_hi_done"), sem("o_ready")
        a_out, b_out, z_done, row_done = sem("a_out"), sem("b_out"), sem("z_done"), sem("row_done")
        ga_summed, ga_reduced, comb_ready, rows_landed = sem("ga_summed"), sem("ga_reduced"), sem("comb_ready"), sem("rows_landed")
        res_landed, x1_var, x1_sqrt, x1_ready, x1_sq, xn_ready, xn_turned = [
            sem(n) for n in ("res_landed", "x1_var", "x1_sqrt", "x1_ready", "x1_sq", "xn_ready", "xn_turned")]
        gm_reduced, gm_copied, comb_m_ready, x1_saved = sem("gm_reduced"), sem("gm_copied"), sem("comb_m_ready"), sem("x1_saved")
        h2_tmp, h2_hi_done, h2_ready = sem("h2_tmp"), sem("h2_hi_done"), sem("h2_ready")
        relu_done, y_done, y_hi_done, y_ready, mlp_free = sem("relu_done"), sem("y_done"), sem("y_hi_done"), sem("y_ready"), sem("mlp_free")
        y_sq, y_var, y_sqrt, x1_landed, out_ready, out_saved = [sem(n) for n in ("y_sq", "y_var", "y_sqrt", "x1_landed", "out_ready", "out_saved")]

        q_b = a["w_in"].rearrange("l (u q p) n -> (l u) p q n", q=QROWS, p=P)[:, :, :, 1536:3072].rearrange(
            "u p q (h e) -> u p q h e", h=HEADS)
        PROJ = [3072, 1024, 0, 512, "rot", "plain0", "plain1"]
        TOKENS_OUT = [True, True, True, True, True, False, False]
        TURNS = [4, 2, 4, 4, 4, 0, 0]
        STATS = {1: 1, 2: 2, 3: 4, 4: 4}
        TURNS_SUM = [int(np.sum(TURNS[:b])) for b in range(len(TURNS) + 1)]

        block = ctx.enter_context(nc.Block())

        @block.sync
        def _(sp):
            def load(at, source, n=COLS * QROWS, shape=None):
                if at.i is not None or at.const >= RING:
                    sp.wait_ge(raw_used, at.count(1, 1 - RING))
                dst = raw[at.slot()][:, :, :]
                if shape:
                    dst = dst.rearrange("p q n -> p (q n)")[:, 0:n].rearrange(*shape[0], **shape[1])
                sp.dma_start(dst, source).then_inc(raw_landed[at.slot()], 16)

            def ada(at, j, col):
                load(at, w_ada[j, :, :, bass.ds(col, COLS)])

            r = 0
            for name, n in (("c", KD), ("g_pre_attn", KD), ("g_pre_mlp", KD), ("g_out_a", HEADS), ("g_out_b", HEADS), ("g_ckv", KR)):
                sp.dma_start(vec_rows[r:r + n, 0, :], a[name].rearrange("l (k p) -> (l k) p", p=P)).then_inc(vec_landed, 16)
                r += n
            sp.dma_start(vec_rows[0:6 * KD, 1, :], a["b_ada"].rearrange("l (k p) -> (l k) p", p=P)).then_inc(vec_landed, 16)
            sp.dma_start(ident[:], a["ident"]).then_inc(const_landed, 16)
            for cb in range(NB):
                r = START_RAW * cb
                for g, col in enumerate((SC_A, SH_A)):
                    for j in range(UNITS_D):
                        ada(At(r + g * UNITS_D + j), j, col + COLS * cb)
                r += 2 * UNITS_D
                for j in range(2):
                    load(At(r + j), w_in[2 * cb + j, :, :, PROJ[0]:PROJ[0] + COLS])
                load(At(r + 2), w_in4[cb, :, :, 3584:3584 + ROPE_B], 4 * ROPE_B, (("p (q n) -> p q n",), {"q": 4}))
            for b in range(1, PROJ_BLOCKS + 1):
                for j in range(UNITS_D):
                    r = PROJ_RAW + 2 * UNITS_D * (b - 1) + 2 * j
                    if PROJ[b] == "rot":
                        at = At(r)
                        sp.wait_ge(raw_used, at.count(1, 1 - RING))
                        for q in range(QROWS):
                            sp.dma_start(raw[at.slot()][:, q, :].rearrange("p (h e) -> p h e", h=HEADS),
                                         q_b[j, :, q, :, P:P + ROPE_B]).then_inc(raw_landed[at.slot()], 16)
                    elif isinstance(PROJ[b], str):
                        at = At(r)
                        sp.wait_ge(raw_used, at.count(1, 1 - RING))
                        h0 = 4 * int(PROJ[b][-1])
                        for q in range(QROWS):
                            sp.dma_start(raw[at.slot()][:, q, :].rearrange("p (h e) -> p h e", h=4),
                                         q_b[j, :, q, h0:h0 + 4, 0:P]).then_inc(raw_landed[at.slot()], 16)
                    else:
                        load(At(r), w_in[j, :, :, PROJ[b]:PROJ[b] + COLS])
                    ada(At(r + 1), j, SC_M + COLS * (b - 1) if b <= 4 else SH_M + COLS * (b - 5))
            for j in range(KV_UNITS):
                at = At(KV_RAW + 3 * j)
                sp.wait_ge(raw_used, at.count(1, 1 - RING))
                blk, u = j // 2, j % 2
                for q in range(QROWS):
                    src = w_kv[u, :, q, 4 * (blk % 2):4 * (blk % 2) + 4, P * (blk // 2):P * (blk // 2) + P]
                    sp.dma_start(raw[at.slot()][:, q, :].rearrange("p (h e) -> p h e", h=4), src).then_inc(raw_landed[at.slot()], 16)
                for m in range(2):
                    g, jj = divmod(2 * j + m, UNITS_D)
                    ada(At(KV_RAW + 3 * j + 1 + m), jj, SH_M + COLS * (2 + g))
            with sp.Fori(0, NB) as n:
                for j in range(UNITS_D):
                    at = At(OUT_RAW + 3 * j, n, OUT_RAW_N)
                    load(at, w_out[j, :, :, bass.ds(n * COLS, COLS)])
                    for m in range(2):
                        ada(at.plus(1 + m), 2 * (j % 4) + m, n * COLS + (GT_A if j < 4 else GT_M))
            with sp.Fori(0, GROUPS) as g:
                at = At(MLP_RAW, g, MLP_N)
                for f in range(2):
                    for j in range(UNITS_D):
                        load(at.plus(f * UNITS_D + j), w_up[j, :, :, bass.ds(g * (FCH * P) + f * COLS, COLS)])
                for n in range(NB):
                    for j in range(DN_U):
                        load(at.plus(UP_UNITS + n * DN_U + j), w_dn[g * DN_U + j, :, :, n * COLS:(n + 1) * COLS])
            sp.wait_ge(w_used, MLP_W + MLP_N * (GROUPS - 1) + UP_UNITS)
            sp.wait_ge(x1_saved, 16 * NT)
            for t in range(NT):
                sp.dma_start(x1_back[:, t, :], x1_d[t]).then_inc(x1_landed, 16)
            for t in range(NT):
                sp.wait_ge(out_ready, t + 1)
                sp.dma_start(out_d[t], x1_back[:, t, :]).then_inc(out_saved, 16)
            sp.wait_ge(out_saved, 16 * NT)

        landings = [0] * RING
        landed_at = {}
        for r in range(OUT_RAW):
            two = (KV_RAW <= r and (r - KV_RAW) % 3 == 0) or (
                PROJ_RAW <= r < KV_RAW and (r - PROJ_RAW) % 2 == 0 and isinstance(PROJ[1 + (r - PROJ_RAW) // (2 * UNITS_D)], str))
            landings[r % RING] += 32 if two else 16
            landed_at[r] = landings[r % RING]

        def wait_raw(engine, at):
            if at.const < OUT_RAW:
                assert at.i is None
                value = landed_at[at.const]
            else:
                slot = at.slot()
                before = landings[slot]
                nth = At(at.const - OUT_RAW, at.i, at.per)
                value = nth.count(16, before + 16, RING)
            engine.wait_ge(raw_landed[at.slot()], value)

        def stage_w(r, w):
            return r, w

        def at_out(n, j):
            if isinstance(n, int):
                return At(OUT_RAW + OUT_RAW_N * n + 3 * j), At(OUT_W + OUT_W_N * n + j)
            return At(OUT_RAW + 3 * j, n, OUT_RAW_N), At(OUT_W + j, n, OUT_W_N)

        def at_mlp(g, j):
            if isinstance(g, int):
                return At(MLP_RAW + MLP_N * g + j), At(MLP_W + MLP_N * g + j)
            return At(MLP_RAW + j, g, MLP_N), At(MLP_W + j, g, MLP_N)

        @block.scalar
        def _(act):
            own = Chain(act, act_own)

            def split_hi(r, w, pairs=None):
                wait_raw(act, r)
                if w.i is not None or w.const >= RING:
                    act.wait_ge(w_used, w.count(1, 1 - RING))
                for dst, src in (pairs or [(hi[w.slot()][:], raw[r.slot()][:])]):
                    ins = nc.scalar.activation(dst, src, ACT.Copy)
                ins.then_inc(hi_ready, 1)

            def proj_at(b, j):
                return At(PROJ_RAW + 2 * UNITS_D * (b - 1) + 2 * j), At(PROJ_W + UNITS_D * (b - 1) + j)

            for t in range(NT):
                act.dma_start(x_tok[:, t, :], x_d[t]).then_inc(x_landed[t], 16)
            act.dma_start(rot[:], a["rot"]).then_inc(tab_landed, 16)
            act.dma_start(tab_t[:], a["tab_t"]).then_inc(tab_landed, 16)
            act.dma_start(tab_a[:], a["tab_a"]).then_inc(tab_landed, 16)
            act.dma_start(tab_b[:], a["tab_b"]).then_inc(tab_landed, 16)
            act.dma_start(g_q[:], a["g_q_a"].partition_broadcast(P)[:, 0, :]).then_inc(tab_landed, 16)
            act.dma_start(g_k[:], a["g_k_a"].partition_broadcast(P)[:, 0, :]).then_inc(tab_landed, 16)
            act.wait_ge(vec_ready, 2)
            nc.scalar.activation(silu_t[:], gains[:, 0:KD], ACT.Exp, scale=-1.0).then_inc(exp_c, 1)
            for t in range(NT):
                act.wait_ge(x_landed[t], 16)
                nc.scalar.activation(x_t[:, 4 * t:4 * t + 4, :].rearrange("p k n -> p (k n)"), x_tok[:, t, :], ACT.Square,
                                         accum_out=stat[:, t, 0:1]).then_inc(x_sq, 1)
            act.wait_ge(x_var, 1)
            nc.scalar.activation(stat_s[:, :, 0:1], stat_v[:, :, 0:1], ACT.Sqrt).then_inc(x_sqrt, 1)
            for k in range(KD):
                act.wait_ge(x_turned, k + 1)
                nc.scalar.activation(x_t[:, k, :], bank[k % 4][:], ACT.Copy).then_inc(x_t_ready, 1)
            for cb in range(NB):
                for j in range(4):
                    act.wait_ge(h_tmp, 4 * cb + j + 1)
                    nc.scalar.activation(h_hi[:, 4 * cb + j, :], tmp[j % 2][:], ACT.Copy).then_inc(h_hi_ready, 1)
                r, w = START_RAW * cb + 2 * UNITS_D, START_W * cb
                for j in range(2):
                    split_hi(At(r + j), At(w + j))
                s = At(w + 2).slot()
                dup = hi[s][:].rearrange("p q n -> p (q n)")[:, 0:4 * P].rearrange("p (k m e) -> p k m e", k=4, m=2)
                src = raw[At(r + 2).slot()][:].rearrange("p q n -> p (q n)")[:, 0:4 * ROPE_B].rearrange("p (k e) -> p k e", k=4)
                split_hi(At(r + 2), At(w + 2), [(dup[:, :, m, :], src) for m in range(2)])

            def copy_out(b):
                s = sets[b % 2]
                if b == 0:
                    for t in range(NT):
                        nc.scalar.activation(tok[:, t, :], s[t][:], ACT.Square, accum_out=stat[:, t, 0:1]).then_inc(c_sq, 1)
                elif b == 1:
                    for t in range(NT):
                        nc.scalar.activation(tok[:, t, 0:2 * P], s[t][:, 0:2 * P], ACT.Copy)
                        nc.scalar.activation(v_gqa[:, t, :, :].rearrange("p g e -> p (g e)"), s[t][:, 2 * P:4 * P], ACT.Copy).then_inc(copied, 1)
                elif b <= 4:
                    for t in range(NT):
                        nc.scalar.activation(tok[:, t, :], s[t][:], ACT.Copy).then_inc(copied, 1)
                elif b <= 6:
                    for n in range(4):
                        nc.scalar.activation(q_o[:, HEADS + 4 * (b - 5) + n, :], s[n][:], ACT.Copy).then_inc(copied, 1)
                elif b <= 8:
                    for n in range(4):
                        nc.scalar.activation(k_nope[:, 4 * (b - 7) + n, :], s[n][:], ACT.Copy).then_inc(copied, 1)
                else:
                    for t in range(NT):
                        dst = v_lat[:, t, 4 * (b - 9):4 * (b - 9) + 4, :].rearrange("p h e -> p (h e)")
                        nc.scalar.activation(dst, s[t][:], ACT.Copy).then_inc(copied, 1)

            def turned_copy(b):
                for n in range(TURNS[b]):
                    act.wait_ge(turned, TURNS_SUM[b] + n + 1)
                    src = sets[b % 2][n][:]
                    if b == 0:
                        k = 3 * KD + 2 * HEADS + n
                        nc.scalar.activation(ckv[:, n, :], src, ACT.Copy, scale=gains[:, k:k + 1]).then_inc(turned_out, 1)
                    elif b == 1:
                        nc.scalar.activation(k_gqa[:, n, :], src, ACT.Copy).then_inc(turned_out, 1)
                    elif b <= 3:
                        nc.scalar.activation(q_o[:, 4 * (b - 2) + n, :], src, ACT.Copy).then_inc(turned_out, 1)
                    else:
                        nc.scalar.activation(q_rot[:, n, :], src, ACT.Copy).then_inc(turned_out, 1)

            roots = 0
            for b in range(1, PROJ_BLOCKS + 1):
                for j in range(UNITS_D):
                    split_hi(*proj_at(b, j))
                    if b == 1 and j == 0:
                        act.wait_ge(w_used, PROJ_W)
                        nc.scalar.activation(tmp[0][:], bank[4][:], ACT.Copy).then_inc(kr_copied, 1)
                    if j == 2 and b >= 2:
                        turned_copy(b - 2)
                    if j == 3:
                        if b >= 2:
                            act.wait_ge(w_used, PROJ_W + UNITS_D * (b - 1))
                            if b <= 5 :
                                act.wait_ge(turned, TURNS_SUM[b - 1])
                        copy_out(b - 1)
                    if j == 4 and b in (1, 2, 3, 4):
                        roots += 1
                        act.wait_ge(var_ready, roots)
                        n = STATS[b]
                        nc.scalar.activation(stat_s[:, :, 0:n], stat_v[:, :, 0:n], ACT.Sqrt).then_inc(sqrt_ready, 1)
                    if j == 5 and b == 1:
                        act.wait_ge(rstd_ready, 1)
                        for t in range(NT):
                            nc.scalar.activation(tok[:, t, :], sets[0][t][:], ACT.Copy, scale=rstd[:, t, 0:1]).then_inc(copied, 1)
                    if j == 7 and b == 1:
                        act.wait_ge(kr_sum, 1)
                        nc.scalar.activation(kr_hi[0:64, 0, :], tmp[0][0:64, :], ACT.Copy)
                        nc.scalar.activation(kr_hi[64:128, 1, :], tmp[0][64:128, :], ACT.Copy).then_inc(kr_hi_done, 1)
                    if j == 5 and b == 6:
                        act.wait_ge(turned_out, TURNS_SUM[1])
                        act.wait_ge(tok_ready, 4 * 4)
                        act.wait_ge(turned, TURNS_SUM[5])
                        for k in range(KR):
                            nc.scalar.activation(c_hi[:, k, :], ckv[:, k, :], ACT.Copy).then_inc(c_hi_done, 1)
            for j in range(KV_UNITS):
                split_hi(At(KV_RAW + 3 * j), At(KV_W + j))
                if j % 2 and j >= 3:
                    b = 6 + (j - 3) // 2
                    act.wait_ge(w_used, KV_W if b == 6 else KV_W + 2 * (b - 6))
                    copy_out(b)
            def out_his(n, js):
                for j in js:
                    split_hi(*at_out(n, j))
            for b in (9, 10):
                if b == 9:
                    split_hi(*at_out(0, 0))
                    split_hi(*at_out(0, 1))
                act.wait_ge(w_used, KV_W + 2 * (b - 6))
                copy_out(b)
            split_hi(*at_out(0, 2))
            split_hi(*at_out(0, 3))

            def q_stage(grp, h, H):
                if not (isinstance(H, int) and H == 0):
                    act.wait_ge(s_done, H * 4)
                src = q_o[:, grp * HEADS + h, :] if isinstance(h, int) else q_o[:, bass.ds(h + grp * HEADS, 1), :].rearrange("p a n -> p (a n)")
                ins = nc.scalar.activation(stage["q"][0][:], src, ACT.Copy)
                if grp:
                    ins = nc.scalar.activation(stage["qr"][0][:], q_rot[:, bass.ds(h // 2, 1), :].rearrange("p a n -> p (a n)"), ACT.Copy)
                ins.then_inc(q_hi_done, 1)

            def exp(grp, t, H):
                act.wait_ge(nb_ready, H * 4 + (t + 1))
                nc.scalar.activation(prob[:, t, :], bank[t][:], ACT.Exp, bias=nbias[:, t:t + 1],
                                     scale=SCALE_B if grp else SCALE_A, accum_out=total[:, t:t + 1]).then_inc(exp_done, 1)

            def attend(H, nxt, first=False):
                if nxt:
                    q_stage(*nxt)
                for t in range(NT):
                    act.wait_ge(p_turned, H * 4 + (t + 1))
                    if t == 0:
                        act.wait_ge(pv_done, H)
                    nc.scalar.activation(pt_hi[:, :, t * P:(t + 1) * P], bank[4 + t % 2][:].rearrange("p (c n) -> p c n", c=NT), ACT.Copy).then_inc(pt_hi_done, 1)
                    if nxt:
                        exp(nxt[0], t, nxt[2])
                    if t == 0 and not first:
                        head_out(H)

            def head_out(H):
                act.wait_ge(pv_done, H)
                nc.scalar.activation(q_o[:, bass.ds(H - 1, 1), :].rearrange("p a n -> p (a n)"), bank[6][:], ACT.Copy).then_inc(o_done, 1)

            q_stage(0, 0, 0)
            for t in range(NT):
                exp(0, t, 0)
            attend(0, (0, 1, 1), first=True)
            with act.Fori(1, HEADS - 1) as h:
                attend(h, (0, h + 1, h + 1))
            attend(HEADS - 1, (1, 0, HEADS))
            with act.Fori(0, HEADS - 1) as h:
                attend(h + HEADS, (1, h + 1, h + (HEADS + 1)))
            attend(2 * HEADS - 1, None)
            head_out(2 * HEADS)

            act.wait_ge(s_done, 4 * 2 * HEADS)
            act.wait_ge(pt_done, 4 * 2 * HEADS + 2)
            for k in range(KD):
                if k == KD - 1:
                    act.wait_ge(o_done, 2 * HEADS)
                nc.scalar.activation(o_hi[:, k, :], q_o[:, k, :], ACT.Copy, scale=gains[:, 3 * KD + k:3 * KD + k + 1]).then_inc(o_hi_done, 1)
            act.wait_ge(r_var, 1)
            nc.scalar.activation(stat_s[:, 0:2, :], stat_v[:, 0:2, :], ACT.Sqrt).then_inc(r_sqrt, 1)

            def a_part(n):
                act.wait_ge(r_ready, 1)
                if isinstance(n, int):
                    act.wait_ge(w_used, OUT_W + OUT_W_N * n + 4)
                else:
                    act.wait_ge(w_used, n * OUT_W_N + (OUT_W + 4))
                act.wait_ge(z_done, n * 4)
                for t in range(NT):
                    nc.scalar.activation(part[:, t, :], bank[t][:], ACT.Copy, scale=r_out[:, 0, t:t + 1]).then_inc(a_out, 1)

            def squares(n):
                for t in range(NT):
                    act.wait_ge(z_done, n * 4 + (t + 1))
                    dst = row_sq[:, t, bass.ds(n, 1)]
                    nc.scalar.activation(part[:, t, :], part[:, t, :], ACT.Square, accum_out=dst).then_inc(row_done, 1)

            with act.Fori(0, NB - 1) as n:
                out_his(n, range(4, 8))
                a_part(n)
                for j in range(4):
                    split_hi(At(OUT_RAW + OUT_RAW_N + 3 * j, n, OUT_RAW_N), At(OUT_W + OUT_W_N + j, n, OUT_W_N))
                squares(n)
            out_his(NB - 1, range(4, 8))
            a_part(NB - 1)
            for j in range(4):
                split_hi(*at_mlp(0, j))
            squares(NB - 1)

            act.wait_ge(x1_var, 1)
            nc.scalar.activation(stat_s[:, :, 0:1], stat_v[:, :, 0:1], ACT.Sqrt).then_inc(x1_sqrt, 1)
            act.wait_ge(gm_reduced, 1)
            for n in range(NB):
                nc.scalar.activation(gm_acc[:, n * COLS:(n + 1) * COLS], bank[4 + n][:], ACT.Copy).then_inc(gm_copied, 1)
            for t in range(NT):
                act.wait_ge(x1_ready, t + 1)
                act.dma_start(x1_d[t], x_res[:, t, :]).then_inc(x1_saved, 16)
                nc.scalar.activation(z_tok[:, t, :], x_res[:, t, :], ACT.Square, accum_out=stat[:, t, 1:2]).then_inc(x1_sq, 1)
                act.wait_ge(x1_var, t + 2)
                nc.scalar.activation(stat_s[:, t, 1:2], stat_v[:, t, 1:2], ACT.Sqrt).then_inc(x1_sqrt, 1)
            for k in range(KD):
                act.wait_ge(h2_tmp, k + 1)
                nc.scalar.activation(h2_hi[:, k, :], tmp_u[k % 2][:], ACT.Copy).then_inc(h2_hi_done, 1)

            def relu_square(g, f):
                n0 = f * 4
                def relu(c):
                    nc.scalar.activation(tmp_u[c % 2][:], sets[f][c][:], ACT.Relu).then_inc(relu_done, 1)
                def square_hi(c):
                    act.wait_ge(y_done, g * FCH + (n0 + c + 1))
                    nc.scalar.activation(y_hi[:, n0 + c, :], tmp_y[c % 2][:], ACT.Copy).then_inc(y_hi_done, 1)
                relu(0)
                relu(1)
                for c in range(4):
                    square_hi(c)
                    if c + 2 < 4:
                        relu(c + 2)

            def mlp_group(g, first):
                for j in range(4 if first else 0, MLP_N):
                    r, w = at_mlp(g, j)
                    split_hi(r, w)
                    if j == UNITS_D + 3:
                        act.wait_ge(w_used, w.count(1, 1 - 4))
                        act.wait_ge(y_ready, g * FCH)
                        relu_square(g, 0)
                    if j == UP_UNITS + 3:
                        act.wait_ge(w_used, w.count(1, 1 - 4))
                        relu_square(g, 1)

            act.wait_ge(x1_saved, 16 * NT)
            mlp_group(0, True)
            with act.Fori(1, GROUPS) as g:
                mlp_group(g, False)
            for t in range(NT):
                act.wait_ge(mlp_free, 4 * (6 * GROUPS) + 4)
                act.wait_ge(y_sq, t)
                nc.scalar.activation(y_junk[:], y_acc[:, t, :], ACT.Square, accum_out=stat[:, t, 2:3]).then_inc(y_sq, 1)
            act.wait_ge(y_var, 1)
            nc.scalar.activation(stat_s[:, :, 2:3], stat_v[:, :, 2:3], ACT.Sqrt).then_inc(y_sqrt, 1)

        @block.vector
        def _(dve):
            own = Chain(dve, dve_own)
            tt, ts, stt = nc.vector.tensor_tensor, nc.vector.tensor_scalar, nc.vector.scalar_tensor_tensor

            def split_lo(r, w, pairs=None):
                dve.wait_ge(hi_ready, w.count(1, 1))
                for dst, src, high in (pairs or [(lo[w.slot()][:], raw[r.slot()][:], hi[w.slot()][:])]):
                    ins = tt(dst, src, high.bitcast(F32), ALU.subtract)
                ins.then_inc(raw_used, 1)

            def modulate(at, j, acc, done=None):
                wait_raw(dve, at)
                for q in range(QROWS):
                    k = QROWS * j + q
                    w = raw[at.slot()][:, q, :]
                    if k == 0:
                        ins = ts(acc, w, silu_c[:, 0:1], None, ALU.mult)
                    else:
                        ins = stt(acc, w, silu_c[:, k:k + 1], acc, ALU.mult, ALU.add)
                    if q == QROWS - 1:
                        ins.then_inc(raw_used, 1)
                        dve.wait_ge(raw_used, at.count(1, 1))
                    else:
                        own.step(ins)

            def rsqrt_tail(dst, src):
                own.step(nc.vector.reciprocal(dst, src))

            for n, dst in ((0, gains), (1, bias)):
                dve.wait_ge(vec_turned, n + 1)
                width = 3 * KD + 2 * HEADS + KR if n == 0 else 6 * KD
                nc.vector.tensor_copy(dst[:], bank[4 + n][:, 0:width]).then_inc(vec_ready, 1)
            dve.wait_ge(exp_c, 1)
            own.step(ts(silu_t[:], silu_t[:], 1.0, None, ALU.add))
            own.step(nc.vector.reciprocal(silu_t[:], silu_t[:]))
            own.step(tt(silu_c[:], gains[:, 0:KD], silu_t[:], ALU.mult))

            def start_units(cb, g):
                acc = mod_acc[g][:]
                for j in range(UNITS_D):
                    modulate(At(START_RAW * cb + UNITS_D * g + j), j, acc)
                dve.sem_inc(mod_summed, 1)

            dve.wait_ge(x_sq, NT)
            ts(stat_v[:, :, 0:1], stat[:, :, 0:1], 1.0 / D, EPS, ALU.mult, ALU.add).then_inc(x_var, 1)
            dve.wait_ge(x_sqrt, 1)
            own.step(nc.vector.reciprocal(rstd[:, :, 0:1], stat_s[:, :, 0:1]))
            for t in range(NT):
                ts(x_tok[:, t, :], x_tok[:, t, :], rstd[:, t, 0:1], None, ALU.mult).then_inc(x_normed, 1)

            for cb in range(NB):
                start_units(cb, 0)
                start_units(cb, 1)
                dve.wait_ge(mod_reduced, cb + 1)
                s = cb % 2
                own.step(tt(gsc_a[:, s, :], bank[5][:, 0:4], bias[:, KD + 4 * cb:KD + 4 * cb + 4], ALU.add))
                tt(shf_a[:, s, :], bank[5][:, 4:8], bias[:, 4 * cb:4 * cb + 4], ALU.add).then_inc(mod_read, 1)
                own.step(stt(gsc_a[:, s, :], gsc_a[:, s, :], 1.0, gains[:, KD + 4 * cb:KD + 4 * cb + 4], ALU.add, ALU.mult))
                for j in range(4):
                    k = 4 * cb + j
                    dve.wait_ge(x_t_ready, k + 1)
                    dve.wait_ge(mod_read, cb + 1)
                    ts(tmp[j % 2][:], x_t[:, k, :], gsc_a[:, s, j:j + 1], shf_a[:, s, j:j + 1], ALU.mult, ALU.add).then_inc(h_tmp, 1)
                    if j:
                        dve.wait_ge(h_hi_ready, k)
                        tt(h_lo[:, k - 1, :], tmp[(j - 1) % 2][:], h_hi[:, k - 1, :].bitcast(F32), ALU.subtract).then_inc(h_ready, 1)
                        dve.wait_ge(h_ready, k)
                dve.wait_ge(h_hi_ready, 4 * cb + 4)
                tt(h_lo[:, 4 * cb + 3, :], tmp[1][:], h_hi[:, 4 * cb + 3, :].bitcast(F32), ALU.subtract).then_inc(h_ready, 1)
                r, w = START_RAW * cb + 2 * UNITS_D, START_W * cb
                for j in range(2):
                    split_lo(At(r + j), At(w + j))
                four = lambda t: t[:].rearrange("p q n -> p (q n)")[:, 0:4 * P].rearrange("p (k m e) -> p k m e", k=4, m=2)
                s = At(w + 2).slot()
                src = raw[At(r + 2).slot()][:].rearrange("p q n -> p (q n)")[:, 0:4 * ROPE_B].rearrange("p (k e) -> p k e", k=4)
                split_lo(At(r + 2), At(w + 2), [(four(lo[s])[:, :, m, :], src, four(hi[s])[:, :, m, :]) for m in range(2)])

            def fold(g):
                own.step(tt(tab_g[:, 0], tab_a[:, 0], g[:].unsqueeze(1).broadcast_to([P, NT, P]), ALU.mult))
                swap = lambda x, s: x.rearrange("p (r s e) -> p r s e", r=2, s=2)[:, :, s, :]
                for s in range(2):
                    own.step(tt(tab_g[:, 1].rearrange("p t (r s e) -> p t r s e", r=2, s=2)[:, :, :, s, :],
                                tab_a[:, 1].rearrange("p t (r s e) -> p t r s e", r=2, s=2)[:, :, :, s, :],
                                swap(g[:], 1 - s).unsqueeze(1).broadcast_to([P, NT, 2, 32]), ALU.mult))

            def rope(t, heads, table, width, done):
                e = width // 4
                x = tok[:, t, 0:heads * width].rearrange("p (h d) -> p h d", h=heads)
                ca = tmp[0][:, 0:heads * width].rearrange("p (h d) -> p h d", h=heads)
                cos = table[:, 0, t, :].unsqueeze(1).broadcast_to([P, heads, width])
                tt(ca, x, cos, ALU.mult)
                for s in range(2):
                    for r in range(2):
                        at, of = r * 2 * e + s * e, r * 2 * e + (1 - s) * e
                        sin = table[:, 1, t, at:at + e].unsqueeze(1).broadcast_to([P, heads, e])
                        ins = tt(tmp[1][:, 0:heads * width].rearrange("p (h d) -> p h d", h=heads)[:, :, at:at + e], x[:, :, of:of + e], sin, ALU.mult)
                own.step(ins)
                tt(tok[:, t, 0:heads * width], tmp[0][:, 0:heads * width], tmp[1][:, 0:heads * width], ALU.add).then_inc(tok_ready, 1)

            copies = 0
            for b in range(1, PROJ_BLOCKS + 1):
                heads = {2: 2, 3: 4, 4: 4, 5: 8}.get(b)
                for j in range(UNITS_D):
                    r = PROJ_RAW + 2 * UNITS_D * (b - 1) + 2 * j
                    split_lo(At(r), At(PROJ_W + UNITS_D * (b - 1) + j))
                    if j == 0 and b >= 3:
                        g = b - 3
                        dve.wait_ge(mod_reduced, NB + g + 1)
                        nc.vector.tensor_copy(mod_m[:, 4 * g:4 * g + 4], sets[b % 2][0][:, 0:4]).then_inc(mod_read, 1)
                    modulate(At(r + 1), j, mod_acc[(b - 1) % 2][:])
                    if j == UNITS_D - 1:
                        dve.sem_inc(mod_summed, 1)
                    if b == 1:
                        if j == 3:
                            dve.wait_ge(c_sq, NT)
                            ts(stat_v[:, :, 0:1], stat[:, :, 0:1], 1.0 / RANK, EPS, ALU.mult, ALU.add).then_inc(var_ready, 1)
                        if j == 4:
                            dve.wait_ge(sqrt_ready, 1)
                            nc.vector.reciprocal(rstd[:, :, 0:1], stat_s[:, :, 0:1]).then_inc(rstd_ready, 1)
                        if j == 6:
                            dve.wait_ge(kr_turned, 1)
                            dve.wait_ge(tab_landed, 16 * 6)
                            own.step(tt(tmp[0][:], tmp[0][:], tab_t[:, 0], ALU.mult))
                            own.step(tt(tmp[1][:], bank[0][:], tab_t[:, 1], ALU.mult))
                            tt(tmp[0][:], tmp[0][:], tmp[1][:], ALU.add).then_inc(kr_sum, 1)
                        if j == 7:
                            dve.wait_ge(kr_hi_done, 1)
                            tt(kr_lo[0:64, 0, :], tmp[0][0:64, :], kr_hi[0:64, 0, :].bitcast(F32), ALU.subtract)
                            tt(kr_lo[64:128, 1, :], tmp[0][64:128, :], kr_hi[64:128, 1, :].bitcast(F32), ALU.subtract).then_inc(kr_ready, 1)
                            dve.wait_ge(kr_ready, 1)
                            fold(g_k)
                    elif heads:
                        if j == 3:
                            copies += 4
                        if j == 3 and b <= 4:
                            for t in range(NT):
                                dve.wait_ge(copied, 4 * (b - 1) + t + 1)
                                n = heads * P
                                own.step(tt(tmp[t % 2][:, 0:n], tok[:, t, 0:n], tok[:, t, 0:n], ALU.mult))
                                own.step(nc.vector.tensor_reduce(stat[:, t, 0:heads], tmp[t % 2][:, 0:n].rearrange("p (h d) -> p h d", h=heads), AX.X, ALU.add))
                            ts(stat_v[:, :, 0:heads], stat[:, :, 0:heads], 1.0 / P, EPS, ALU.mult, ALU.add).then_inc(var_ready, 1)
                        if j == 4 and b <= 4:
                            dve.wait_ge(sqrt_ready, b)
                            own.step(nc.vector.reciprocal(rstd[:, :, 0:heads], stat_s[:, :, 0:heads]))
                            if b == 3:
                                fold(g_q)
                        if j >= 4:
                            t = j - 4
                            dve.wait_ge(copied, 4 * (b - 1) + t + 1)
                            if b <= 4:
                                x = tok[:, t, 0:heads * P].rearrange("p (h d) -> p h d", h=heads)
                                own.step(tt(x, x, rstd[:, t, 0:heads].unsqueeze(2).broadcast_to([P, heads, P]), ALU.mult))
                                rope(t, heads, tab_g, P, b)
                            else:
                                rope(t, heads, tab_b, ROPE_B, b)
                if b == 6:
                    for k in range(KR):
                        dve.wait_ge(c_hi_done, k + 1)
                        tt(c_lo[:, k, :], ckv[:, k, :], c_hi[:, k, :].bitcast(F32), ALU.subtract).then_inc(c_ready, 1)

            for j in range(KV_UNITS):
                split_lo(At(KV_RAW + 3 * j), At(KV_W + j))
                for m in range(2):
                    g, jj = divmod(2 * j + m, UNITS_D)
                    if jj == 0 and g == 0:
                        dve.wait_ge(mod_reduced, NB + 5)
                        nc.vector.tensor_copy(mod_m[:, 16:20], sets[1][0][:, 0:4]).then_inc(mod_read, 1)
                    modulate(At(KV_RAW + 3 * j + 1 + m), jj, mod_acc[(0, 2)[g]][:])
                    if jj == UNITS_D - 1:
                        dve.sem_inc(mod_summed, 1)

            def out_units(n, js, nn=None):
                for j in js:
                    r, w = at_out(n, j) if nn is None else (At(OUT_RAW + OUT_RAW_N + 3 * j, nn, OUT_RAW_N), At(OUT_W + OUT_W_N + j, nn, OUT_W_N))
                    split_lo(r, w)
                    at_n = n if nn is None else nn + 1
                    for m in range(2):
                        if j < 4:
                            acc = ga_acc[:, bass.ds(at_n & 1, 1), :].rearrange("p a n -> p (a n)") if not isinstance(at_n, int) else ga_acc[:, at_n & 1, :]
                        else:
                            acc = gm_acc[:, bass.ds(at_n * COLS, COLS)]
                        modulate(r.plus(1 + m), 2 * (j % 4) + m, acc)
                    if j == 3:
                        dve.sem_inc(ga_summed, 1)
                    if nn is not None and j == 2:
                        combine(nn)

            out_units(0, range(4))

            def q_stage(grp, h, H):
                dve.wait_ge(q_hi_done, H + 1)
                src = q_o[:, bass.ds(h + grp * HEADS, 1), :].rearrange("p a n -> p (a n)")
                ins = tt(stage["q"][1][:], src, stage["q"][0][:].bitcast(F32), ALU.subtract)
                if grp:
                    ins = tt(stage["qr"][1][:], q_rot[:, bass.ds(h // 2, 1), :].rearrange("p a n -> p (a n)"), stage["qr"][0][:].bitcast(F32), ALU.subtract)
                ins.then_inc(q_ready, 1)

            def row_max(grp, t, H):
                dve.wait_ge(s_done, H * 4 + (t + 1))
                own.step(nc.vector.reduce_max(top[:, t:t + 1], bank[t][:], AX.X))
                ts(nbias[:, t:t + 1], top[:, t:t + 1], -(SCALE_B if grp else SCALE_A), None, ALU.mult).then_inc(nb_ready, 1)

            def normalise(t, H):
                dve.wait_ge(exp_done, H * 4 + (t + 1))
                own.step(nc.vector.reciprocal(rtotal[:, t:t + 1], total[:, t:t + 1]))
                ts(prob[:, t, :], prob[:, t, :], rtotal[:, t:t + 1], None, ALU.mult).then_inc(p_ready, 1)

            def attend(H, nxt):
                if nxt:
                    q_stage(*nxt)
                for t in range(NT):
                    dve.wait_ge(pt_hi_done, H * 4 + (t + 1))
                    tt(pt_lo[:, :, t * P:(t + 1) * P], bank[4 + t % 2][:].rearrange("p (c n) -> p c n", c=NT),
                       pt_hi[:, :, t * P:(t + 1) * P].bitcast(F32), ALU.subtract).then_inc(pt_done, 1)
                    if nxt:
                        row_max(nxt[0], t, nxt[2])
                        if t:
                            normalise(t - 1, nxt[2])
                if nxt:
                    normalise(NT - 1, nxt[2])

            dve.sem_inc(pt_done, 2)
            q_stage(0, 0, 0)
            for t in range(NT):
                row_max(0, t, 0)
                normalise(t, 0)
            attend(0, (0, 1, 1))
            PER = 8
            with dve.Fori(1, HEADS - 1) as h:
                own.enter(h - 1, PER)
                attend(h, (0, h + 1, h + 1))
            own.leave(HEADS - 2)
            attend(HEADS - 1, (1, 0, HEADS))
            with dve.Fori(0, HEADS - 1) as h:
                own.enter(h, PER)
                attend(h + HEADS, (1, h + 1, h + (HEADS + 1)))
            own.leave(HEADS - 1)
            attend(2 * HEADS - 1, None)

            dve.wait_ge(mod_reduced, NB + 8)
            own.step(nc.vector.tensor_copy(mod_m[:, 20:32], bank[7][:, 0:12]))
            own.step(tt(gsc_m[:], mod_m[:, 0:KD], bias[:, SC_M // P:SC_M // P + KD], ALU.add))
            own.step(stt(gsc_m[:], gsc_m[:], 1.0, gains[:, 2 * KD:3 * KD], ALU.add, ALU.mult))
            tt(shf_m[:], mod_m[:, KD:2 * KD], bias[:, SH_M // P:SH_M // P + KD], ALU.add).then_inc(mod_read, 1)

            for k in range(KD):
                dve.wait_ge(o_hi_done, k + 1)
                stt(o_lo[:, k, :], q_o[:, k, :], gains[:, 3 * KD + k:3 * KD + k + 1], o_hi[:, k, :].bitcast(F32), ALU.mult, ALU.subtract).then_inc(o_ready, 1)
            dve.wait_ge(sq_reduced, 1)
            own.step(ts(stat_v[:, 0:2, :], bank[7][:, 16:24].rearrange("p (g t) -> p g t", g=2), 1.0 / (HEADS * P), EPS, ALU.mult, ALU.add))
            dve.sem_inc(r_var, 1)
            dve.wait_ge(r_sqrt, 1)
            nc.vector.reciprocal(r_out[:], stat_s[:, 0:2, :]).then_inc(r_ready, 1)
            dve.wait_ge(r_ready, 1)

            def combine(n):
                dve.wait_ge(ga_reduced, n + 1)
                dve.wait_ge(rows_landed, n * 32 + 32)
                own.step(tt(comb[:], bank[0][:], rows[:, 0, :], ALU.add))
                tt(comb[:], comb[:], rows[:, 1, :], ALU.mult).then_inc(comb_ready, 1)

            def b_part(n):
                dve.wait_ge(w_used, n * OUT_W_N + (OUT_W + OUT_W_N))
                dve.wait_ge(comb_ready, n + 1)
                dve.wait_ge(a_out, n * 4 + 4)
                for t in range(NT):
                    own.step(stt(part[:, t, :], bank[4 + t][:], r_out[:, 1, t:t + 1], part[:, t, :], ALU.mult, ALU.add))
                    tt(z_tok[:, t, bass.ds(n * COLS, COLS)], part[:, t, :], comb[:], ALU.mult).then_inc(z_done, 1)

            with dve.Fori(0, NB - 1) as n:
                own.enter(n, 8 + 8 + 1 + NT)
                out_units(n, range(4, 8))
                out_units(None, range(4), nn=n)
                b_part(n)
            own.leave(NB - 1)
            out_units(NB - 1, range(4, 8))
            for j in range(4):
                split_lo(*at_mlp(0, j))
                if j == 2:
                    combine(NB - 1)
            b_part(NB - 1)

            dve.wait_ge(row_done, NB * 4)
            own.step(nc.vector.tensor_reduce(stat[:, :, 0:1], row_sq[:], AX.X, ALU.add))
            ts(stat_v[:, :, 0:1], stat[:, :, 0:1], 1.0 / D, EPS, ALU.mult, ALU.add).then_inc(x1_var, 1)
            dve.wait_ge(x1_sqrt, 1)
            own.step(nc.vector.reciprocal(rstd[:, :, 0:1], stat_s[:, :, 0:1]))
            dve.wait_ge(res_landed, 16 * NT)

            def scale_x1(t):
                dve.wait_ge(x1_sq, t + 1)
                ts(stat_v[:, t, 1:2], stat[:, t, 1:2], 1.0 / D, EPS, ALU.mult, ALU.add).then_inc(x1_var, 1)
                dve.wait_ge(x1_sqrt, t + 2)
                own.step(nc.vector.reciprocal(rstd[:, t, 1:2], stat_s[:, t, 1:2]))
                ts(z_tok[:, t, :], x_res[:, t, :], rstd[:, t, 1:2], None, ALU.mult).then_inc(xn_ready, 1)

            for t in range(NT):
                stt(x_res[:, t, :], z_tok[:, t, :], rstd[:, t, 0:1], x_res[:, t, :], ALU.mult, ALU.add).then_inc(x1_ready, 1)
                if t:
                    scale_x1(t - 1)
            scale_x1(NT - 1)
            for k in range(KD):
                dve.wait_ge(xn_turned, k + 1)
                if k >= 2:
                    dve.wait_ge(h2_ready, k - 1)
                ts(tmp_u[k % 2][:], bank[k % 8][:], gsc_m[:, k:k + 1], shf_m[:, k:k + 1], ALU.mult, ALU.add).then_inc(h2_tmp, 1)
                if k:
                    dve.wait_ge(h2_hi_done, k)
                    tt(h2_lo[:, k - 1, :], tmp_u[(k - 1) % 2][:], h2_hi[:, k - 1, :].bitcast(F32), ALU.subtract).then_inc(h2_ready, 1)
            dve.wait_ge(h2_hi_done, KD)
            tt(h2_lo[:, KD - 1, :], tmp_u[(KD - 1) % 2][:], h2_hi[:, KD - 1, :].bitcast(F32), ALU.subtract).then_inc(h2_ready, 1)

            dve.sem_inc(mlp_free, 4)

            def squares(g, f):
                n0 = 4 * f
                for c in range(4):
                    dve.wait_ge(relu_done, g * FCH + (n0 + c + 1))
                    stt(tmp_y[c % 2][:], sets[f][c][:], 0.0, tmp_u[c % 2][:], ALU.max, ALU.mult).then_inc(y_done, 1)
                    dve.wait_ge(y_hi_done, g * FCH + (n0 + c + 1))
                    tt(y_lo[:, n0 + c, :], tmp_y[c % 2][:], y_hi[:, n0 + c, :].bitcast(F32), ALU.subtract).then_inc(y_ready, 1)
                    dve.wait_ge(y_ready, g * FCH + (n0 + c + 1))
                dve.sem_inc(mlp_free, 4)

            def down_add(n, first):
                for t in range(NT):
                    dst = y_acc[:, t, n * COLS:(n + 1) * COLS]
                    src = sets[n % 2][t][:]
                    ins = nc.vector.tensor_copy(dst, src) if first else tt(dst, src, dst, ALU.add)
                    ins.then_inc(mlp_free, 1)

            def mlp_group(g, first, before_first):
                for j in range(4 if first else 0, MLP_N):
                    r, w = at_mlp(g, j)
                    split_lo(r, w)
                    if j == 3:
                        dve.wait_ge(w_used, w.count(1, 1 - 4))
                        down_add(NB - 1, before_first)
                    if j == UNITS_D + 3:
                        squares(g, 0)
                    if j == UP_UNITS + 3:
                        squares(g, 1)
                    if j > UP_UNITS + 3 and (j - UP_UNITS) % DN_U == DN_U - 1:
                        dve.wait_ge(w_used, w.count(1, 1 - 4))
                        down_add((j - UP_UNITS) // DN_U - 1, first)

            mlp_group(0, True, False)
            mlp_group(1, False, True)
            with dve.Fori(2, GROUPS) as g:
                mlp_group(g, False, False)
            dve.wait_ge(w_used, MLP_W + MLP_N * GROUPS)
            down_add(NB - 1, False)

            dve.wait_ge(y_sq, NT)
            ts(stat_v[:, :, 2:3], stat[:, :, 2:3], 1.0 / D, EPS, ALU.mult, ALU.add).then_inc(y_var, 1)
            dve.wait_ge(y_sqrt, 1)
            own.step(nc.vector.reciprocal(rstd[:, :, 2:3], stat_s[:, :, 2:3]))
            dve.wait_ge(comb_m_ready, 1)
            dve.wait_ge(x1_landed, 16 * NT)
            for t in range(NT):
                own.step(stt(y_acc[:, t, :], y_acc[:, t, :], rstd[:, t, 2:3], gm_acc[:], ALU.mult, ALU.mult))
                tt(x1_back[:, t, :], y_acc[:, t, :], x1_back[:, t, :], ALU.add).then_inc(out_ready, 1)

        @block.tensor
        def _(pe):
            mm = nc.tensor.matmul

            def unit_tokens(w, acc, act_hi, act_lo, k0, first, last):
                s = w.slot()
                for t in range(NT):
                    for q in range(QROWS):
                        k = k0 + q
                        xh, xl = act_hi[:, k, t * P:(t + 1) * P], act_lo[:, k, t * P:(t + 1) * P]
                        mm(acc[t][:], xh, hi[s][:, q, :], start=first and q == 0, stop=False)
                        mm(acc[t][:], xh, lo[s][:, q, :], start=False, stop=False)
                        ins = mm(acc[t][:], xl, hi[s][:, q, :], start=False, stop=last and q == QROWS - 1)
                ins.then_inc(w_used, 1)

            def unit_columns(w, acc, act_hi, act_lo, k0, first, last):
                s = w.slot()
                for n in range(4):
                    for q in range(QROWS):
                        k = k0 + q
                        wh, wl = hi[s][:, q, n * P:(n + 1) * P], lo[s][:, q, n * P:(n + 1) * P]
                        mm(acc[n][:], wh, act_hi[:, k, :], start=first and q == 0, stop=False)
                        mm(acc[n][:], wh, act_lo[:, k, :], start=False, stop=False)
                        ins = mm(acc[n][:], wl, act_hi[:, k, :], start=False, stop=last and q == QROWS - 1)
                ins.then_inc(w_used, 1)

            pe.wait_ge(const_landed, 16)
            pe.wait_ge(vec_landed, 16 * 7)
            width = 3 * KD + 2 * HEADS + KR
            nc.tensor.transpose(bank[4][:, 0:width], vec_rows[0:width, 0, :], ident[0:width, 0:width]).then_inc(vec_turned, 1)
            nc.tensor.transpose(bank[5][:, 0:6 * KD], vec_rows[0:6 * KD, 1, :], ident[0:6 * KD, 0:6 * KD]).then_inc(vec_turned, 1)
            pe.wait_ge(x_normed, NT)
            for k in range(KD):
                if k >= 4:
                    pe.wait_ge(x_t_ready, k - 3)
                for t in range(NT):
                    ins = nc.tensor.transpose(bank[k % 4][:, t * P:(t + 1) * P], x_tok[:, t, k * P:(k + 1) * P], ident[:])
                ins.then_inc(x_turned, 1)
            pe.wait_ge(ones_ready, 1)
            pe.wait_ge(vec_ready, 2)
            for cb in range(NB):
                pe.wait_ge(mod_summed, 2 * cb + 2)
                if cb:
                    pe.wait_ge(mod_read, cb)
                for g in range(2):
                    for j in range(4):
                        ins = mm(bank[5][:, 4 * g + j:4 * g + j + 1], mod_acc[g][:, j * P:(j + 1) * P], ones[:, 0:1], start=True, stop=True)
                ins.then_inc(mod_reduced, 1)
                pe.wait_ge(x_t_ready, KD)
                r, w = START_RAW * cb + 2 * UNITS_D, START_W * cb
                for j in range(2):
                    pe.wait_ge(h_ready, 4 * cb + 2 * j + 2)
                    pe.wait_ge(raw_used, r + j + 1)
                    unit_tokens(At(w + j), sets[0], h_hi, h_lo, 4 * cb + 2 * j, cb == 0 and j == 0, cb == NB - 1 and j == 1)
                pe.wait_ge(raw_used, r + 3)
                s = At(w + 2).slot()
                for k in range(4):
                    wh, wl = (x[s][:].rearrange("p q n -> p (q n)")[:, k * P:(k + 1) * P] for x in (hi, lo))
                    xh, xl = h_hi[:, 4 * cb + k, :], h_lo[:, 4 * cb + k, :]
                    mm(bank[4][:], wh, xh, start=cb == 0 and k == 0, stop=False)
                    mm(bank[4][:], wh, xl, start=False, stop=False)
                    ins = mm(bank[4][:], wl, xh, start=False, stop=cb == NB - 1 and k == 3)
                ins.then_inc(w_used, 1)

            def turn(b):
                if b == 0:
                    pe.wait_ge(copied, 4)
                    pe.wait_ge(kr_sum, 1)
                else:
                    pe.wait_ge(tok_ready, 4 * b)
                for n in range(TURNS[b]):
                    for t in range(NT):
                        ins = nc.tensor.transpose(sets[b % 2][n][:, t * P:(t + 1) * P], tok[:, t, n * P:(n + 1) * P], ident[:])
                    ins.then_inc(turned, 1)

            for b in range(1, PROJ_BLOCKS + 1):
                for j in range(UNITS_D):
                    r, w = PROJ_RAW + 2 * UNITS_D * (b - 1) + 2 * j, PROJ_W + UNITS_D * (b - 1) + j
                    pe.wait_ge(raw_used, r + 1)
                    if j == 0:
                        if b == 1:
                            pe.wait_ge(kr_copied, 1)
                            pe.wait_ge(mod_read, NB)
                        else:
                            pe.wait_ge(turned_out, TURNS_SUM[b - 1])
                            pe.wait_ge(copied, 4 * (b - 1))
                            if b >= 3:
                                pe.wait_ge(mod_read, NB + b - 2) if b >= 4 else None
                    unit = unit_tokens if TOKENS_OUT[b] else unit_columns
                    unit(At(w), sets[b % 2], h_hi, h_lo, QROWS * j, j == 0, j == UNITS_D - 1)
                    if j == 4 and b == 1:
                        pe.wait_ge(tab_landed, 16 * 6)
                        pe.wait_ge(c_sq, 4)
                        pe.wait_ge(copied, 4)
                        mm(bank[0][:], rot[:], tmp[0][:], start=True, stop=True).then_inc(kr_turned, 1)
                    if j == 4 and b >= 2:
                        pe.wait_ge(mod_summed, 2 * NB + b - 1)
                        pe.wait_ge(copied, 4 * b)
                        for n in range(4):
                            ins = mm(sets[(b - 1) % 2][0][:, n:n + 1], mod_acc[(b - 2) % 2][:, n * P:(n + 1) * P], ones[:, 0:1], start=True, stop=True)
                        ins.then_inc(mod_reduced, 1)
                    if j == 6 and b <= 5:
                        if b >= 2:
                            pe.wait_ge(mod_read, NB + b - 1)
                        turn(b - 1)

            for i, b in enumerate((7, 8, 9, 10)):
                pe.wait_ge(copied, 4 * (b - 1))
                if b == 7:
                    pe.wait_ge(mod_read, NB + 5)
                    pe.wait_ge(c_ready, KR)
                for j in range(2):
                    pe.wait_ge(raw_used, KV_RAW + 3 * (2 * i + j) + 1)
                    unit = unit_columns if b < 9 else unit_tokens
                    unit(At(KV_W + 2 * i + j), sets[b % 2], c_hi, c_lo, 2 * j, j == 0, j == 1)
            pe.wait_ge(mod_summed, 2 * NB + 8)
            pe.wait_ge(copied, 4 * 10)
            for g, acc in ((5, 1), (6, 0), (7, 2)):
                for n in range(4):
                    c = 4 * (g - 5) + n
                    ins = mm(bank[7][:, c:c + 1], mod_acc[acc][:, n * P:(n + 1) * P], ones[:, 0:1], start=True, stop=True)
                ins.then_inc(mod_reduced, 1)
            pe.wait_ge(copied, 4 * 11)
            pe.wait_ge(kr_ready, 1)

            def scores(grp, h, H, t):
                if t == 0:
                    pe.wait_ge(q_ready, H + 1)
                    pe.wait_ge(k_ready, H + 1)
                (qh, ql), (kh, kl) = stage["q"], stage["k"]
                cut = lambda x: x[:, t * P:(t + 1) * P]
                mm(bank[t][:], cut(qh), kh[:], start=True, stop=False)
                mm(bank[t][:], cut(qh), kl[:], start=False, stop=False)
                ins = mm(bank[t][:], cut(ql), kh[:], start=False, stop=not grp)
                if grp:
                    rh, rl = stage["qr"]
                    par = bass.ds(h & 1, 1) if not isinstance(h, int) else slice(h & 1, (h & 1) + 1)
                    krh, krl = (x[:, par, :].rearrange("p a n -> p (a n)") for x in (kr_hi, kr_lo))
                    mm(bank[t][:], cut(rh), krh, start=False, stop=False)
                    mm(bank[t][:], cut(rh), krl, start=False, stop=False)
                    ins = mm(bank[t][:], cut(rl), krh, start=False, stop=True)
                ins.then_inc(s_done, 1)

            def attend(H, nxt):
                for t in range(NT):
                    pe.wait_ge(p_ready, H * 4 + (t + 1))
                    pe.wait_ge(pt_done, H * 4 + (t + 1))
                    for c in range(NT):
                        ins = nc.tensor.transpose(bank[4 + t % 2][:, c * P:(c + 1) * P], prob[:, t, c * P:(c + 1) * P], ident[:])
                    ins.then_inc(p_turned, 1)
                    if nxt:
                        scores(*nxt, t)
                pe.wait_ge(pt_done, H * 4 + 6)
                pe.wait_ge(v_ready, H + 1)
                pe.wait_ge(o_done, H)
                (vh, vl) = stage["v"]
                for c in range(NT):
                    v = slice(c * P, (c + 1) * P)
                    mm(bank[6][:], vh[:, v], pt_hi[:, c, :], start=c == 0, stop=False)
                    mm(bank[6][:], vh[:, v], pt_lo[:, c, :], start=False, stop=False)
                    ins = mm(bank[6][:], vl[:, v], pt_hi[:, c, :], start=False, stop=c == NT - 1)
                ins.then_inc(pv_done, 1)

            for t in range(NT):
                scores(0, 0, 0, t)
            attend(0, (0, 1, 1))
            with pe.Fori(1, HEADS - 1) as h:
                attend(h, (0, h + 1, h + 1))
            attend(HEADS - 1, (1, 0, HEADS))
            with pe.Fori(0, HEADS - 1) as h:
                attend(h + HEADS, (1, h + 1, h + (HEADS + 1)))
            attend(2 * HEADS - 1, None)

            pe.wait_ge(sq_ready, 2 * HEADS)
            pe.wait_ge(mod_read, NB + 6)
            for g in range(2):
                for t in range(NT):
                    c = 16 + 4 * g + t
                    ins = mm(bank[7][:, c:c + 1], sq_sum[:, g, t * P:(t + 1) * P], ones[:, 0:1], start=True, stop=True)
            ins.then_inc(sq_reduced, 1)
            with pe.Fori(0, NB) as n:
                for j in range(UNITS_D):
                    r, w = at_out(n, j)
                    pe.wait_ge(raw_used, r.count(1, 1))
                    pe.wait_ge(o_ready, 2 * j + 2)
                    if j == 0:
                        pe.wait_ge(comb_ready, n)
                    if j == 4:
                        pe.wait_ge(z_done, n * 4)
                        pe.wait_ge(r_ready, 1)
                    unit_tokens(w, sets[j // 4], o_hi, o_lo, QROWS * j, j % 4 == 0, j % 4 == 3)
                    if j == 6:
                        pe.wait_ge(a_out, n * 4 + 4)
                        pe.wait_ge(ga_summed, n + 1)
                        src = ga_acc[:, bass.ds(n & 1, 1), :].rearrange("p a n -> p (a n)")
                        mm(bank[0][:], ones[:], src, start=True, stop=True).then_inc(ga_reduced, 1)
            pe.wait_ge(z_done, 4 * NB)
            for n in range(NB):
                ins = mm(bank[4 + n][:], ones[:], gm_acc[:, n * COLS:(n + 1) * COLS], start=True, stop=True)
            ins.then_inc(gm_reduced, 1)
            pe.wait_ge(comb_ready, NB)
            pe.wait_ge(gm_copied, NB)
            for t in range(NT):
                pe.wait_ge(xn_ready, t + 1)
                for k in range(8):
                    ins = nc.tensor.transpose(bank[k][:, t * P:(t + 1) * P], z_tok[:, t, k * P:(k + 1) * P], ident[:])
                    if t == NT - 1:
                        ins.then_inc(xn_turned, 1)
            for k in range(8, KD):
                pe.wait_ge(h2_tmp, k - 7)
                for t in range(NT):
                    ins = nc.tensor.transpose(bank[k % 8][:, t * P:(t + 1) * P], z_tok[:, t, k * P:(k + 1) * P], ident[:])
                ins.then_inc(xn_turned, 1)
            pe.wait_ge(h2_tmp, 12)

            with pe.Fori(0, GROUPS) as g:
                for f in range(2):
                    for j in range(UNITS_D):
                        r, w = at_mlp(g, f * UNITS_D + j)
                        pe.wait_ge(raw_used, r.count(1, 1))
                        if f == 0:
                            pe.wait_ge(h2_ready, 2 * j + 2)
                        if j == 0:
                            pe.wait_ge(mlp_free, g * 24 + 4 * f)
                        unit_columns(w, sets[f], h2_hi, h2_lo, QROWS * j, j == 0, j == UNITS_D - 1)
                for n in range(NB):
                    for j in range(DN_U):
                        r, w = at_mlp(g, UP_UNITS + n * DN_U + j)
                        pe.wait_ge(raw_used, r.count(1, 1))
                        if n == 0:
                            pe.wait_ge(y_ready, g * FCH + 2 * j + 2)
                        if j == 0:
                            pe.wait_ge(mlp_free, g * 24 + 4 * (n + 2))
                        unit_tokens(w, sets[n % 2], y_hi, y_lo, QROWS * j, j == 0, j == DN_U - 1)

        @block.gpsimd
        def _(pool):
            own = Chain(pool, pool_own)
            tt = nc.gpsimd.tensor_tensor
            nc.gpsimd.memset(ones[:], 1.0).then_inc(ones_ready, 1)
            pool.wait_ge(ones_ready, 1)
            own.step(nc.gpsimd.memset(kr_hi[64:128, 0, :].bitcast(F32), 0.0))
            own.step(nc.gpsimd.memset(kr_hi[0:64, 1, :].bitcast(F32), 0.0))
            own.step(nc.gpsimd.memset(kr_lo[64:128, 0, :].bitcast(F32), 0.0))
            own.step(nc.gpsimd.memset(kr_lo[0:64, 1, :].bitcast(F32), 0.0))

            def split(name, src):
                h, l = stage[name]
                mine = head_raw[name]
                as_src = (lambda x: x.rearrange("p (c e) -> p c e", c=NT)) if name == "v" else (lambda x: x)
                nc.gpsimd.tensor_copy(as_src(mine[:]), src)
                own.step(nc.gpsimd.tensor_copy(as_src(h[:]), src))
                return tt(l[:], mine[:], h[:].bitcast(F32), ALU.subtract)

            def keys(grp, h, H):
                if not (isinstance(H, int) and H == 0):
                    pool.wait_ge(s_done, H * 4)
                src = k_nope[:, bass.ds(h, 1), :] if grp else k_gqa[:, bass.ds(h // 4, 1), :]
                split("k", src.rearrange("p a n -> p (a n)")).then_inc(k_ready, 1)

            def values(grp, h, H):
                pool.wait_ge(pv_done, H)
                src = v_lat[:, :, bass.ds(h, 1), :] if grp else v_gqa[:, :, bass.ds(h // 4, 1), :]
                split("v", src.rearrange("p t a e -> p t (a e)")).then_inc(v_ready, 1)

            def square(H, grp, first):
                pool.wait_ge(o_done, H + 1)
                mine = head_raw["o"]
                own.step(nc.gpsimd.tensor_copy(mine[:], q_o[:, bass.ds(H, 1), :].rearrange("p a n -> p (a n)")))
                if first:
                    tt(sq_sum[:, grp, :], mine[:], mine[:], ALU.mult).then_inc(sq_ready, 1)
                else:
                    own.step(tt(sq[:], mine[:], mine[:], ALU.mult))
                    tt(sq_sum[:, grp, :], sq_sum[:, grp, :], sq[:], ALU.add).then_inc(sq_ready, 1)
                pool.wait_ge(sq_ready, H + 1)

            pool.wait_ge(copied, 4 * 11)
            pool.wait_ge(turned_out, TURNS_SUM[5])
            pool.wait_ge(w_used, OUT_W)
            keys(0, 0, 0)
            values(0, 0, 0)
            keys(0, 1, 1)
            values_A = 4
            for H in (1,):
                values(0, 1, 1)
                keys(0, 2, 2)
                square(0, 0, True)
            with pool.Fori(2, HEADS - 1) as h:
                own.enter(h - 2, 4)
                values(0, h, h)
                keys(0, h + 1, h + 1)
                square(h - 1, 0, False)
            own.leave(HEADS - 3)
            values(0, HEADS - 1, HEADS - 1)
            keys(1, 0, HEADS)
            square(HEADS - 2, 0, False)
            values(1, 0, HEADS)
            keys(1, 1, HEADS + 1)
            square(HEADS - 1, 0, False)
            values(1, 1, HEADS + 1)
            keys(1, 2, HEADS + 2)
            square(HEADS, 1, True)
            with pool.Fori(2, HEADS - 1) as h:
                own.enter(h - 2, 4)
                values(1, h, h + HEADS)
                keys(1, h + 1, h + (HEADS + 1))
                square(h + (HEADS - 1), 1, False)
            own.leave(HEADS - 3)
            values(1, HEADS - 1, 2 * HEADS - 1)
            square(2 * HEADS - 2, 1, False)
            square(2 * HEADS - 1, 1, False)
            pool.wait_ge(sq_reduced, 1)
            for t in range(NT):
                pool.dma_start(x_res[:, t, :], x_d[t]).then_inc(res_landed, 16)
            for n in range(NB):
                if n:
                    pool.wait_ge(comb_ready, n)
                pool.dma_start(rows[:, 0, :], b_rows[:, GT_A + n * COLS:GT_A + (n + 1) * COLS].partition_broadcast(P)[:, 0, :]).then_inc(rows_landed, 16)
                pool.dma_start(rows[:, 1, :], a["g_post_attn"][:, n * COLS:(n + 1) * COLS].partition_broadcast(P)[:, 0, :]).then_inc(rows_landed, 16)
            for n in range(NB):
                if n == 0:
                    pool.wait_ge(comb_ready, NB)
                pool.dma_start(rows[:, 0, :], b_rows[:, GT_M + n * COLS:GT_M + (n + 1) * COLS].partition_broadcast(P)[:, 0, :]).then_inc(rows_landed, 16)
                pool.dma_start(rows[:, 1, :], a["g_post_mlp"][:, n * COLS:(n + 1) * COLS].partition_broadcast(P)[:, 0, :]).then_inc(rows_landed, 16)
                pool.wait_ge(rows_landed, 32 * (NB + n + 1))
                pool.wait_ge(gm_copied, NB)
                dst = gm_acc[:, n * COLS:(n + 1) * COLS]
                own.step(tt(dst, dst, rows[:, 0, :], ALU.add))
                own.step(tt(dst, dst, rows[:, 1, :], ALU.mult))
            pool.sem_inc(comb_m_ready, 1)


def kernel(**inputs):
    import concourse.bacc as bacc
    from concourse.bass_utils import run_bass_kernel_spmd

    nc = bacc.Bacc("TRN2", target_bir_lowering=False, num_devices=1)
    arrays = {name: np.ascontiguousarray(v) for name, v in inputs.items()}
    arrays.update(tables())
    aps = {name: nc.dram_tensor("in_" + name, v.shape, F32, kind="ExternalInput").ap() for name, v in arrays.items()}
    out = nc.dram_tensor("out", (1, T, D), F32, kind="ExternalOutput").ap()
    x1_dram = nc.dram_tensor("x1_dram", (T, D), F32, kind="Internal").ap()
    build(nc, aps, out, x1_dram)
    r = run_bass_kernel_spmd(nc, [{"in_" + name: v for name, v in arrays.items()}], core_ids=[0])
    return r.results[0]["out"]


def tables():
    f = np.float32
    row, col = (np.arange(T) // 64).astype(f), (np.arange(T) % 64).astype(f)

    def angles(dim):
        half = dim // 2
        inv = np.power(f(10000.0), -np.arange(0, half, 2, dtype=f) / f(half)).astype(f)
        r, c = row[:, None] * inv[None], col[:, None] * inv[None]
        ang = np.concatenate([r, r, c, c], axis=-1).astype(f)
        sign = np.tile(np.repeat(np.array([-1, 1], f), dim // 4), 2)
        return np.stack([np.cos(ang), np.sin(ang) * sign]).astype(f)

    rot = np.zeros((P, P), f)
    for i in range(P):
        rot[i ^ (ROPE_B // 4), i] = 1.0
    tok_major = lambda t: np.ascontiguousarray(t.reshape(2, NT, P, -1).transpose(2, 0, 1, 3))
    b = angles(ROPE_B)
    tab_t = np.concatenate([b.transpose(2, 0, 1)] * 2, axis=0)
    return {"ident": np.eye(P, dtype=f), "rot": rot, "tab_a": tok_major(angles(P)), "tab_b": tok_major(b),
            "tab_t": np.ascontiguousarray(tab_t)}
```

```python
import math
from contextlib import ExitStack

import numpy as np

import concourse.bass as bass
from concourse import mybir

F32, F32R = mybir.dt.float32, mybir.dt.float32r
ACT, ALU, AX = mybir.ActivationFunctionType, mybir.AluOpType, mybir.AxisListType

P = 128
T = 512
NT = T // P
D = 2048
KD = D // P
COLS = 512
NB = D // COLS
QROWS = 2
RING = 4
HEADS = 8
RANK = 512
KR = RANK // P
ROPE_B = 64
D_FF = 4 * D
GROUPS = 8
FCH = D_FF // GROUPS // P
EPS = 1e-6
SCALE_A = 1.0 / math.sqrt(128)
SCALE_B = 1.0 / math.sqrt(128 + ROPE_B)
SH_A, SC_A, GT_A, SH_M, SC_M, GT_M = [i * D for i in range(6)]

UNITS_D = KD // QROWS
START_RAW, START_W = 2 * UNITS_D + 3, 3


def start_mod(cb, g):
    return START_RAW * cb + (UNITS_D if g else -3 if cb else 0)


def start_w(cb):
    return START_RAW * (cb + 1) + (UNITS_D - 3 if cb < NB - 1 else -3)


PROJ_RAW = NB * START_RAW
PROJ_W = NB * START_W
PROJ_BLOCKS = 6
KV_RAW = PROJ_RAW + PROJ_BLOCKS * 2 * UNITS_D
KV_W = PROJ_W + PROJ_BLOCKS * UNITS_D
KV_UNITS = 8
OUT_RAW = KV_RAW + 3 * KV_UNITS
OUT_W = KV_W + KV_UNITS
OUT_RAW_N, OUT_W_N = 3 * UNITS_D, UNITS_D
MLP_RAW = OUT_RAW + NB * OUT_RAW_N
MLP_W = OUT_W + NB * OUT_W_N
UP_UNITS, DOWN_UNITS = 2 * UNITS_D, NB * FCH // QROWS
MLP_N = UP_UNITS + DOWN_UNITS
DN_U = FCH // QROWS


class At:

    def __init__(self, const, i=None, per=0):
        assert per % RING == 0
        self.const, self.i, self.per = const, i, per

    def slot(self):
        return self.const % RING

    def count(self, times=1, more=0, each=1):
        fixed = times * (self.const // each) + more
        return fixed if self.i is None else self.i * (times * self.per // each) + fixed

    def plus(self, n):
        return At(self.const + n, self.i, self.per)


class Chain:

    def __init__(self, engine, sem):
        self.engine, self.sem, self.n, self.loop = engine, sem, 0, 0

    def step(self, instruction):
        instruction.then_inc(self.sem, 1)
        self.n += 1
        self.engine.wait_ge(self.sem, self.loop + self.n)

    def enter(self, i, per):
        self.loop, self.at, self.per = i * per, self.n, per

    def leave(self, times):
        assert self.n - self.at == self.per, (self.n - self.at, self.per)
        self.loop, self.n = 0, self.at + times * self.per


def build(nc, a, out, x1_dram):
    with ExitStack() as ctx:
        sem = lambda name: ctx.enter_context(nc.semaphore(name))
        base = 16512
        KB = 1024
        room = ctx.enter_context(nc.sbuf_tensor("room", [P, 53000], F32))

        def sb(name, kb, shape, dtype=F32):
            size = int(np.prod(shape)) * 4
            assert base + int(kb * KB) + size <= 229344, name
            return nc.alloc_sbuf_tensor_at(name, [P] + list(shape), dtype, offset=base + int(kb * KB))

        place = [0.0]

        def small(name, shape):
            t = sb(name, place[0], shape)
            place[0] += math.ceil(int(np.prod(shape)) * 4 / 32) * 32 / KB
            assert place[0] <= 4
            return t

        ident = small("ident", [P])
        rot = small("rot", [P])
        ones = small("ones", [P])
        gains = small("gains", [KD * 3 + 2 * HEADS + KR])
        bias = small("bias", [6 * KD])
        g_q, g_k = sb("g_q", 206, [P]), sb("g_k", 206.5, [P])
        silu_c = small("silu_c", [KD])
        silu_t = small("silu_t", [KD])
        gsc_a = small("gsc_a", [2, 4])
        shf_a = small("shf_a", [2, 4])
        mod_m = small("mod_m", [2 * KD])
        gsc_m = small("gsc_m", [KD])
        shf_m = small("shf_m", [KD])
        stat = small("stat", [NT, 4])
        stat_v = small("stat_v", [NT, 4])
        stat_s = small("stat_s", [NT, 4])
        rstd = small("rstd", [NT, 4])
        top = small("top", [NT])
        nbias = small("nbias", [NT])
        total = small("total", [NT])
        rtotal = small("rtotal", [NT])
        r_out = small("r_out", [2, NT])
        row_sq = small("row_sq", [NT, NB])
        raw = [sb(f"raw{i}", 4 + 4 * i, [QROWS, COLS]) for i in range(RING)]
        hi = [sb(f"hi{i}", 20 + 4 * i, [QROWS, COLS], F32R) for i in range(RING)]
        lo = [sb(f"lo{i}", 36 + 4 * i, [QROWS, COLS], F32R) for i in range(RING)]
        x_tok = sb("x_tok", 52, [NT, D])
        h_hi, h_lo = sb("h_hi", 52, [KD, T], F32R), sb("h_lo", 84, [KD, T], F32R)
        prob = sb("prob", 52, [NT, T])
        k_nope = sb("k_nope", 68, [HEADS, T])
        v_lat = sb("v_lat", 84, [NT, HEADS, P])
        stage = {}
        for n, name in enumerate(("q", "k", "v", "qr")):
            stage[name] = (sb(f"{name}_hi", 100 + 4 * n, [T], F32R), sb(f"{name}_lo", 102 + 4 * n, [T], F32R))
        o_hi, o_lo = sb("o_hi", 52, [KD, T], F32R), sb("o_lo", 84, [KD, T], F32R)
        h2_hi, h2_lo = sb("h2_hi", 52, [KD, T], F32R), sb("h2_lo", 84, [KD, T], F32R)
        x1_back = sb("x1_back", 52, [NT, D])
        y_junk = sb("y_junk", 84, [D])
        x_t = sb("x_t", 116, [KD, T])
        q_o = sb("q_o", 116, [2 * HEADS, T])
        z_tok = sb("z_tok", 116, [NT, D])
        y_acc = sb("y_acc", 116, [NT, D])
        q_rot = sb("q_rot", 148, [HEADS // 2, T])
        k_gqa = sb("k_gqa", 156, [2, T])
        v_gqa = sb("v_gqa", 160, [NT, 2, P])
        kr_hi, kr_lo = sb("kr_hi", 164, [2, T], F32R), sb("kr_lo", 168, [2, T], F32R)
        ckv = sb("ckv", 172, [KR, T])
        sq = sb("sq", 172, [T])
        sq_sum = sb("sq_sum", 174, [2, T])
        x_res = sb("x_res", 148, [NT, D])
        y_hi, y_lo = sb("y_hi", 148, [FCH, T], F32R), sb("y_lo", 164, [FCH, T], F32R)
        start_acc = [sb(f"start_acc{i}", 148 + 4 * i, [2, COLS]) for i in range(4)]
        mod_acc = [sb(f"mod_acc{i}", 180 + 2 * i, [COLS]) for i in range(3)]
        tab_b = sb("tab_b", 184, [2, NT, ROPE_B])
        tab_a = sb("tab_a", 186, [2, NT, P])
        tab_g = sb("tab_g", 190, [2, NT, P])
        tab_t = sb("tab_t", 190, [2, T])
        tok = sb("tok", 194, [NT, COLS])
        vec_rows = sb("vec_rows", 194, [2, P])
        h_f32 = [sb(f"h_f32_{i}", 194 + 2 * i, [T]) for i in range(4)]
        tmp = [sb(f"tmp{i}", 202 + 2 * i, [COLS]) for i in range(2)]
        c_hi, c_lo = sb("c_hi", 186, [KR, T], F32R), sb("c_lo", 194, [KR, T], F32R)
        pt_hi, pt_lo = sb("pt_hi", 186, [NT, T], F32R), sb("pt_lo", 194, [NT, T], F32R)
        ga_acc = sb("ga_acc", 202, [2, COLS])
        gm_acc = sb("gm_acc", 180, [D])
        part = sb("part", 188, [NT, COLS])
        comb = sb("comb", 196, [COLS])
        rows = sb("rows", 198, [2, COLS])
        tmp_u = [sb(f"tmp_u{i}", 188 + 2 * i, [T]) for i in range(2)]
        h2_f32 = [sb(f"h2_f32_{i}", 188 + 2 * i, [T]) for i in range(4)]
        tmp_y = [sb(f"tmp_y{i}", 192 + 2 * i, [T]) for i in range(2)]

        bank = [ctx.enter_context(nc.psum_tensor(f"bank{i}", [P, COLS], F32)) for i in range(8)]
        sets = (bank[0:4], bank[4:8])

        w_ada = a["w_ada"].rearrange("l (u q p) n -> (l u) p q n", q=QROWS, p=P)
        w_in = a["w_in"].rearrange("l (u q p) n -> (l u) p q n", q=QROWS, p=P)
        w_in4 = a["w_in"].rearrange("l (u q p) n -> (l u) p q n", q=4, p=P)
        w_kv = a["w_kv_b"].rearrange("l (u q p) (h e) -> (l u) p q h e", q=QROWS, p=P, h=HEADS)
        w_out = a["w_out"].rearrange("l (u q p) n -> (l u) p q n", q=QROWS, p=P)
        w_up = a["w_mlp_in"].rearrange("l (u q p) n -> (l u) p q n", q=QROWS, p=P)
        w_dn = a["w_mlp_out"].rearrange("l (u q p) n -> (l u) p q n", q=QROWS, p=P)
        x_d = a["x"].rearrange("b (t p) d -> (b t) p d", p=P)
        out_d = out.rearrange("b (t p) d -> (b t) p d", p=P)
        x1_d = x1_dram.rearrange("(t p) d -> t p d", p=P)
        b_rows = a["b_ada"]

        raw_landed = [sem(f"raw_landed{i}") for i in range(RING)]
        raw_used = sem("raw_used")
        hi_ready = sem("hi_ready")
        w_used = sem("w_used")
        x_landed = [sem(f"x_landed{i}") for i in range(NT)]
        vec_landed, const_landed, tab_landed = sem("vec_landed"), sem("const_landed"), sem("tab_landed")
        ones_ready = sem("ones_ready")
        dve_own, act_own, pool_own, pe_own = sem("dve_own"), sem("act_own"), sem("pool_own"), sem("pe_own")
        vec_turned, vec_ready, exp_c, silu_ready = sem("vec_turned"), sem("vec_ready"), sem("exp_c"), sem("silu_ready")
        x_sq, x_var, x_sqrt, x_normed, x_turned, x_t_ready = [sem(f"x_{n}") for n in ("sq", "var", "sqrt", "normed", "turned", "t_ready")]
        mod_summed, mod_reduced, mod_read = sem("mod_summed"), sem("mod_reduced"), sem("mod_read")
        pair_own, cols_ready, h_hi_ready, h_ready = sem("pair_own"), sem("cols_ready"), sem("h_hi_ready"), sem("h_ready")
        copied = sem("copied")
        c_sq, kr_copied, kr_turned, kr_sum, kr_hi_done, kr_ready = [sem(n) for n in ("c_sq", "kr_copied", "kr_turned", "kr_sum", "kr_hi_done", "kr_ready")]
        var_ready, sqrt_ready, rstd_ready, tok_ready = sem("var_ready"), sem("sqrt_ready"), sem("rstd_ready"), sem("tok_ready")
        turned, turned_out = sem("turned"), sem("turned_out")
        c_hi_done, c_ready = sem("c_hi_done"), sem("c_ready")
        qk_hi_done, qk_ready, v_hi_done, v_ready, rt_ready = [sem(n) for n in ("qk_hi_done", "qk_ready", "v_hi_done", "v_ready", "rt_ready")]
        y_zero = sem("y_zero")
        s_done, nb_ready, exp_done, p_ready, p_turned, pt_hi_done, pt_done, pv_done, o_done = [
            sem(n) for n in ("s_done", "nb_ready", "exp_done", "p_ready", "p_turned", "pt_hi_done", "pt_done", "pv_done", "o_done")]
        sq_ready, sq_reduced, r_var, r_sqrt, r_ready, r_free = [sem(n) for n in ("sq_ready", "sq_reduced", "r_var", "r_sqrt", "r_ready", "r_free")]
        o_hi_done, o_ready = sem("o_hi_done"), sem("o_ready")
        a_out, b_out, z_done, row_done = sem("a_out"), sem("b_out"), sem("z_done"), sem("row_done")
        ga_summed, ga_reduced, comb_ready, rows_landed = sem("ga_summed"), sem("ga_reduced"), sem("comb_ready"), sem("rows_landed")
        res_landed, x1_var, x1_sqrt, x1_ready, x1_sq, xn_ready, xn_turned = [
            sem(n) for n in ("res_landed", "x1_var", "x1_sqrt", "x1_ready", "x1_sq", "xn_ready", "xn_turned")]
        gm_reduced, gm_copied, comb_m_ready, x1_saved = sem("gm_reduced"), sem("gm_copied"), sem("comb_m_ready"), sem("x1_saved")
        h2_tmp, h2_hi_done, h2_ready = sem("h2_tmp"), sem("h2_hi_done"), sem("h2_ready")
        relu_done, y_done, y_hi_done, y_ready, mlp_free = sem("relu_done"), sem("y_done"), sem("y_hi_done"), sem("y_ready"), sem("mlp_free")
        y_sq, y_var, y_sqrt, x1_landed, out_ready, out_saved = [sem(n) for n in ("y_sq", "y_var", "y_sqrt", "x1_landed", "out_ready", "out_saved")]

        q_b = a["w_in"].rearrange("l (u q p) n -> (l u) p q n", q=QROWS, p=P)[:, :, :, 1536:3072].rearrange(
            "u p q (h e) -> u p q h e", h=HEADS)
        PROJ = [3072, 1024, 0, 512, "rot", "plain0", "plain1"]
        TOKENS_OUT = [True, True, True, True, True, False, False]
        TURNS = [4, 2, 4, 4, 4, 0, 0]
        STATS = {1: 1, 2: 2, 3: 4, 4: 4}
        TURNS_SUM = [int(np.sum(TURNS[:b])) for b in range(len(TURNS) + 1)]

        block = ctx.enter_context(nc.Block())

        @block.sync
        def _(sp):
            def load(at, source, n=COLS * QROWS, shape=None):
                if at.i is not None or at.const >= RING:
                    sp.wait_ge(raw_used, at.count(1, 1 - RING))
                dst = raw[at.slot()][:, :, :]
                if shape:
                    dst = dst.rearrange("p q n -> p (q n)")[:, 0:n].rearrange(*shape[0], **shape[1])
                sp.dma_start(dst, source).then_inc(raw_landed[at.slot()], 16)

            def ada(at, j, col):
                load(at, w_ada[j, :, :, bass.ds(col, COLS)])

            r = 0
            for name, n in (("c", KD), ("g_pre_attn", KD), ("g_pre_mlp", KD), ("g_out_a", HEADS), ("g_out_b", HEADS), ("g_ckv", KR)):
                sp.dma_start(vec_rows[r:r + n, 0, :], a[name].rearrange("l (k p) -> (l k) p", p=P)).then_inc(vec_landed, 16)
                r += n
            sp.dma_start(vec_rows[0:6 * KD, 1, :], a["b_ada"].rearrange("l (k p) -> (l k) p", p=P)).then_inc(vec_landed, 16)
            sp.dma_start(ident[:], a["ident"]).then_inc(const_landed, 16)
            def start_weights(cb):
                for j in range(2):
                    load(At(start_w(cb) + j), w_in[2 * cb + j, :, :, PROJ[0]:PROJ[0] + COLS])
                load(At(start_w(cb) + 2), w_in4[cb, :, :, 3584:3584 + ROPE_B], 4 * ROPE_B, (("p (q n) -> p q n",), {"q": 4}))

            for cb in range(NB):
                for g, col in enumerate((SC_A, SH_A)):
                    for j in range(UNITS_D):
                        ada(At(start_mod(cb, g) + j), j, col + COLS * cb)
                    if g == 0 and cb:
                        start_weights(cb - 1)
            start_weights(NB - 1)
            for b in range(1, PROJ_BLOCKS + 1):
                for j in range(UNITS_D):
                    r = PROJ_RAW + 2 * UNITS_D * (b - 1) + 2 * j
                    if PROJ[b] == "rot":
                        at = At(r)
                        sp.wait_ge(raw_used, at.count(1, 1 - RING))
                        for q in range(QROWS):
                            sp.dma_start(raw[at.slot()][:, q, :].rearrange("p (h e) -> p h e", h=HEADS),
                                         q_b[j, :, q, :, P:P + ROPE_B]).then_inc(raw_landed[at.slot()], 16)
                    elif isinstance(PROJ[b], str):
                        at = At(r)
                        sp.wait_ge(raw_used, at.count(1, 1 - RING))
                        h0 = 4 * int(PROJ[b][-1])
                        for q in range(QROWS):
                            sp.dma_start(raw[at.slot()][:, q, :].rearrange("p (h e) -> p h e", h=4),
                                         q_b[j, :, q, h0:h0 + 4, 0:P]).then_inc(raw_landed[at.slot()], 16)
                    else:
                        load(At(r), w_in[j, :, :, PROJ[b]:PROJ[b] + COLS])
                    ada(At(r + 1), j, SC_M + COLS * (b - 1) if b <= 4 else SH_M + COLS * (b - 5))
            for j in range(KV_UNITS):
                at = At(KV_RAW + 3 * j)
                sp.wait_ge(raw_used, at.count(1, 1 - RING))
                blk, u = j // 2, j % 2
                for q in range(QROWS):
                    src = w_kv[u, :, q, 4 * (blk % 2):4 * (blk % 2) + 4, P * (blk // 2):P * (blk // 2) + P]
                    sp.dma_start(raw[at.slot()][:, q, :].rearrange("p (h e) -> p h e", h=4), src).then_inc(raw_landed[at.slot()], 16)
                for m in range(2):
                    g, jj = divmod(2 * j + m, UNITS_D)
                    ada(At(KV_RAW + 3 * j + 1 + m), jj, SH_M + COLS * (2 + g))
            with sp.Fori(0, NB) as n:
                for j in range(UNITS_D):
                    at = At(OUT_RAW + 3 * j, n, OUT_RAW_N)
                    load(at, w_out[j, :, :, bass.ds(n * COLS, COLS)])
                    for m in range(2):
                        ada(at.plus(1 + m), 2 * (j % 4) + m, n * COLS + (GT_A if j < 4 else GT_M))
            with sp.Fori(0, GROUPS) as g:
                at = At(MLP_RAW, g, MLP_N)
                for f in range(2):
                    for j in range(UNITS_D):
                        load(at.plus(f * UNITS_D + j), w_up[j, :, :, bass.ds(g * (FCH * P) + f * COLS, COLS)])
                for n in range(NB):
                    for j in range(DN_U):
                        load(at.plus(UP_UNITS + n * DN_U + j), w_dn[g * DN_U + j, :, :, n * COLS:(n + 1) * COLS])
            sp.wait_ge(w_used, MLP_W + MLP_N * (GROUPS - 1) + UP_UNITS)
            sp.wait_ge(x1_saved, 16 * NT)
            for t in range(NT):
                sp.dma_start(x1_back[:, t, :], x1_d[t]).then_inc(x1_landed, 16)
            for t in range(NT):
                sp.wait_ge(out_ready, t + 1)
                sp.dma_start(out_d[t], x1_back[:, t, :]).then_inc(out_saved, 16)
            sp.wait_ge(out_saved, 16 * NT)

        landings = [0] * RING
        landed_at = {}
        for r in range(OUT_RAW):
            two = (KV_RAW <= r and (r - KV_RAW) % 3 == 0) or (
                PROJ_RAW <= r < KV_RAW and (r - PROJ_RAW) % 2 == 0 and isinstance(PROJ[1 + (r - PROJ_RAW) // (2 * UNITS_D)], str))
            landings[r % RING] += 32 if two else 16
            landed_at[r] = landings[r % RING]

        def wait_raw(engine, at):
            if at.const < OUT_RAW:
                assert at.i is None
                value = landed_at[at.const]
            else:
                slot = at.slot()
                before = landings[slot]
                nth = At(at.const - OUT_RAW, at.i, at.per)
                value = nth.count(16, before + 16, RING)
            engine.wait_ge(raw_landed[at.slot()], value)

        def stage_w(r, w):
            return r, w

        def at_out(n, j):
            if isinstance(n, int):
                return At(OUT_RAW + OUT_RAW_N * n + 3 * j), At(OUT_W + OUT_W_N * n + j)
            return At(OUT_RAW + 3 * j, n, OUT_RAW_N), At(OUT_W + j, n, OUT_W_N)

        def at_mlp(g, j):
            if isinstance(g, int):
                return At(MLP_RAW + MLP_N * g + j), At(MLP_W + MLP_N * g + j)
            return At(MLP_RAW + j, g, MLP_N), At(MLP_W + j, g, MLP_N)

        @block.scalar
        def _(act):
            own = Chain(act, act_own)

            def split_hi(r, w, pairs=None):
                wait_raw(act, r)
                if w.i is not None or w.const >= RING:
                    act.wait_ge(w_used, w.count(1, 1 - RING))
                for dst, src in (pairs or [(hi[w.slot()][:], raw[r.slot()][:])]):
                    ins = nc.scalar.activation(dst, src, ACT.Copy)
                ins.then_inc(hi_ready, 1)

            def proj_at(b, j):
                return At(PROJ_RAW + 2 * UNITS_D * (b - 1) + 2 * j), At(PROJ_W + UNITS_D * (b - 1) + j)

            for t in range(NT):
                act.dma_start(x_tok[:, t, :], x_d[t]).then_inc(x_landed[t], 16)
            act.wait_ge(vec_ready, 2)
            nc.scalar.activation(silu_t[:], gains[:, 0:KD], ACT.Exp, scale=-1.0).then_inc(exp_c, 1)
            for t in range(NT):
                act.wait_ge(x_landed[t], 16)
                nc.scalar.activation(x_t[:, 4 * t:4 * t + 4, :].rearrange("p k n -> p (k n)"), x_tok[:, t, :], ACT.Square,
                                         accum_out=stat[:, t, 0:1]).then_inc(x_sq, 1)
            act.wait_ge(x_var, 1)
            nc.scalar.activation(stat_s[:, :, 0:1], stat_v[:, :, 0:1], ACT.Sqrt).then_inc(x_sqrt, 1)
            for k in range(KD):
                act.wait_ge(x_turned, k + 1)
                nc.scalar.activation(x_t[:, k, :], bank[k % 4][:], ACT.Copy).then_inc(x_t_ready, 1)
            for cb in range(NB):
                for j in range(4):
                    k = 4 * cb + j
                    if j == 0:
                        act.wait_ge(cols_ready, cb + 1)
                    if k >= 4:
                        act.wait_ge(h_ready, k - 3)
                    g, b = gsc_a[:, cb % 2, j:j + 1], shf_a[:, cb % 2, j:j + 1]
                    nc.scalar.activation(h_f32[j][:], x_t[:, k, :], ACT.Identity, scale=g, bias=b)
                    nc.scalar.activation(h_hi[:, k, :], x_t[:, k, :], ACT.Identity, scale=g, bias=b).then_inc(h_hi_ready, 1)
                r, w = start_w(cb), START_W * cb
                for j in range(2):
                    split_hi(At(r + j), At(w + j))
                s = At(w + 2).slot()
                dup = hi[s][:].rearrange("p q n -> p (q n)")[:, 0:4 * P].rearrange("p (k m e) -> p k m e", k=4, m=2)
                src = raw[At(r + 2).slot()][:].rearrange("p q n -> p (q n)")[:, 0:4 * ROPE_B].rearrange("p (k e) -> p k e", k=4)
                split_hi(At(r + 2), At(w + 2), [(dup[:, :, m, :], src) for m in range(2)])
                if cb == 2:
                    act.dma_start(rot[:], a["rot"]).then_inc(tab_landed, 16)
                    act.dma_start(tab_t[:], a["tab_t"]).then_inc(tab_landed, 16)
                    act.dma_start(tab_a[:], a["tab_a"]).then_inc(tab_landed, 16)
                    act.dma_start(tab_b[:], a["tab_b"]).then_inc(tab_landed, 16)
                    act.dma_start(g_q[:], a["g_q_a"].partition_broadcast(P)[:, 0, :]).then_inc(tab_landed, 16)
                    act.dma_start(g_k[:], a["g_k_a"].partition_broadcast(P)[:, 0, :]).then_inc(tab_landed, 16)

            def copy_out(b):
                s = sets[b % 2]
                if b == 0:
                    for t in range(NT):
                        nc.scalar.activation(tok[:, t, :], s[t][:], ACT.Square, accum_out=stat[:, t, 0:1]).then_inc(c_sq, 1)
                elif b == 1:
                    for t in range(NT):
                        nc.scalar.activation(tok[:, t, 0:2 * P], s[t][:, 0:2 * P], ACT.Copy)
                        nc.scalar.activation(v_gqa[:, t, :, :].rearrange("p g e -> p (g e)"), s[t][:, 2 * P:4 * P], ACT.Copy).then_inc(copied, 1)
                elif b <= 4:
                    for t in range(NT):
                        nc.scalar.activation(tok[:, t, :], s[t][:], ACT.Copy).then_inc(copied, 1)
                elif b <= 6:
                    for n in range(4):
                        nc.scalar.activation(q_o[:, HEADS + 4 * (b - 5) + n, :], s[n][:], ACT.Copy).then_inc(copied, 1)
                elif b <= 8:
                    for n in range(4):
                        nc.scalar.activation(k_nope[:, 4 * (b - 7) + n, :], s[n][:], ACT.Copy).then_inc(copied, 1)
                else:
                    for t in range(NT):
                        dst = v_lat[:, t, 4 * (b - 9):4 * (b - 9) + 4, :].rearrange("p h e -> p (h e)")
                        nc.scalar.activation(dst, s[t][:], ACT.Copy).then_inc(copied, 1)

            def turned_copy(b):
                for n in range(TURNS[b]):
                    act.wait_ge(turned, TURNS_SUM[b] + n + 1)
                    src = sets[b % 2][n][:]
                    if b == 0:
                        k = 3 * KD + 2 * HEADS + n
                        nc.scalar.activation(ckv[:, n, :], src, ACT.Copy, scale=gains[:, k:k + 1]).then_inc(turned_out, 1)
                    elif b == 1:
                        nc.scalar.activation(k_gqa[:, n, :], src, ACT.Copy).then_inc(turned_out, 1)
                    elif b <= 3:
                        nc.scalar.activation(q_o[:, 4 * (b - 2) + n, :], src, ACT.Copy).then_inc(turned_out, 1)
                    else:
                        nc.scalar.activation(q_rot[:, n, :], src, ACT.Copy).then_inc(turned_out, 1)

            roots = 0
            for b in range(1, PROJ_BLOCKS + 1):
                for j in range(UNITS_D):
                    split_hi(*proj_at(b, j))
                    if b == 1 and j == 0:
                        act.wait_ge(w_used, PROJ_W)
                        nc.scalar.activation(tmp[0][:], bank[4][:], ACT.Copy).then_inc(kr_copied, 1)
                    if j == 2 and b >= 2:
                        turned_copy(b - 2)
                    if j == 3:
                        if b >= 2:
                            act.wait_ge(w_used, PROJ_W + UNITS_D * (b - 1))
                            if b <= 5 :
                                act.wait_ge(turned, TURNS_SUM[b - 1])
                        copy_out(b - 1)
                    if j == 4 and b in (1, 2, 3, 4):
                        roots += 1
                        act.wait_ge(var_ready, roots)
                        n = STATS[b]
                        nc.scalar.activation(stat_s[:, :, 0:n], stat_v[:, :, 0:n], ACT.Sqrt).then_inc(sqrt_ready, 1)
                    if j == 5 and b == 1:
                        act.wait_ge(rstd_ready, 1)
                        for t in range(NT):
                            nc.scalar.activation(tok[:, t, :], sets[0][t][:], ACT.Copy, scale=rstd[:, t, 0:1]).then_inc(copied, 1)
                    if j == 7 and b == 1:
                        act.wait_ge(kr_sum, 1)
                        nc.scalar.activation(kr_hi[0:64, 0, :], tmp[0][0:64, :], ACT.Copy)
                        nc.scalar.activation(kr_hi[64:128, 1, :], tmp[0][64:128, :], ACT.Copy).then_inc(kr_hi_done, 1)
                    if j == 5 and b == 6:
                        act.wait_ge(turned_out, TURNS_SUM[1])
                        act.wait_ge(tok_ready, 4 * 4)
                        act.wait_ge(turned, TURNS_SUM[5])
                        for k in range(KR):
                            nc.scalar.activation(c_hi[:, k, :], ckv[:, k, :], ACT.Copy).then_inc(c_hi_done, 1)
            for j in range(KV_UNITS):
                split_hi(At(KV_RAW + 3 * j), At(KV_W + j))
                if j % 2 and j >= 3:
                    b = 6 + (j - 3) // 2
                    act.wait_ge(w_used, KV_W if b == 6 else KV_W + 2 * (b - 6))
                    copy_out(b)
            def out_his(n, js):
                for j in js:
                    split_hi(*at_out(n, j))
            for b in (9, 10):
                if b == 9:
                    split_hi(*at_out(0, 0))
                    split_hi(*at_out(0, 1))
                act.wait_ge(w_used, KV_W + 2 * (b - 6))
                copy_out(b)
            split_hi(*at_out(0, 2))
            split_hi(*at_out(0, 3))

            flat = lambda x: x.rearrange("p a n -> p (a n)")

            def stage_head(grp, h, H):
                if not (isinstance(H, int) and H == 0):
                    act.wait_ge(s_done, H * 4)
                nc.scalar.activation(stage["q"][0][:], flat(q_o[:, bass.ds(h + grp * HEADS, 1), :]), ACT.Copy)
                if grp:
                    nc.scalar.activation(stage["qr"][0][:], flat(q_rot[:, bass.ds(h // 2, 1), :]), ACT.Copy)
                src = k_nope[:, bass.ds(h, 1), :] if grp else k_gqa[:, bass.ds(h // 4, 1), :]
                nc.scalar.activation(stage["k"][0][:], flat(src), ACT.Copy).then_inc(qk_hi_done, 1)

            def stage_values(grp, h, H):
                src = v_lat[:, :, bass.ds(h, 1), :] if grp else v_gqa[:, :, bass.ds(h // 4, 1), :]
                nc.scalar.activation(stage["v"][0][:].rearrange("p (c e) -> p c e", c=NT), src.rearrange("p t a e -> p t (a e)"), ACT.Copy).then_inc(v_hi_done, 1)

            def exp(grp, t, H):
                act.wait_ge(nb_ready, H * 4 + (t + 1))
                nc.scalar.activation(prob[:, t, :], bank[t][:], ACT.Exp, bias=nbias[:, t:t + 1],
                                     scale=SCALE_B if grp else SCALE_A, accum_out=total[:, t:t + 1]).then_inc(exp_done, 1)

            def head_out(H):
                act.wait_ge(pv_done, H)
                nc.scalar.activation(flat(q_o[:, bass.ds(H - 1, 1), :]), bank[6][:], ACT.Copy)
                act.wait_ge(sq_ready, H - 1)
                nc.scalar.activation(sq[:], bank[6][:], ACT.Square).then_inc(o_done, 1)

            def attend(cur, nxt, after, first=False):
                H = cur[2]
                for t in range(NT):
                    act.wait_ge(p_turned, H * 4 + (t + 1))
                    if t == 0:
                        act.wait_ge(pv_done, H)
                    nc.scalar.activation(pt_hi[:, :, t * P:(t + 1) * P], bank[4 + t % 2][:].rearrange("p (c n) -> p c n", c=NT), ACT.Copy).then_inc(pt_hi_done, 1)
                    if t == 0:
                        if not first:
                            head_out(H)
                        stage_values(*cur)
                    if t and nxt:
                        exp(nxt[0], t - 1, nxt[2])
                if nxt:
                    exp(nxt[0], NT - 1, nxt[2])
                if after:
                    stage_head(*after)

            A = lambda h: (0, h, h)
            B = lambda h: (1, h, h + HEADS)
            stage_head(*A(0))
            for t in range(NT):
                exp(0, t, 0)
            stage_head(*A(1))
            attend(A(0), A(1), A(2), first=True)
            with act.Fori(1, HEADS - 2) as h:
                attend(A(h), A(h + 1), A(h + 2))
            attend(A(HEADS - 2), A(HEADS - 1), B(0))
            attend(A(HEADS - 1), B(0), B(1))
            with act.Fori(0, HEADS - 2) as h:
                attend(B(h), B(h + 1), B(h + 2))
            attend(B(HEADS - 2), B(HEADS - 1), None)
            attend(B(HEADS - 1), None, None)
            head_out(2 * HEADS)

            act.wait_ge(s_done, 4 * 2 * HEADS)
            act.wait_ge(pt_done, 4 * 2 * HEADS + 2)
            for k in range(KD):
                if k == KD - 1:
                    act.wait_ge(o_done, 2 * HEADS)
                nc.scalar.activation(o_hi[:, k, :], q_o[:, k, :], ACT.Copy, scale=gains[:, 3 * KD + k:3 * KD + k + 1]).then_inc(o_hi_done, 1)
            act.wait_ge(r_var, 1)
            nc.scalar.activation(stat_s[:, 0:2, :], stat_v[:, 0:2, :], ACT.Sqrt).then_inc(r_sqrt, 1)

            def a_part(n):
                act.wait_ge(r_ready, 1)
                if isinstance(n, int):
                    act.wait_ge(w_used, OUT_W + OUT_W_N * n + 4)
                else:
                    act.wait_ge(w_used, n * OUT_W_N + (OUT_W + 4))
                act.wait_ge(z_done, n * 4)
                for t in range(NT):
                    nc.scalar.activation(part[:, t, :], bank[t][:], ACT.Copy, scale=r_out[:, 0, t:t + 1]).then_inc(a_out, 1)

            def squares(n):
                for t in range(NT):
                    act.wait_ge(z_done, n * 4 + (t + 1))
                    dst = row_sq[:, t, bass.ds(n, 1)]
                    nc.scalar.activation(part[:, t, :], part[:, t, :], ACT.Square, accum_out=dst).then_inc(row_done, 1)

            with act.Fori(0, NB - 1) as n:
                out_his(n, range(4, 8))
                a_part(n)
                for j in range(4):
                    split_hi(At(OUT_RAW + OUT_RAW_N + 3 * j, n, OUT_RAW_N), At(OUT_W + OUT_W_N + j, n, OUT_W_N))
                squares(n)
            out_his(NB - 1, range(4, 8))
            a_part(NB - 1)
            for j in range(4):
                split_hi(*at_mlp(0, j))
            squares(NB - 1)

            act.wait_ge(x1_var, 1)
            nc.scalar.activation(stat_s[:, :, 0:1], stat_v[:, :, 0:1], ACT.Sqrt).then_inc(x1_sqrt, 1)
            act.wait_ge(gm_reduced, 1)
            for n in range(NB):
                nc.scalar.activation(gm_acc[:, n * COLS:(n + 1) * COLS], bank[4 + n][:], ACT.Copy).then_inc(gm_copied, 1)
            for t in range(NT):
                act.wait_ge(x1_ready, t + 1)
                act.dma_start(x1_d[t], x_res[:, t, :]).then_inc(x1_saved, 16)
                nc.scalar.activation(z_tok[:, t, :], x_res[:, t, :], ACT.Square, accum_out=stat[:, t, 1:2]).then_inc(x1_sq, 1)
                act.wait_ge(x1_var, t + 2)
                nc.scalar.activation(stat_s[:, t, 1:2], stat_v[:, t, 1:2], ACT.Sqrt).then_inc(x1_sqrt, 1)
            for k in range(KD):
                act.wait_ge(h2_tmp, k + 1)
                nc.scalar.activation(h2_hi[:, k, :], tmp_u[k % 2][:], ACT.Copy).then_inc(h2_hi_done, 1)

            def relu_square(g, f):
                n0 = f * 4
                def relu(c):
                    nc.scalar.activation(tmp_u[c % 2][:], sets[f][c][:], ACT.Relu).then_inc(relu_done, 1)
                def square_hi(c):
                    act.wait_ge(y_done, g * FCH + (n0 + c + 1))
                    nc.scalar.activation(y_hi[:, n0 + c, :], tmp_y[c % 2][:], ACT.Copy).then_inc(y_hi_done, 1)
                relu(0)
                relu(1)
                for c in range(4):
                    square_hi(c)
                    if c + 2 < 4:
                        relu(c + 2)

            def mlp_group(g, first):
                for j in range(4 if first else 0, MLP_N):
                    r, w = at_mlp(g, j)
                    split_hi(r, w)
                    if j == UNITS_D + 3:
                        act.wait_ge(w_used, w.count(1, 1 - 4))
                        act.wait_ge(y_ready, g * FCH)
                        relu_square(g, 0)
                    if j == UP_UNITS + 3:
                        act.wait_ge(w_used, w.count(1, 1 - 4))
                        relu_square(g, 1)

            act.wait_ge(x1_saved, 16 * NT)
            mlp_group(0, True)
            with act.Fori(1, GROUPS) as g:
                mlp_group(g, False)
            for t in range(NT):
                act.wait_ge(mlp_free, 4 * (6 * GROUPS) + 4)
                act.wait_ge(y_sq, t)
                nc.scalar.activation(y_junk[:], y_acc[:, t, :], ACT.Square, accum_out=stat[:, t, 2:3]).then_inc(y_sq, 1)
            act.wait_ge(y_var, 1)
            nc.scalar.activation(stat_s[:, :, 2:3], stat_v[:, :, 2:3], ACT.Sqrt).then_inc(y_sqrt, 1)

        @block.vector
        def _(dve):
            own = Chain(dve, dve_own)
            tt, ts, stt = nc.vector.tensor_tensor, nc.vector.tensor_scalar, nc.vector.scalar_tensor_tensor

            def split_lo(r, w, pairs=None):
                dve.wait_ge(hi_ready, w.count(1, 1))
                for dst, src, high in (pairs or [(lo[w.slot()][:], raw[r.slot()][:], hi[w.slot()][:])]):
                    ins = tt(dst, src, high.bitcast(F32), ALU.subtract)
                ins.then_inc(raw_used, 1)

            def modulate(at, j, acc, done=None):
                wait_raw(dve, at)
                for q in range(QROWS):
                    k = QROWS * j + q
                    w = raw[at.slot()][:, q, :]
                    if k == 0:
                        ins = ts(acc, w, silu_c[:, 0:1], None, ALU.mult)
                    else:
                        ins = stt(acc, w, silu_c[:, k:k + 1], acc, ALU.mult, ALU.add)
                    if q == QROWS - 1:
                        ins.then_inc(raw_used, 1)
                        dve.wait_ge(raw_used, at.count(1, 1))
                    else:
                        own.step(ins)

            def rsqrt_tail(dst, src):
                own.step(nc.vector.reciprocal(dst, src))

            for n, dst in ((0, gains), (1, bias)):
                dve.wait_ge(vec_turned, n + 1)
                width = 3 * KD + 2 * HEADS + KR if n == 0 else 6 * KD
                nc.vector.tensor_copy(dst[:], bank[4 + n][:, 0:width]).then_inc(vec_ready, 1)
            dve.wait_ge(exp_c, 1)
            own.step(ts(silu_t[:], silu_t[:], 1.0, None, ALU.add))
            own.step(nc.vector.reciprocal(silu_t[:], silu_t[:]))
            own.step(tt(silu_c[:], gains[:, 0:KD], silu_t[:], ALU.mult))

            def modulate_pairs(cb, g):
                acc = start_acc[2 * (cb % 2) + g]
                for j in range(UNITS_D):
                    at = At(start_mod(cb, g) + j)
                    wait_raw(dve, at)
                    for q in range(QROWS):
                        k, w = QROWS * j + q, raw[at.slot()][:, q, :]
                        if j == 0:
                            ins = ts(acc[:, q, :], w, silu_c[:, k:k + 1], None, ALU.mult)
                        else:
                            if q == 0:
                                dve.wait_ge(pair_own, pairs[0])
                            else:
                                dve.wait_ge(raw_used, at.const)
                            ins = stt(acc[:, q, :], w, silu_c[:, k:k + 1], acc[:, q, :], ALU.mult, ALU.add)
                        if q == 0:
                            ins.then_inc(pair_own, 1)
                            pairs[0] += 1
                        else:
                            ins.then_inc(raw_used, 1)
                dve.wait_ge(pair_own, pairs[0])
                dve.wait_ge(raw_used, at.const + 1)
                dve.sem_inc(mod_summed, 1)

            pairs = [0]

            dve.wait_ge(x_sq, NT)
            ts(stat_v[:, :, 0:1], stat[:, :, 0:1], 1.0 / D, EPS, ALU.mult, ALU.add).then_inc(x_var, 1)
            dve.wait_ge(x_sqrt, 1)
            own.step(nc.vector.reciprocal(rstd[:, :, 0:1], stat_s[:, :, 0:1]))
            for t in range(NT):
                ts(x_tok[:, t, :], x_tok[:, t, :], rstd[:, t, 0:1], None, ALU.mult).then_inc(x_normed, 1)

            def columns(cb):
                dve.wait_ge(mod_reduced, cb + 1)
                s = cb % 2
                own.step(tt(gsc_a[:, s, :], bank[5][:, 0:4], bias[:, KD + 4 * cb:KD + 4 * cb + 4], ALU.add))
                tt(shf_a[:, s, :], bank[5][:, 4:8], bias[:, 4 * cb:4 * cb + 4], ALU.add).then_inc(mod_read, 1)
                stt(gsc_a[:, s, :], gsc_a[:, s, :], 1.0, gains[:, KD + 4 * cb:KD + 4 * cb + 4], ALU.add, ALU.mult).then_inc(cols_ready, 1)

            def start_lo(cb):
                for j in range(4):
                    k = 4 * cb + j
                    dve.wait_ge(h_hi_ready, k + 1)
                    tt(h_lo[:, k, :], h_f32[j][:], h_hi[:, k, :].bitcast(F32), ALU.subtract).then_inc(h_ready, 1)
                r, w = start_w(cb), START_W * cb
                for j in range(2):
                    split_lo(At(r + j), At(w + j))
                four = lambda t: t[:].rearrange("p q n -> p (q n)")[:, 0:4 * P].rearrange("p (k m e) -> p k m e", k=4, m=2)
                s = At(w + 2).slot()
                src = raw[At(r + 2).slot()][:].rearrange("p q n -> p (q n)")[:, 0:4 * ROPE_B].rearrange("p (k e) -> p k e", k=4)
                split_lo(At(r + 2), At(w + 2), [(four(lo[s])[:, :, m, :], src, four(hi[s])[:, :, m, :]) for m in range(2)])

            for cb in range(NB):
                modulate_pairs(cb, 0)
                if cb:
                    start_lo(cb - 1)
                modulate_pairs(cb, 1)
                columns(cb)
            start_lo(NB - 1)

            def fold(g):
                own.step(tt(tab_g[:, 0], tab_a[:, 0], g[:].unsqueeze(1).broadcast_to([P, NT, P]), ALU.mult))
                swap = lambda x, s: x.rearrange("p (r s e) -> p r s e", r=2, s=2)[:, :, s, :]
                for s in range(2):
                    own.step(tt(tab_g[:, 1].rearrange("p t (r s e) -> p t r s e", r=2, s=2)[:, :, :, s, :],
                                tab_a[:, 1].rearrange("p t (r s e) -> p t r s e", r=2, s=2)[:, :, :, s, :],
                                swap(g[:], 1 - s).unsqueeze(1).broadcast_to([P, NT, 2, 32]), ALU.mult))

            def rope(t, heads, table, width, done):
                e = width // 4
                x = tok[:, t, 0:heads * width].rearrange("p (h d) -> p h d", h=heads)
                ca = tmp[0][:, 0:heads * width].rearrange("p (h d) -> p h d", h=heads)
                cos = table[:, 0, t, :].unsqueeze(1).broadcast_to([P, heads, width])
                tt(ca, x, cos, ALU.mult)
                for s in range(2):
                    for r in range(2):
                        at, of = r * 2 * e + s * e, r * 2 * e + (1 - s) * e
                        sin = table[:, 1, t, at:at + e].unsqueeze(1).broadcast_to([P, heads, e])
                        ins = tt(tmp[1][:, 0:heads * width].rearrange("p (h d) -> p h d", h=heads)[:, :, at:at + e], x[:, :, of:of + e], sin, ALU.mult)
                own.step(ins)
                tt(tok[:, t, 0:heads * width], tmp[0][:, 0:heads * width], tmp[1][:, 0:heads * width], ALU.add).then_inc(tok_ready, 1)

            copies = 0
            for b in range(1, PROJ_BLOCKS + 1):
                heads = {2: 2, 3: 4, 4: 4, 5: 8}.get(b)
                for j in range(UNITS_D):
                    r = PROJ_RAW + 2 * UNITS_D * (b - 1) + 2 * j
                    split_lo(At(r), At(PROJ_W + UNITS_D * (b - 1) + j))
                    if j == 0 and b >= 3:
                        g = b - 3
                        dve.wait_ge(mod_reduced, NB + g + 1)
                        nc.vector.tensor_copy(mod_m[:, 4 * g:4 * g + 4], sets[b % 2][0][:, 0:4]).then_inc(mod_read, 1)
                    modulate(At(r + 1), j, mod_acc[(b - 1) % 2][:])
                    if j == UNITS_D - 1:
                        dve.sem_inc(mod_summed, 1)
                    if b == 1:
                        if j == 3:
                            dve.wait_ge(c_sq, NT)
                            ts(stat_v[:, :, 0:1], stat[:, :, 0:1], 1.0 / RANK, EPS, ALU.mult, ALU.add).then_inc(var_ready, 1)
                        if j == 4:
                            dve.wait_ge(sqrt_ready, 1)
                            nc.vector.reciprocal(rstd[:, :, 0:1], stat_s[:, :, 0:1]).then_inc(rstd_ready, 1)
                        if j == 6:
                            dve.wait_ge(kr_turned, 1)
                            dve.wait_ge(tab_landed, 16 * 6)
                            own.step(tt(tmp[0][:], tmp[0][:], tab_t[:, 0], ALU.mult))
                            own.step(tt(tmp[1][:], bank[0][:], tab_t[:, 1], ALU.mult))
                            tt(tmp[0][:], tmp[0][:], tmp[1][:], ALU.add).then_inc(kr_sum, 1)
                        if j == 7:
                            dve.wait_ge(kr_hi_done, 1)
                            tt(kr_lo[0:64, 0, :], tmp[0][0:64, :], kr_hi[0:64, 0, :].bitcast(F32), ALU.subtract)
                            tt(kr_lo[64:128, 1, :], tmp[0][64:128, :], kr_hi[64:128, 1, :].bitcast(F32), ALU.subtract).then_inc(kr_ready, 1)
                            dve.wait_ge(kr_ready, 1)
                            fold(g_k)
                    elif heads:
                        if j == 3:
                            copies += 4
                        if j == 3 and b <= 4:
                            for t in range(NT):
                                dve.wait_ge(copied, 4 * (b - 1) + t + 1)
                                n = heads * P
                                own.step(tt(tmp[t % 2][:, 0:n], tok[:, t, 0:n], tok[:, t, 0:n], ALU.mult))
                                own.step(nc.vector.tensor_reduce(stat[:, t, 0:heads], tmp[t % 2][:, 0:n].rearrange("p (h d) -> p h d", h=heads), AX.X, ALU.add))
                            ts(stat_v[:, :, 0:heads], stat[:, :, 0:heads], 1.0 / P, EPS, ALU.mult, ALU.add).then_inc(var_ready, 1)
                        if j == 4 and b <= 4:
                            dve.wait_ge(sqrt_ready, b)
                            own.step(nc.vector.reciprocal(rstd[:, :, 0:heads], stat_s[:, :, 0:heads]))
                            if b == 3:
                                fold(g_q)
                        if j >= 4:
                            t = j - 4
                            dve.wait_ge(copied, 4 * (b - 1) + t + 1)
                            if b <= 4:
                                x = tok[:, t, 0:heads * P].rearrange("p (h d) -> p h d", h=heads)
                                own.step(tt(x, x, rstd[:, t, 0:heads].unsqueeze(2).broadcast_to([P, heads, P]), ALU.mult))
                                rope(t, heads, tab_g, P, b)
                            else:
                                rope(t, heads, tab_b, ROPE_B, b)
                if b == 6:
                    for k in range(KR):
                        dve.wait_ge(c_hi_done, k + 1)
                        tt(c_lo[:, k, :], ckv[:, k, :], c_hi[:, k, :].bitcast(F32), ALU.subtract).then_inc(c_ready, 1)

            for j in range(KV_UNITS):
                split_lo(At(KV_RAW + 3 * j), At(KV_W + j))
                for m in range(2):
                    g, jj = divmod(2 * j + m, UNITS_D)
                    if jj == 0 and g == 0:
                        dve.wait_ge(mod_reduced, NB + 5)
                        nc.vector.tensor_copy(mod_m[:, 16:20], sets[1][0][:, 0:4]).then_inc(mod_read, 1)
                    modulate(At(KV_RAW + 3 * j + 1 + m), jj, mod_acc[(0, 2)[g]][:])
                    if jj == UNITS_D - 1:
                        dve.sem_inc(mod_summed, 1)

            def out_units(n, js, nn=None):
                for j in js:
                    r, w = at_out(n, j) if nn is None else (At(OUT_RAW + OUT_RAW_N + 3 * j, nn, OUT_RAW_N), At(OUT_W + OUT_W_N + j, nn, OUT_W_N))
                    split_lo(r, w)
                    at_n = n if nn is None else nn + 1
                    for m in range(2):
                        if j < 4:
                            acc = ga_acc[:, bass.ds(at_n & 1, 1), :].rearrange("p a n -> p (a n)") if not isinstance(at_n, int) else ga_acc[:, at_n & 1, :]
                        else:
                            acc = gm_acc[:, bass.ds(at_n * COLS, COLS)]
                        modulate(r.plus(1 + m), 2 * (j % 4) + m, acc)
                    if j == 3:
                        dve.sem_inc(ga_summed, 1)
                    if nn is not None and j == 2:
                        combine(nn)

            out_units(0, range(4))

            flat = lambda x: x.rearrange("p a n -> p (a n)")

            def stage_head(grp, h, H):
                dve.wait_ge(qk_hi_done, H + 1)
                low = lambda name, src: tt(stage[name][1][:], src, stage[name][0][:].bitcast(F32), ALU.subtract)
                low("q", flat(q_o[:, bass.ds(h + grp * HEADS, 1), :]))
                if grp:
                    low("qr", flat(q_rot[:, bass.ds(h // 2, 1), :]))
                low("k", flat(k_nope[:, bass.ds(h, 1), :] if grp else k_gqa[:, bass.ds(h // 4, 1), :])).then_inc(qk_ready, 1)

            def stage_values(grp, h, H):
                dve.wait_ge(v_hi_done, H + 1)
                src = v_lat[:, :, bass.ds(h, 1), :] if grp else v_gqa[:, :, bass.ds(h // 4, 1), :]
                cut = lambda x: x.rearrange("p (c e) -> p c e", c=NT)
                tt(cut(stage["v"][1][:]), src.rearrange("p t a e -> p t (a e)"), cut(stage["v"][0][:].bitcast(F32)), ALU.subtract).then_inc(v_ready, 1)

            def row_max(grp, t, H):
                dve.wait_ge(s_done, H * 4 + (t + 1))
                own.step(nc.vector.reduce_max(top[:, t:t + 1], bank[t][:], AX.X))
                ts(nbias[:, t:t + 1], top[:, t:t + 1], -(SCALE_B if grp else SCALE_A), None, ALU.mult).then_inc(nb_ready, 1)

            def invert(t, H):
                dve.wait_ge(exp_done, H * 4 + (t + 1))
                nc.vector.reciprocal(rtotal[:, t:t + 1], total[:, t:t + 1]).then_inc(rt_ready, 1)

            def attend(cur, nxt, after):
                H = cur[2]
                for t in range(NT):
                    dve.wait_ge(pt_hi_done, H * 4 + (t + 1))
                    tt(pt_lo[:, :, t * P:(t + 1) * P], bank[4 + t % 2][:].rearrange("p (c n) -> p c n", c=NT),
                       pt_hi[:, :, t * P:(t + 1) * P].bitcast(F32), ALU.subtract).then_inc(pt_done, 1)
                    if nxt:
                        row_max(nxt[0], t, nxt[2])
                    if t == 0:
                        stage_values(*cur)
                    if nxt and t >= 2:
                        invert(t - 2, nxt[2])
                if nxt:
                    invert(NT - 2, nxt[2])
                    invert(NT - 1, nxt[2])
                if after:
                    stage_head(*after)

            A = lambda h: (0, h, h)
            B = lambda h: (1, h, h + HEADS)
            dve.sem_inc(pt_done, 2)
            stage_head(*A(0))
            for t in range(NT):
                row_max(0, t, 0)
                if t:
                    invert(t - 1, 0)
            invert(NT - 1, 0)
            stage_head(*A(1))
            attend(A(0), A(1), A(2))
            with dve.Fori(1, HEADS - 2) as h:
                own.enter(h - 1, NT)
                attend(A(h), A(h + 1), A(h + 2))
            own.leave(HEADS - 3)
            attend(A(HEADS - 2), A(HEADS - 1), B(0))
            attend(A(HEADS - 1), B(0), B(1))
            with dve.Fori(0, HEADS - 2) as h:
                own.enter(h, NT)
                attend(B(h), B(h + 1), B(h + 2))
            own.leave(HEADS - 2)
            attend(B(HEADS - 2), B(HEADS - 1), None)
            attend(B(HEADS - 1), None, None)

            dve.wait_ge(mod_reduced, NB + 8)
            own.step(nc.vector.tensor_copy(mod_m[:, 20:32], bank[7][:, 0:12]))
            own.step(tt(gsc_m[:], mod_m[:, 0:KD], bias[:, SC_M // P:SC_M // P + KD], ALU.add))
            own.step(stt(gsc_m[:], gsc_m[:], 1.0, gains[:, 2 * KD:3 * KD], ALU.add, ALU.mult))
            tt(shf_m[:], mod_m[:, KD:2 * KD], bias[:, SH_M // P:SH_M // P + KD], ALU.add).then_inc(mod_read, 1)

            for k in range(KD):
                dve.wait_ge(o_hi_done, k + 1)
                stt(o_lo[:, k, :], q_o[:, k, :], gains[:, 3 * KD + k:3 * KD + k + 1], o_hi[:, k, :].bitcast(F32), ALU.mult, ALU.subtract).then_inc(o_ready, 1)
            dve.wait_ge(sq_reduced, 1)
            own.step(ts(stat_v[:, 0:2, :], bank[7][:, 16:24].rearrange("p (g t) -> p g t", g=2), 1.0 / (HEADS * P), EPS, ALU.mult, ALU.add))
            dve.sem_inc(r_var, 1)
            dve.wait_ge(r_sqrt, 1)
            nc.vector.reciprocal(r_out[:], stat_s[:, 0:2, :]).then_inc(r_ready, 1)
            dve.wait_ge(r_ready, 1)

            def combine(n):
                dve.wait_ge(ga_reduced, n + 1)
                dve.wait_ge(rows_landed, n * 32 + 32)
                own.step(tt(comb[:], bank[0][:], rows[:, 0, :], ALU.add))
                tt(comb[:], comb[:], rows[:, 1, :], ALU.mult).then_inc(comb_ready, 1)

            def b_part(n):
                dve.wait_ge(w_used, n * OUT_W_N + (OUT_W + OUT_W_N))
                dve.wait_ge(comb_ready, n + 1)
                dve.wait_ge(a_out, n * 4 + 4)
                for t in range(NT):
                    own.step(stt(part[:, t, :], bank[4 + t][:], r_out[:, 1, t:t + 1], part[:, t, :], ALU.mult, ALU.add))
                    tt(z_tok[:, t, bass.ds(n * COLS, COLS)], part[:, t, :], comb[:], ALU.mult).then_inc(z_done, 1)

            with dve.Fori(0, NB - 1) as n:
                own.enter(n, 8 + 8 + 1 + NT)
                out_units(n, range(4, 8))
                out_units(None, range(4), nn=n)
                b_part(n)
            own.leave(NB - 1)
            out_units(NB - 1, range(4, 8))
            for j in range(4):
                split_lo(*at_mlp(0, j))
                if j == 2:
                    combine(NB - 1)
            b_part(NB - 1)

            dve.wait_ge(row_done, NB * 4)
            own.step(nc.vector.tensor_reduce(stat[:, :, 0:1], row_sq[:], AX.X, ALU.add))
            ts(stat_v[:, :, 0:1], stat[:, :, 0:1], 1.0 / D, EPS, ALU.mult, ALU.add).then_inc(x1_var, 1)
            dve.wait_ge(x1_sqrt, 1)
            own.step(nc.vector.reciprocal(rstd[:, :, 0:1], stat_s[:, :, 0:1]))
            dve.wait_ge(res_landed, 16 * NT)

            def scale_x1(t):
                dve.wait_ge(x1_sq, t + 1)
                ts(stat_v[:, t, 1:2], stat[:, t, 1:2], 1.0 / D, EPS, ALU.mult, ALU.add).then_inc(x1_var, 1)
                dve.wait_ge(x1_sqrt, t + 2)
                own.step(nc.vector.reciprocal(rstd[:, t, 1:2], stat_s[:, t, 1:2]))
                ts(z_tok[:, t, :], x_res[:, t, :], rstd[:, t, 1:2], None, ALU.mult).then_inc(xn_ready, 1)

            for t in range(NT):
                stt(x_res[:, t, :], z_tok[:, t, :], rstd[:, t, 0:1], x_res[:, t, :], ALU.mult, ALU.add).then_inc(x1_ready, 1)
                if t:
                    scale_x1(t - 1)
            scale_x1(NT - 1)
            for k in range(KD):
                dve.wait_ge(xn_turned, k + 1)
                if k >= 2:
                    dve.wait_ge(h2_ready, k - 1)
                ts(tmp_u[k % 2][:], bank[k % 8][:], gsc_m[:, k:k + 1], shf_m[:, k:k + 1], ALU.mult, ALU.add).then_inc(h2_tmp, 1)
                if k:
                    dve.wait_ge(h2_hi_done, k)
                    tt(h2_lo[:, k - 1, :], tmp_u[(k - 1) % 2][:], h2_hi[:, k - 1, :].bitcast(F32), ALU.subtract).then_inc(h2_ready, 1)
            dve.wait_ge(h2_hi_done, KD)
            tt(h2_lo[:, KD - 1, :], tmp_u[(KD - 1) % 2][:], h2_hi[:, KD - 1, :].bitcast(F32), ALU.subtract).then_inc(h2_ready, 1)

            dve.sem_inc(mlp_free, 4)

            def squares(g, f):
                n0 = 4 * f
                for c in range(4):
                    dve.wait_ge(relu_done, g * FCH + (n0 + c + 1))
                    stt(tmp_y[c % 2][:], sets[f][c][:], 0.0, tmp_u[c % 2][:], ALU.max, ALU.mult).then_inc(y_done, 1)
                    dve.wait_ge(y_hi_done, g * FCH + (n0 + c + 1))
                    tt(y_lo[:, n0 + c, :], tmp_y[c % 2][:], y_hi[:, n0 + c, :].bitcast(F32), ALU.subtract).then_inc(y_ready, 1)
                    dve.wait_ge(y_ready, g * FCH + (n0 + c + 1))
                dve.sem_inc(mlp_free, 4)

            def down_add(n, first):
                for t in range(NT):
                    dst = y_acc[:, t, n * COLS:(n + 1) * COLS]
                    src = sets[n % 2][t][:]
                    ins = nc.vector.tensor_copy(dst, src) if first else tt(dst, src, dst, ALU.add)
                    ins.then_inc(mlp_free, 1)

            def mlp_group(g, first, before_first):
                for j in range(4 if first else 0, MLP_N):
                    r, w = at_mlp(g, j)
                    split_lo(r, w)
                    if j == 3:
                        dve.wait_ge(w_used, w.count(1, 1 - 4))
                        down_add(NB - 1, before_first)
                    if j == UNITS_D + 3:
                        squares(g, 0)
                    if j == UP_UNITS + 3:
                        squares(g, 1)
                    if j > UP_UNITS + 3 and (j - UP_UNITS) % DN_U == DN_U - 1:
                        dve.wait_ge(w_used, w.count(1, 1 - 4))
                        down_add((j - UP_UNITS) // DN_U - 1, first)

            mlp_group(0, True, False)
            mlp_group(1, False, True)
            with dve.Fori(2, GROUPS) as g:
                mlp_group(g, False, False)
            dve.wait_ge(w_used, MLP_W + MLP_N * GROUPS)
            down_add(NB - 1, False)

            dve.wait_ge(y_sq, NT)
            ts(stat_v[:, :, 2:3], stat[:, :, 2:3], 1.0 / D, EPS, ALU.mult, ALU.add).then_inc(y_var, 1)
            dve.wait_ge(y_sqrt, 1)
            own.step(nc.vector.reciprocal(rstd[:, :, 2:3], stat_s[:, :, 2:3]))
            dve.wait_ge(comb_m_ready, 1)
            dve.wait_ge(x1_landed, 16 * NT)
            for t in range(NT):
                own.step(stt(y_acc[:, t, :], y_acc[:, t, :], rstd[:, t, 2:3], gm_acc[:], ALU.mult, ALU.mult))
                tt(x1_back[:, t, :], y_acc[:, t, :], x1_back[:, t, :], ALU.add).then_inc(out_ready, 1)

        @block.tensor
        def _(pe):
            mm = nc.tensor.matmul

            def unit_tokens(w, acc, act_hi, act_lo, k0, first, last):
                s = w.slot()
                for t in range(NT):
                    for q in range(QROWS):
                        k = k0 + q
                        xh, xl = act_hi[:, k, t * P:(t + 1) * P], act_lo[:, k, t * P:(t + 1) * P]
                        mm(acc[t][:], xh, hi[s][:, q, :], start=first and q == 0, stop=False)
                        mm(acc[t][:], xh, lo[s][:, q, :], start=False, stop=False)
                        ins = mm(acc[t][:], xl, hi[s][:, q, :], start=False, stop=last and q == QROWS - 1)
                ins.then_inc(w_used, 1)

            def unit_columns(w, acc, act_hi, act_lo, k0, first, last):
                s = w.slot()
                for n in range(4):
                    for q in range(QROWS):
                        k = k0 + q
                        wh, wl = hi[s][:, q, n * P:(n + 1) * P], lo[s][:, q, n * P:(n + 1) * P]
                        mm(acc[n][:], wh, act_hi[:, k, :], start=first and q == 0, stop=False)
                        mm(acc[n][:], wh, act_lo[:, k, :], start=False, stop=False)
                        ins = mm(acc[n][:], wl, act_hi[:, k, :], start=False, stop=last and q == QROWS - 1)
                ins.then_inc(w_used, 1)

            pe.wait_ge(const_landed, 16)
            pe.wait_ge(vec_landed, 16 * 7)
            width = 3 * KD + 2 * HEADS + KR
            nc.tensor.transpose(bank[4][:, 0:width], vec_rows[0:width, 0, :], ident[0:width, 0:width]).then_inc(vec_turned, 1)
            nc.tensor.transpose(bank[5][:, 0:6 * KD], vec_rows[0:6 * KD, 1, :], ident[0:6 * KD, 0:6 * KD]).then_inc(vec_turned, 1)
            pe.wait_ge(x_normed, NT)
            for k in range(KD):
                if k >= 4:
                    pe.wait_ge(x_t_ready, k - 3)
                for t in range(NT):
                    ins = nc.tensor.transpose(bank[k % 4][:, t * P:(t + 1) * P], x_tok[:, t, k * P:(k + 1) * P], ident[:])
                ins.then_inc(x_turned, 1)
            pe.wait_ge(ones_ready, 1)
            pe.wait_ge(vec_ready, 2)
            def start_products(cb):
                r, w = start_w(cb), START_W * cb
                for j in range(2):
                    pe.wait_ge(h_ready, 4 * cb + 2 * j + 2)
                    pe.wait_ge(raw_used, r + j + 1)
                    unit_tokens(At(w + j), sets[0], h_hi, h_lo, 4 * cb + 2 * j, cb == 0 and j == 0, cb == NB - 1 and j == 1)
                pe.wait_ge(raw_used, r + 3)
                s = At(w + 2).slot()
                for k in range(4):
                    wh, wl = (x[s][:].rearrange("p q n -> p (q n)")[:, k * P:(k + 1) * P] for x in (hi, lo))
                    xh, xl = h_hi[:, 4 * cb + k, :], h_lo[:, 4 * cb + k, :]
                    mm(bank[4][:], wh, xh, start=cb == 0 and k == 0, stop=False)
                    mm(bank[4][:], wh, xl, start=False, stop=False)
                    ins = mm(bank[4][:], wl, xh, start=False, stop=cb == NB - 1 and k == 3)
                ins.then_inc(w_used, 1)

            for cb in range(NB):
                if cb:
                    start_products(cb - 1)
                pe.wait_ge(mod_summed, 2 * cb + 2)
                if cb:
                    pe.wait_ge(mod_read, cb)
                for g in range(2):
                    for j in range(4):
                        for q in range(2):
                            ins = mm(bank[5][:, 4 * g + j:4 * g + j + 1], start_acc[2 * (cb % 2) + g][:, q, j * P:(j + 1) * P],
                                     ones[:, 0:1], start=q == 0, stop=q == 1)
                ins.then_inc(mod_reduced, 1)
            pe.wait_ge(x_t_ready, KD)
            start_products(NB - 1)

            def turn(b):
                if b == 0:
                    pe.wait_ge(copied, 4)
                    pe.wait_ge(kr_sum, 1)
                else:
                    pe.wait_ge(tok_ready, 4 * b)
                for n in range(TURNS[b]):
                    for t in range(NT):
                        ins = nc.tensor.transpose(sets[b % 2][n][:, t * P:(t + 1) * P], tok[:, t, n * P:(n + 1) * P], ident[:])
                    ins.then_inc(turned, 1)

            for b in range(1, PROJ_BLOCKS + 1):
                for j in range(UNITS_D):
                    r, w = PROJ_RAW + 2 * UNITS_D * (b - 1) + 2 * j, PROJ_W + UNITS_D * (b - 1) + j
                    pe.wait_ge(raw_used, r + 1)
                    if j == 0:
                        if b == 1:
                            pe.wait_ge(kr_copied, 1)
                            pe.wait_ge(mod_read, NB)
                        else:
                            pe.wait_ge(turned_out, TURNS_SUM[b - 1])
                            pe.wait_ge(copied, 4 * (b - 1))
                            if b >= 3:
                                pe.wait_ge(mod_read, NB + b - 2) if b >= 4 else None
                    unit = unit_tokens if TOKENS_OUT[b] else unit_columns
                    unit(At(w), sets[b % 2], h_hi, h_lo, QROWS * j, j == 0, j == UNITS_D - 1)
                    if j == 4 and b == 1:
                        pe.wait_ge(tab_landed, 16 * 6)
                        pe.wait_ge(c_sq, 4)
                        pe.wait_ge(copied, 4)
                        mm(bank[0][:], rot[:], tmp[0][:], start=True, stop=True).then_inc(kr_turned, 1)
                    if j == 4 and b >= 2:
                        pe.wait_ge(mod_summed, 2 * NB + b - 1)
                        pe.wait_ge(copied, 4 * b)
                        for n in range(4):
                            ins = mm(sets[(b - 1) % 2][0][:, n:n + 1], mod_acc[(b - 2) % 2][:, n * P:(n + 1) * P], ones[:, 0:1], start=True, stop=True)
                        ins.then_inc(mod_reduced, 1)
                    if j == 6 and b <= 5:
                        if b >= 2:
                            pe.wait_ge(mod_read, NB + b - 1)
                        turn(b - 1)

            for i, b in enumerate((7, 8, 9, 10)):
                pe.wait_ge(copied, 4 * (b - 1))
                if b == 7:
                    pe.wait_ge(mod_read, NB + 5)
                    pe.wait_ge(c_ready, KR)
                for j in range(2):
                    pe.wait_ge(raw_used, KV_RAW + 3 * (2 * i + j) + 1)
                    unit = unit_columns if b < 9 else unit_tokens
                    unit(At(KV_W + 2 * i + j), sets[b % 2], c_hi, c_lo, 2 * j, j == 0, j == 1)
            pe.wait_ge(mod_summed, 2 * NB + 8)
            pe.wait_ge(copied, 4 * 10)
            for g, acc in ((5, 1), (6, 0), (7, 2)):
                for n in range(4):
                    c = 4 * (g - 5) + n
                    ins = mm(bank[7][:, c:c + 1], mod_acc[acc][:, n * P:(n + 1) * P], ones[:, 0:1], start=True, stop=True)
                ins.then_inc(mod_reduced, 1)
            pe.wait_ge(copied, 4 * 11)
            pe.wait_ge(kr_ready, 1)

            def scores(grp, h, H, t):
                if t == 0:
                    pe.wait_ge(qk_ready, H + 1)
                (qh, ql), (kh, kl) = stage["q"], stage["k"]
                cut = lambda x: x[:, t * P:(t + 1) * P]
                mm(bank[t][:], cut(qh), kh[:], start=True, stop=False)
                mm(bank[t][:], cut(qh), kl[:], start=False, stop=False)
                ins = mm(bank[t][:], cut(ql), kh[:], start=False, stop=not grp)
                if grp:
                    rh, rl = stage["qr"]
                    par = bass.ds(h & 1, 1) if not isinstance(h, int) else slice(h & 1, (h & 1) + 1)
                    krh, krl = (x[:, par, :].rearrange("p a n -> p (a n)") for x in (kr_hi, kr_lo))
                    mm(bank[t][:], cut(rh), krh, start=False, stop=False)
                    mm(bank[t][:], cut(rh), krl, start=False, stop=False)
                    ins = mm(bank[t][:], cut(rl), krh, start=False, stop=True)
                ins.then_inc(s_done, 1)

            def turn_probs(t, H):
                pe.wait_ge(p_ready, H * 4 + (t + 1))
                pe.wait_ge(pt_done, H * 4 + (t + 1))
                for c in range(NT):
                    ins = nc.tensor.transpose(bank[4 + t % 2][:, c * P:(c + 1) * P], prob[:, t, c * P:(c + 1) * P], ident[:])
                ins.then_inc(p_turned, 1)

            def attend(H, nxt):
                turn_probs(0, H)
                for t in range(1, NT):
                    turn_probs(t, H)
                    if nxt:
                        scores(*nxt, t - 1)
                if nxt:
                    scores(*nxt, NT - 1)
                pe.wait_ge(pt_done, H * 4 + 6)
                pe.wait_ge(v_ready, H + 1)
                pe.wait_ge(o_done, H)
                (vh, vl) = stage["v"]
                for c in range(NT):
                    v = slice(c * P, (c + 1) * P)
                    mm(bank[6][:], vh[:, v], pt_hi[:, c, :], start=c == 0, stop=False)
                    mm(bank[6][:], vh[:, v], pt_lo[:, c, :], start=False, stop=False)
                    ins = mm(bank[6][:], vl[:, v], pt_hi[:, c, :], start=False, stop=c == NT - 1)
                ins.then_inc(pv_done, 1)

            for t in range(NT):
                scores(0, 0, 0, t)
            with pe.Fori(0, HEADS - 1) as h:
                attend(h, (0, h + 1, h + 1))
            attend(HEADS - 1, (1, 0, HEADS))
            with pe.Fori(0, HEADS - 1) as h:
                attend(h + HEADS, (1, h + 1, h + (HEADS + 1)))
            attend(2 * HEADS - 1, None)

            pe.wait_ge(sq_ready, 2 * HEADS)
            pe.wait_ge(mod_read, NB + 6)
            for g in range(2):
                for t in range(NT):
                    c = 16 + 4 * g + t
                    ins = mm(bank[7][:, c:c + 1], sq_sum[:, g, t * P:(t + 1) * P], ones[:, 0:1], start=True, stop=True)
            ins.then_inc(sq_reduced, 1)
            with pe.Fori(0, NB) as n:
                for j in range(UNITS_D):
                    r, w = at_out(n, j)
                    pe.wait_ge(raw_used, r.count(1, 1))
                    pe.wait_ge(o_ready, 2 * j + 2)
                    if j == 0:
                        pe.wait_ge(comb_ready, n)
                    if j == 4:
                        pe.wait_ge(z_done, n * 4)
                        pe.wait_ge(r_ready, 1)
                    unit_tokens(w, sets[j // 4], o_hi, o_lo, QROWS * j, j % 4 == 0, j % 4 == 3)
                    if j == 6:
                        pe.wait_ge(a_out, n * 4 + 4)
                        pe.wait_ge(ga_summed, n + 1)
                        src = ga_acc[:, bass.ds(n & 1, 1), :].rearrange("p a n -> p (a n)")
                        mm(bank[0][:], ones[:], src, start=True, stop=True).then_inc(ga_reduced, 1)
            pe.wait_ge(z_done, 4 * NB)
            for n in range(NB):
                ins = mm(bank[4 + n][:], ones[:], gm_acc[:, n * COLS:(n + 1) * COLS], start=True, stop=True)
            ins.then_inc(gm_reduced, 1)
            pe.wait_ge(comb_ready, NB)
            pe.wait_ge(gm_copied, NB)
            for t in range(NT):
                pe.wait_ge(xn_ready, t + 1)
                for k in range(8):
                    ins = nc.tensor.transpose(bank[k][:, t * P:(t + 1) * P], z_tok[:, t, k * P:(k + 1) * P], ident[:])
                    if t == NT - 1:
                        ins.then_inc(xn_turned, 1)
            for k in range(8, KD):
                pe.wait_ge(h2_tmp, k - 7)
                for t in range(NT):
                    ins = nc.tensor.transpose(bank[k % 8][:, t * P:(t + 1) * P], z_tok[:, t, k * P:(k + 1) * P], ident[:])
                ins.then_inc(xn_turned, 1)
            pe.wait_ge(h2_tmp, 12)

            with pe.Fori(0, GROUPS) as g:
                for f in range(2):
                    for j in range(UNITS_D):
                        r, w = at_mlp(g, f * UNITS_D + j)
                        pe.wait_ge(raw_used, r.count(1, 1))
                        if f == 0:
                            pe.wait_ge(h2_ready, 2 * j + 2)
                        if j == 0:
                            pe.wait_ge(mlp_free, g * 24 + 4 * f)
                        unit_columns(w, sets[f], h2_hi, h2_lo, QROWS * j, j == 0, j == UNITS_D - 1)
                for n in range(NB):
                    for j in range(DN_U):
                        r, w = at_mlp(g, UP_UNITS + n * DN_U + j)
                        pe.wait_ge(raw_used, r.count(1, 1))
                        if n == 0:
                            pe.wait_ge(y_ready, g * FCH + 2 * j + 2)
                        if j == 0:
                            pe.wait_ge(mlp_free, g * 24 + 4 * (n + 2))
                        unit_tokens(w, sets[n % 2], y_hi, y_lo, QROWS * j, j == 0, j == DN_U - 1)

        @block.gpsimd
        def _(pool):
            own = Chain(pool, pool_own)
            tt = nc.gpsimd.tensor_tensor
            nc.gpsimd.memset(ones[:], 1.0).then_inc(ones_ready, 1)
            pool.wait_ge(ones_ready, 1)
            own.step(nc.gpsimd.memset(kr_hi[64:128, 0, :].bitcast(F32), 0.0))
            own.step(nc.gpsimd.memset(kr_hi[0:64, 1, :].bitcast(F32), 0.0))
            own.step(nc.gpsimd.memset(kr_lo[64:128, 0, :].bitcast(F32), 0.0))
            own.step(nc.gpsimd.memset(kr_lo[0:64, 1, :].bitcast(F32), 0.0))

            def normalise(H):
                for t in range(NT):
                    pool.wait_ge(rt_ready, H * 4 + (t + 1))
                    tt(prob[:, t, :], prob[:, t, :], rtotal[:, t:t + 1].broadcast_to([P, T]), ALU.mult).then_inc(p_ready, 1)

            def add_squares(H, grp):
                pool.wait_ge(o_done, H + 1)
                pool.wait_ge(sq_ready, H)
                tt(sq_sum[:, grp, :], sq_sum[:, grp, :], sq[:], ALU.add).then_inc(sq_ready, 1)

            pool.wait_ge(c_ready, KR)
            own.step(nc.gpsimd.memset(sq_sum[:], 0.0))
            normalise(0)
            normalise(1)
            with pool.Fori(1, HEADS + 1) as h:
                normalise(h + 1)
                add_squares(h - 1, 0)
            with pool.Fori(HEADS + 1, 2 * HEADS - 1) as h:
                normalise(h + 1)
                add_squares(h - 1, 1)
            add_squares(2 * HEADS - 2, 1)
            add_squares(2 * HEADS - 1, 1)
            pool.wait_ge(sq_reduced, 1)
            for t in range(NT):
                pool.dma_start(x_res[:, t, :], x_d[t]).then_inc(res_landed, 16)
            for n in range(NB):
                if n:
                    pool.wait_ge(comb_ready, n)
                pool.dma_start(rows[:, 0, :], b_rows[:, GT_A + n * COLS:GT_A + (n + 1) * COLS].partition_broadcast(P)[:, 0, :]).then_inc(rows_landed, 16)
                pool.dma_start(rows[:, 1, :], a["g_post_attn"][:, n * COLS:(n + 1) * COLS].partition_broadcast(P)[:, 0, :]).then_inc(rows_landed, 16)
            for n in range(NB):
                if n == 0:
                    pool.wait_ge(comb_ready, NB)
                pool.dma_start(rows[:, 0, :], b_rows[:, GT_M + n * COLS:GT_M + (n + 1) * COLS].partition_broadcast(P)[:, 0, :]).then_inc(rows_landed, 16)
                pool.dma_start(rows[:, 1, :], a["g_post_mlp"][:, n * COLS:(n + 1) * COLS].partition_broadcast(P)[:, 0, :]).then_inc(rows_landed, 16)
                pool.wait_ge(rows_landed, 32 * (NB + n + 1))
                pool.wait_ge(gm_copied, NB)
                dst = gm_acc[:, n * COLS:(n + 1) * COLS]
                own.step(tt(dst, dst, rows[:, 0, :], ALU.add))
                own.step(tt(dst, dst, rows[:, 1, :], ALU.mult))
            pool.sem_inc(comb_m_ready, 1)


def kernel(**inputs):
    import concourse.bacc as bacc
    from concourse.bass_utils import run_bass_kernel_spmd

    nc = bacc.Bacc("TRN2", target_bir_lowering=False, num_devices=1)
    arrays = {name: np.ascontiguousarray(v) for name, v in inputs.items()}
    arrays.update(tables())
    aps = {name: nc.dram_tensor("in_" + name, v.shape, F32, kind="ExternalInput").ap() for name, v in arrays.items()}
    out = nc.dram_tensor("out", (1, T, D), F32, kind="ExternalOutput").ap()
    x1_dram = nc.dram_tensor("x1_dram", (T, D), F32, kind="Internal").ap()
    build(nc, aps, out, x1_dram)
    r = run_bass_kernel_spmd(nc, [{"in_" + name: v for name, v in arrays.items()}], core_ids=[0])
    return r.results[0]["out"]


def tables():
    f = np.float32
    row, col = (np.arange(T) // 64).astype(f), (np.arange(T) % 64).astype(f)

    def angles(dim):
        half = dim // 2
        inv = np.power(f(10000.0), -np.arange(0, half, 2, dtype=f) / f(half)).astype(f)
        r, c = row[:, None] * inv[None], col[:, None] * inv[None]
        ang = np.concatenate([r, r, c, c], axis=-1).astype(f)
        sign = np.tile(np.repeat(np.array([-1, 1], f), dim // 4), 2)
        return np.stack([np.cos(ang), np.sin(ang) * sign]).astype(f)

    rot = np.zeros((P, P), f)
    for i in range(P):
        rot[i ^ (ROPE_B // 4), i] = 1.0
    tok_major = lambda t: np.ascontiguousarray(t.reshape(2, NT, P, -1).transpose(2, 0, 1, 3))
    b = angles(ROPE_B)
    tab_t = np.concatenate([b.transpose(2, 0, 1)] * 2, axis=0)
    return {"ident": np.eye(P, dtype=f), "rot": rot, "tab_a": tok_major(angles(P)), "tab_b": tok_major(b),
            "tab_t": np.ascontiguousarray(tab_t)}
```

```python
import math
from contextlib import ExitStack

import numpy as np

import concourse.bass as bass
from concourse import mybir

F32, F32R = mybir.dt.float32, mybir.dt.float32r
ACT, ALU, AX = mybir.ActivationFunctionType, mybir.AluOpType, mybir.AxisListType

P = 128
T = 512
NT = T // P
D = 2048
KD = D // P
COLS = 512
NB = D // COLS
QROWS = 2
RING = 4
HEADS = 8
RANK = 512
KR = RANK // P
ROPE_B = 64
D_FF = 4 * D
GROUPS = 8
FCH = D_FF // GROUPS // P
EPS = 1e-6
SCALE_A = 1.0 / math.sqrt(128)
SCALE_B = 1.0 / math.sqrt(128 + ROPE_B)
SH_A, SC_A, GT_A, SH_M, SC_M, GT_M = [i * D for i in range(6)]

UNITS_D = KD // QROWS
TURN_BANK = (4, 5, 7, 4)
START_RAW, START_W = 2 * UNITS_D + 3, 3


START_W_AFTER = {1: 0, 3: 1, 5: 2}


def start_mod(cb, g, j):
    late = sum(u < j for u in START_W_AFTER) if g and cb else 0
    return START_RAW * cb - (3 if cb else 0) + UNITS_D * g + j + late


def start_w(cb, j):
    if cb == NB - 1:
        return START_RAW * NB - 3 + j
    after = [u for u, w in START_W_AFTER.items() if w == j][0]
    return start_mod(cb + 1, 1, after) + 1


PROJ_RAW = NB * START_RAW
PROJ_W = NB * START_W
PROJ_BLOCKS = 6
KV_RAW = PROJ_RAW + PROJ_BLOCKS * 2 * UNITS_D
KV_W = PROJ_W + PROJ_BLOCKS * UNITS_D
KV_UNITS = 8
OUT_RAW = KV_RAW + 3 * KV_UNITS
OUT_W = KV_W + KV_UNITS
OUT_RAW_N, OUT_W_N = 3 * UNITS_D, UNITS_D
MLP_RAW = OUT_RAW + NB * OUT_RAW_N
MLP_W = OUT_W + NB * OUT_W_N
UP_UNITS, DOWN_UNITS = 2 * UNITS_D, NB * FCH // QROWS
MLP_N = UP_UNITS + DOWN_UNITS
DN_U = FCH // QROWS
FIRST_AFTER = {3: [1], 7: [2, 3], 11: [4], 13: [5]}
FIRST_SPLIT = 6
LAST_ADDS = 24 * GROUPS - 12


class At:

    def __init__(self, const, i=None, per=0):
        assert per % RING == 0
        self.const, self.i, self.per = const, i, per

    def slot(self):
        return self.const % RING

    def count(self, times=1, more=0, each=1):
        fixed = times * (self.const // each) + more
        return fixed if self.i is None else self.i * (times * self.per // each) + fixed

    def plus(self, n):
        return At(self.const + n, self.i, self.per)


class Chain:

    def __init__(self, engine, sem):
        self.engine, self.sem, self.n, self.loop = engine, sem, 0, 0

    def step(self, instruction):
        instruction.then_inc(self.sem, 1)
        self.n += 1
        self.engine.wait_ge(self.sem, self.loop + self.n)

    def enter(self, i, per):
        self.loop, self.at, self.per = i * per, self.n, per

    def leave(self, times):
        assert self.n - self.at == self.per, (self.n - self.at, self.per)
        self.loop, self.n = 0, self.at + times * self.per


def build(nc, a, out, x1_dram):
    with ExitStack() as ctx:
        sem = lambda name: ctx.enter_context(nc.semaphore(name))
        base, KB = 16512, 1024
        room = ctx.enter_context(nc.sbuf_tensor("room", [P, 53000], F32))

        def sb(name, kb, shape, dtype=F32):
            size = int(np.prod(shape)) * 4
            assert int(kb * KB) + size <= 53000 * 4, name
            return nc.alloc_sbuf_tensor_at(name, [P] + list(shape), dtype, offset=base + int(kb * KB))

        place = [0.0]

        def small(name, shape):
            t = sb(name, place[0], shape)
            place[0] += math.ceil(int(np.prod(shape)) * 4 / 32) * 32 / KB
            assert place[0] <= 4
            return t

        ident = small("ident", [P])
        rot = small("rot", [P])
        ones = small("ones", [P])
        gains = small("gains", [KD * 3 + 2 * HEADS + KR])
        bias = small("bias", [6 * KD])
        g_q, g_k = sb("g_q", 206, [P]), sb("g_k", 206.5, [P])
        silu_c = small("silu_c", [KD])
        silu_t = small("silu_t", [KD])
        gsc_a = small("gsc_a", [2, 4])
        shf_a = small("shf_a", [2, 4])
        mod_m = small("mod_m", [2 * KD])
        gsc_m = small("gsc_m", [KD])
        shf_m = small("shf_m", [KD])
        stat = small("stat", [NT, 4])
        stat_v = small("stat_v", [NT, 4])
        stat_s = small("stat_s", [NT, 4])
        rstd = small("rstd", [NT, 4])
        top = small("top", [NT])
        nbias = small("nbias", [NT])
        total = small("total", [NT])
        rtotal = small("rtotal", [NT])
        r_out = small("r_out", [2, NT])
        row_sq = small("row_sq", [NT, NB])
        raw = [sb(f"raw{i}", 4 + 4 * i, [QROWS, COLS]) for i in range(RING)]
        hi = [sb(f"hi{i}", 20 + 4 * i, [QROWS, COLS], F32R) for i in range(RING)]
        lo = [sb(f"lo{i}", 36 + 4 * i, [QROWS, COLS], F32R) for i in range(RING)]
        x_tok = sb("x_tok", 52, [NT, D])
        h_hi, h_lo = sb("h_hi", 52, [KD, T], F32R), sb("h_lo", 84, [KD, T], F32R)
        prob = sb("prob", 52, [NT, T])
        kg_hi, kg_lo = sb("kg_hi", 60, [2, T], F32R), sb("kg_lo", 64, [2, T], F32R)
        vg1 = (sb("vg1_hi", 156, [T], F32R), sb("vg1_lo", 158, [T], F32R))
        k_nope = sb("k_nope", 68, [HEADS, T])
        v_lat = sb("v_lat", 84, [NT, HEADS, P])
        stage = {}
        for n, name in enumerate(("q", "k", "v", "qr")):
            stage[name] = (sb(f"{name}_hi", 100 + 4 * n, [T], F32R), sb(f"{name}_lo", 102 + 4 * n, [T], F32R))
        o_hi, o_lo = sb("o_hi", 52, [KD, T], F32R), sb("o_lo", 84, [KD, T], F32R)
        h2_hi, h2_lo = sb("h2_hi", 52, [KD, T], F32R), sb("h2_lo", 84, [KD, T], F32R)
        x1_back = sb("x1_back", 52, [NT, D])
        z_out = sb("z_out", 84, [NT, D])
        x_t = sb("x_t", 116, [KD, T])
        q_o = sb("q_o", 116, [2 * HEADS, T])
        z_tok = sb("z_tok", 116, [NT, D])
        y_acc = sb("y_acc", 116, [NT, D])
        q_rot = sb("q_rot", 148, [HEADS // 2, T])
        k_gqa = sb("k_gqa", 156, [2, T])
        v_gqa = sb("v_gqa", 160, [NT, 2, P])
        kr_hi, kr_lo = sb("kr_hi", 164, [2, T], F32R), sb("kr_lo", 168, [2, T], F32R)
        ckv = sb("ckv", 172, [KR, T])
        sq = sb("sq", 172, [T])
        sq_sum = sb("sq_sum", 174, [2, T])
        x_res = sb("x_res", 148, [NT, D])
        y_hi, y_lo = sb("y_hi", 148, [FCH, T], F32R), sb("y_lo", 164, [FCH, T], F32R)
        start_acc = [sb(f"start_acc{i}", 148 + 4 * i, [2, COLS]) for i in range(4)]
        mod_acc = [sb(f"mod_acc{i}", 180 + 2 * i, [COLS]) for i in range(3)]
        tab_b = sb("tab_b", 184, [2, NT, ROPE_B])
        tab_a = sb("tab_a", 186, [2, NT, P])
        tab_g = sb("tab_g", 190, [2, NT, P])
        tab_t = sb("tab_t", 190, [2, T])
        tok = sb("tok", 194, [NT, COLS])
        vec_rows = sb("vec_rows", 194, [2, P])
        h_f32 = [sb(f"h_f32_{i}", 194 + 2 * i, [T]) for i in range(4)]
        tmp = [sb(f"tmp{i}", 202 + 2 * i, [COLS]) for i in range(2)]
        c_hi, c_lo = sb("c_hi", 186, [KR, T], F32R), sb("c_lo", 194, [KR, T], F32R)
        pt_hi, pt_lo = sb("pt_hi", 186, [NT, T], F32R), sb("pt_lo", 194, [NT, T], F32R)
        ga_acc = sb("ga_acc", 202, [2, COLS])
        gm_acc = sb("gm_acc", 180, [D])
        part = sb("part", 188, [NT, COLS])
        comb = sb("comb", 196, [COLS])
        rows = sb("rows", 198, [2, COLS])
        sq_junk = sb("sq_junk", 196, [COLS])
        diag = sb("diag", 202, [NT, P])
        tmp_u = [sb(f"tmp_u{i}", 188 + 2 * i, [T]) for i in range(2)]
        h2_f32 = [sb(f"h2_f32_{i}", 188 + 2 * i, [T]) for i in range(4)]
        tmp_y = [sb(f"tmp_y{i}", 192 + 2 * i, [T]) for i in range(2)]

        bank = [ctx.enter_context(nc.psum_tensor(f"bank{i}", [P, COLS], F32)) for i in range(8)]
        sets = (bank[0:4], bank[4:8])

        w_ada = a["w_ada"].rearrange("l (u q p) n -> (l u) p q n", q=QROWS, p=P)
        w_in = a["w_in"].rearrange("l (u q p) n -> (l u) p q n", q=QROWS, p=P)
        w_in4 = a["w_in"].rearrange("l (u q p) n -> (l u) p q n", q=4, p=P)
        w_kv = a["w_kv_b"].rearrange("l (u q p) (h e) -> (l u) p q h e", q=QROWS, p=P, h=HEADS)
        w_out = a["w_out"].rearrange("l (u q p) n -> (l u) p q n", q=QROWS, p=P)
        w_up = a["w_mlp_in"].rearrange("l (u q p) n -> (l u) p q n", q=QROWS, p=P)
        w_dn = a["w_mlp_out"].rearrange("l (u q p) n -> (l u) p q n", q=QROWS, p=P)
        x_d = a["x"].rearrange("b (t p) d -> (b t) p d", p=P)
        out_d = out.rearrange("b (t p) d -> (b t) p d", p=P)
        x1_d = x1_dram.rearrange("(t p) d -> t p d", p=P)
        b_rows = a["b_ada"]

        def sems(names):
            return [sem(n) for n in names.split()]

        raw_landed = [sem(f"raw_landed{i}") for i in range(RING)]
        raw_used, hi_ready, w_used = sems("raw_used hi_ready w_used")
        dve_own, pool_own, pair_own = sems("dve_own pool_own pair_own")
        x_landed = [sem(f"x_landed{i}") for i in range(NT)]
        vec_landed, const_landed, tab_landed, ones_ready = sems("vec_landed const_landed tab_landed ones_ready")
        vec_turned, vec_ready, exp_c = sems("vec_turned vec_ready exp_c")
        x_sq, x_var, x_sqrt, x_normed, x_turned, x_t_ready = sems("x_sq x_var x_sqrt x_normed x_turned x_t_ready")
        mod_summed, mod_reduced, mod_read = sems("mod_summed mod_reduced mod_read")
        cols_ready, h_hi_ready, h_ready = sems("cols_ready h_hi_ready h_ready")
        copied, c_sq, var_ready, sqrt_ready, rstd_ready = sems("copied c_sq var_ready sqrt_ready rstd_ready")
        tok_ready, turned, turned_out = sems("tok_ready turned turned_out")
        kr_copied, kr_turned, kr_sum, kr_hi_done, kr_ready = sems("kr_copied kr_turned kr_sum kr_hi_done kr_ready")
        c_hi_done, c_ready, kg_hi_done, kg_ready = sems("c_hi_done c_ready kg_hi_done kg_ready")
        q_hi_done, k_hi_done, qk_ready, v_hi_done, v_ready = sems("q_hi_done k_hi_done qk_ready v_hi_done v_ready")
        s_done, nb_ready, exp_done, rt_ready, p_ready = sems("s_done nb_ready exp_done rt_ready p_ready")
        p_turned, pt_hi_done, pt_done, pv_done, o_done = sems("p_turned pt_hi_done pt_done pv_done o_done")
        sq_ready, sq_reduced, r_var, r_sqrt, r_ready = sems("sq_ready sq_reduced r_var r_sqrt r_ready")
        o_hi_done, o_ready, a_out, b_tile, b_sum, z_done, row_done = sems("o_hi_done o_ready a_out b_tile b_sum z_done row_done")
        ga_summed, ga_reduced, comb_ready, rows_landed = sems("ga_summed ga_reduced comb_ready rows_landed")
        gm_reduced, gm_copied, comb_m_ready = sems("gm_reduced gm_copied comb_m_ready")
        res_landed, x1_var, x1_sqrt, x1_ready, x1_sq = sems("res_landed x1_var x1_sqrt x1_ready x1_sq")
        xn_ready, xn_turned, x1_saved = sems("xn_ready xn_turned x1_saved")
        h2_mid, h2_hi_done, h2_ready = sems("h2_mid h2_hi_done h2_ready")
        relu_done, y_done, y_hi_done, y_ready, mlp_free, y_zero = sems("relu_done y_done y_hi_done y_ready mlp_free y_zero")
        z_ready, y_sq, y_var, y_sqrt, x1_landed, out_ready, out_saved = sems("z_ready y_sq y_var y_sqrt x1_landed out_ready out_saved")

        q_b = a["w_in"].rearrange("l (u q p) n -> (l u) p q n", q=QROWS, p=P)[:, :, :, 1536:3072].rearrange(
            "u p q (h e) -> u p q h e", h=HEADS)
        PROJ = [3072, 1024, 0, 512, "rot", "plain0", "plain1"]
        TOKENS_OUT = [True, True, True, True, True, False, False]
        TURNS = [4, 2, 4, 4, 4, 0, 0]
        STATS = {1: 1, 2: 2, 3: 4, 4: 4}
        TURNS_SUM = [int(np.sum(TURNS[:b])) for b in range(len(TURNS) + 1)]

        block = ctx.enter_context(nc.Block())

        @block.sync
        def _(sp):
            def load(at, source, n=COLS * QROWS, shape=None):
                if at.i is not None or at.const >= RING:
                    sp.wait_ge(raw_used, at.count(1, 1 - RING))
                dst = raw[at.slot()][:, :, :]
                if shape:
                    dst = dst.rearrange("p q n -> p (q n)")[:, 0:n].rearrange(*shape[0], **shape[1])
                sp.dma_start(dst, source).then_inc(raw_landed[at.slot()], 16)

            def ada(at, j, col):
                load(at, w_ada[j, :, :, bass.ds(col, COLS)])

            r = 0
            for name, n in (("c", KD), ("g_pre_attn", KD), ("g_pre_mlp", KD), ("g_out_a", HEADS), ("g_out_b", HEADS), ("g_ckv", KR)):
                sp.dma_start(vec_rows[r:r + n, 0, :], a[name].rearrange("l (k p) -> (l k) p", p=P)).then_inc(vec_landed, 16)
                r += n
            sp.dma_start(vec_rows[0:6 * KD, 1, :], a["b_ada"].rearrange("l (k p) -> (l k) p", p=P)).then_inc(vec_landed, 16)
            sp.dma_start(ident[:], a["ident"]).then_inc(const_landed, 16)

            def start_weights(cb, j):
                if j < 2:
                    load(At(start_w(cb, j)), w_in[2 * cb + j, :, :, PROJ[0]:PROJ[0] + COLS])
                else:
                    load(At(start_w(cb, j)), w_in4[cb, :, :, 3584:3584 + ROPE_B], 4 * ROPE_B, (("p (q n) -> p q n",), {"q": 4}))

            for cb in range(NB):
                for g, col in enumerate((SC_A, SH_A)):
                    for j in range(UNITS_D):
                        ada(At(start_mod(cb, g, j)), j, col + COLS * cb)
                        if g and cb and j in START_W_AFTER:
                            start_weights(cb - 1, START_W_AFTER[j])
            for j in range(3):
                start_weights(NB - 1, j)
            for b in range(1, PROJ_BLOCKS + 1):
                for j in range(UNITS_D):
                    r = PROJ_RAW + 2 * UNITS_D * (b - 1) + 2 * j
                    if PROJ[b] == "rot":
                        at = At(r)
                        sp.wait_ge(raw_used, at.count(1, 1 - RING))
                        for q in range(QROWS):
                            sp.dma_start(raw[at.slot()][:, q, :].rearrange("p (h e) -> p h e", h=HEADS),
                                         q_b[j, :, q, :, P:P + ROPE_B]).then_inc(raw_landed[at.slot()], 16)
                    elif isinstance(PROJ[b], str):
                        at = At(r)
                        sp.wait_ge(raw_used, at.count(1, 1 - RING))
                        h0 = 4 * int(PROJ[b][-1])
                        for q in range(QROWS):
                            sp.dma_start(raw[at.slot()][:, q, :].rearrange("p (h e) -> p h e", h=4),
                                         q_b[j, :, q, h0:h0 + 4, 0:P]).then_inc(raw_landed[at.slot()], 16)
                    else:
                        load(At(r), w_in[j, :, :, PROJ[b]:PROJ[b] + COLS])
                    ada(At(r + 1), j, SC_M + COLS * (b - 1) if b <= 4 else SH_M + COLS * (b - 5))
            for j in range(KV_UNITS):
                at = At(KV_RAW + 3 * j)
                sp.wait_ge(raw_used, at.count(1, 1 - RING))
                blk, u = j // 2, j % 2
                for q in range(QROWS):
                    src = w_kv[u, :, q, 4 * (blk % 2):4 * (blk % 2) + 4, P * (blk // 2):P * (blk // 2) + P]
                    sp.dma_start(raw[at.slot()][:, q, :].rearrange("p (h e) -> p h e", h=4), src).then_inc(raw_landed[at.slot()], 16)
                for m in range(2):
                    g, jj = divmod(2 * j + m, UNITS_D)
                    ada(At(KV_RAW + 3 * j + 1 + m), jj, SH_M + COLS * (2 + g))
            with sp.Fori(0, NB) as n:
                for j in range(UNITS_D):
                    at = At(OUT_RAW + 3 * j, n, OUT_RAW_N)
                    load(at, w_out[j, :, :, bass.ds(n * COLS, COLS)])
                    for m in range(2):
                        ada(at.plus(1 + m), 2 * (j % 4) + m, n * COLS + (GT_A if j < 4 else GT_M))
            with sp.Fori(0, GROUPS) as g:
                at = At(MLP_RAW, g, MLP_N)
                for f in range(2):
                    for j in range(UNITS_D):
                        load(at.plus(f * UNITS_D + j), w_up[j, :, :, bass.ds(g * (FCH * P) + f * COLS, COLS)])
                for n in range(NB):
                    for j in range(DN_U):
                        load(at.plus(UP_UNITS + n * DN_U + j), w_dn[g * DN_U + j, :, :, n * COLS:(n + 1) * COLS])
            sp.wait_ge(w_used, MLP_W + MLP_N * (GROUPS - 1) + UP_UNITS)
            sp.wait_ge(x1_saved, 16 * NT)
            for t in range(NT):
                sp.dma_start(x1_back[:, t, :], x1_d[t]).then_inc(x1_landed, 16)
            for t in range(NT):
                for half in range(2):
                    sp.wait_ge(out_ready, 2 * t + half + 1)
                    cols = slice(half * D // 2, (half + 1) * D // 2)
                    sp.dma_start(out_d[t][:, cols], x1_back[:, t, cols]).then_inc(out_saved, 16)
            sp.wait_ge(out_saved, 16 * 2 * NT)

        landings = [0] * RING
        landed_at = {}
        for r in range(OUT_RAW):
            two = (KV_RAW <= r and (r - KV_RAW) % 3 == 0) or (
                PROJ_RAW <= r < KV_RAW and (r - PROJ_RAW) % 2 == 0 and isinstance(PROJ[1 + (r - PROJ_RAW) // (2 * UNITS_D)], str))
            landings[r % RING] += 32 if two else 16
            landed_at[r] = landings[r % RING]

        def wait_raw(engine, at):
            if at.const < OUT_RAW:
                assert at.i is None
                value = landed_at[at.const]
            else:
                slot = at.slot()
                before = landings[slot]
                nth = At(at.const - OUT_RAW, at.i, at.per)
                value = nth.count(16, before + 16, RING)
            engine.wait_ge(raw_landed[at.slot()], value)

        def at_out(n, j):
            if isinstance(n, int):
                return At(OUT_RAW + OUT_RAW_N * n + 3 * j), At(OUT_W + OUT_W_N * n + j)
            return At(OUT_RAW + 3 * j, n, OUT_RAW_N), At(OUT_W + j, n, OUT_W_N)

        def at_mlp(g, j):
            if isinstance(g, int):
                return At(MLP_RAW + MLP_N * g + j), At(MLP_W + MLP_N * g + j)
            return At(MLP_RAW + j, g, MLP_N), At(MLP_W + j, g, MLP_N)

        @block.scalar
        def _(act):
            def split_hi(r, w, pairs=None):
                wait_raw(act, r)
                if w.i is not None or w.const >= RING:
                    act.wait_ge(w_used, w.count(1, 1 - RING))
                for dst, src in (pairs or [(hi[w.slot()][:], raw[r.slot()][:])]):
                    ins = nc.scalar.activation(dst, src, ACT.Copy)
                ins.then_inc(hi_ready, 1)

            def proj_at(b, j):
                return At(PROJ_RAW + 2 * UNITS_D * (b - 1) + 2 * j), At(PROJ_W + UNITS_D * (b - 1) + j)

            act.wait_ge(vec_ready, 2)
            nc.scalar.activation(silu_t[:], gains[:, 0:KD], ACT.Exp, scale=-1.0).then_inc(exp_c, 1)
            for t in range(NT):
                act.wait_ge(raw_used, 2 * t + 1)
                act.dma_start(x_tok[:, t, :], x_d[t]).then_inc(x_landed[t], 16)
            for t in range(NT):
                act.wait_ge(x_landed[t], 16)
                nc.scalar.activation(x_t[:, 4 * t:4 * t + 4, :].rearrange("p k n -> p (k n)"), x_tok[:, t, :], ACT.Square,
                                         accum_out=stat[:, t, 0:1]).then_inc(x_sq, 1)
            act.wait_ge(x_var, 1)
            nc.scalar.activation(stat_s[:, :, 0:1], stat_v[:, :, 0:1], ACT.Sqrt).then_inc(x_sqrt, 1)
            for k in range(KD):
                act.wait_ge(x_turned, k + 1)
                nc.scalar.activation(x_t[:, k, :], bank[k % 4][:], ACT.Copy).then_inc(x_t_ready, 1)
            def start_w_hi(cb, j):
                at, w = At(start_w(cb, j)), At(START_W * cb + j)
                if j < 2:
                    split_hi(at, w)
                else:
                    dup = hi[w.slot()][:].rearrange("p q n -> p (q n)")[:, 0:4 * P].rearrange("p (k m e) -> p k m e", k=4, m=2)
                    src = raw[at.slot()][:].rearrange("p q n -> p (q n)")[:, 0:4 * ROPE_B].rearrange("p (k e) -> p k e", k=4)
                    split_hi(at, w, [(dup[:, :, m, :], src) for m in range(2)])

            for cb in range(NB):
                if cb == NB - 1:
                    start_w_hi(cb, 0)
                for j in range(4):
                    k = 4 * cb + j
                    if j == 0:
                        act.wait_ge(cols_ready, cb + 1)
                    if k >= 4:
                        act.wait_ge(h_ready, k - 3)
                    g, b = gsc_a[:, cb % 2, j:j + 1], shf_a[:, cb % 2, j:j + 1]
                    nc.scalar.activation(h_f32[j][:], x_t[:, k, :], ACT.Identity, scale=g, bias=b)
                    nc.scalar.activation(h_hi[:, k, :], x_t[:, k, :], ACT.Identity, scale=g, bias=b).then_inc(h_hi_ready, 1)
                for j in range(1 if cb == NB - 1 else 0, 3):
                    start_w_hi(cb, j)
                if cb == 2:
                    act.dma_start(rot[:], a["rot"]).then_inc(tab_landed, 16)
                    act.dma_start(tab_t[:], a["tab_t"]).then_inc(tab_landed, 16)
                    act.dma_start(tab_a[:], a["tab_a"]).then_inc(tab_landed, 16)
                    act.dma_start(tab_b[:], a["tab_b"]).then_inc(tab_landed, 16)
                    act.dma_start(g_q[:], a["g_q_a"].partition_broadcast(P)[:, 0, :]).then_inc(tab_landed, 16)
                    act.dma_start(g_k[:], a["g_k_a"].partition_broadcast(P)[:, 0, :]).then_inc(tab_landed, 16)

            def copy_out(b):
                s = sets[b % 2]
                if b == 0:
                    for t in range(NT):
                        nc.scalar.activation(tok[:, t, :], s[t][:], ACT.Square, accum_out=stat[:, t, 0:1]).then_inc(c_sq, 1)
                elif b == 1:
                    for t in range(NT):
                        nc.scalar.activation(tok[:, t, 0:2 * P], s[t][:, 0:2 * P], ACT.Copy)
                        nc.scalar.activation(v_gqa[:, t, :, :].rearrange("p g e -> p (g e)"), s[t][:, 2 * P:4 * P], ACT.Copy).then_inc(copied, 1)
                elif b <= 4:
                    for t in range(NT):
                        nc.scalar.activation(tok[:, t, :], s[t][:], ACT.Copy).then_inc(copied, 1)
                elif b <= 6:
                    for n in range(4):
                        nc.scalar.activation(q_o[:, HEADS + 4 * (b - 5) + n, :], s[n][:], ACT.Copy).then_inc(copied, 1)
                elif b <= 8:
                    for n in range(4):
                        nc.scalar.activation(k_nope[:, 4 * (b - 7) + n, :], s[n][:], ACT.Copy).then_inc(copied, 1)
                else:
                    for t in range(NT):
                        dst = v_lat[:, t, 4 * (b - 9):4 * (b - 9) + 4, :].rearrange("p h e -> p (h e)")
                        nc.scalar.activation(dst, s[t][:], ACT.Copy).then_inc(copied, 1)

            def turned_copy(b):
                for n in range(TURNS[b]):
                    act.wait_ge(turned, TURNS_SUM[b] + n + 1)
                    src = sets[b % 2][n][:]
                    if b == 0:
                        k = 3 * KD + 2 * HEADS + n
                        nc.scalar.activation(ckv[:, n, :], src, ACT.Copy, scale=gains[:, k:k + 1]).then_inc(turned_out, 1)
                    elif b == 1:
                        nc.scalar.activation(k_gqa[:, n, :], src, ACT.Copy).then_inc(turned_out, 1)
                    elif b <= 3:
                        nc.scalar.activation(q_o[:, 4 * (b - 2) + n, :], src, ACT.Copy).then_inc(turned_out, 1)
                    else:
                        nc.scalar.activation(q_rot[:, n, :], src, ACT.Copy).then_inc(turned_out, 1)

            roots = 0
            for b in range(1, PROJ_BLOCKS + 1):
                for j in range(UNITS_D):
                    split_hi(*proj_at(b, j))
                    if b == 1 and j == 0:
                        act.wait_ge(w_used, PROJ_W)
                        nc.scalar.activation(tmp[0][:], bank[4][:], ACT.Copy).then_inc(kr_copied, 1)
                    if j == 2 and b >= 2:
                        turned_copy(b - 2)
                    if j == 3:
                        if b >= 2:
                            act.wait_ge(w_used, PROJ_W + UNITS_D * (b - 1))
                            if b <= 5:
                                act.wait_ge(turned, TURNS_SUM[b - 1])
                        copy_out(b - 1)
                    if j == 4 and b in (1, 2, 3, 4):
                        roots += 1
                        act.wait_ge(var_ready, roots)
                        n = STATS[b]
                        nc.scalar.activation(stat_s[:, :, 0:n], stat_v[:, :, 0:n], ACT.Sqrt).then_inc(sqrt_ready, 1)
                    if j == 5 and b == 1:
                        act.wait_ge(rstd_ready, 1)
                        for t in range(NT):
                            nc.scalar.activation(tok[:, t, :], sets[0][t][:], ACT.Copy, scale=rstd[:, t, 0:1]).then_inc(copied, 1)
                    if j == 7 and b == 1:
                        act.wait_ge(kr_sum, 1)
                        nc.scalar.activation(kr_hi[0:64, 0, :], tmp[0][0:64, :], ACT.Copy)
                        nc.scalar.activation(kr_hi[64:128, 1, :], tmp[0][64:128, :], ACT.Copy).then_inc(kr_hi_done, 1)
                    if j == 5 and b == 6:
                        act.wait_ge(turned_out, TURNS_SUM[1])
                        act.wait_ge(tok_ready, 4 * 4)
                        act.wait_ge(turned, TURNS_SUM[5])
                        for k in range(KR):
                            nc.scalar.activation(c_hi[:, k, :], ckv[:, k, :], ACT.Copy).then_inc(c_hi_done, 1)
            flat = lambda x: x.rearrange("p a n -> p (a n)")

            def stage_q(grp, h, H):
                if not (isinstance(H, int) and H == 0):
                    act.wait_ge(s_done, H * 4)
                nc.scalar.activation(stage["q"][0][:], flat(q_o[:, bass.ds(h + grp * HEADS, 1), :]), ACT.Copy).then_inc(q_hi_done, 1)

            def stage_k(h):
                nc.scalar.activation(stage["qr"][0][:], flat(q_rot[:, bass.ds(h // 2, 1), :]), ACT.Copy)
                nc.scalar.activation(stage["k"][0][:], flat(k_nope[:, bass.ds(h, 1), :]), ACT.Copy).then_inc(k_hi_done, 1)

            def values_hi(dst, g):
                nc.scalar.activation(dst[0][:].rearrange("p (c e) -> p c e", c=NT), v_gqa[:, :, g, :], ACT.Copy).then_inc(v_hi_done, 1)

            for j in range(KV_UNITS):
                split_hi(At(KV_RAW + 3 * j), At(KV_W + j))
                if j % 2 and j >= 3:
                    b = 6 + (j - 3) // 2
                    act.wait_ge(w_used, KV_W if b == 6 else KV_W + 2 * (b - 6))
                    copy_out(b)
                if j == 4:
                    nc.scalar.activation(kg_hi[:], k_gqa[:], ACT.Copy).then_inc(kg_hi_done, 1)
                if j == 5:
                    stage_q(0, 0, 0)
                    values_hi(stage["v"], 0)
            act.wait_ge(kg_ready, 1)
            values_hi(vg1, 1)
            split_hi(*at_out(0, 0))
            act.wait_ge(w_used, KV_W + 6)
            copy_out(9)
            split_hi(*at_out(0, 1))
            split_hi(*at_out(0, 2))
            act.wait_ge(w_used, KV_W + 8)
            copy_out(10)
            split_hi(*at_out(0, 3))

            def out_his(n, js):
                for j in js:
                    split_hi(*at_out(n, j))

            def stage_values(h):
                nc.scalar.activation(stage["v"][0][:].rearrange("p (c e) -> p c e", c=NT), v_lat[:, :, bass.ds(h, 1), :].rearrange("p t a e -> p t (a e)"),
                                     ACT.Copy).then_inc(v_hi_done, 1)

            def exp(grp, t, H):
                act.wait_ge(nb_ready, H * 4 + (t + 1))
                nc.scalar.activation(prob[:, t, :], bank[t][:], ACT.Exp, bias=nbias[:, t:t + 1],
                                     scale=SCALE_B if grp else SCALE_A, accum_out=total[:, t:t + 1]).then_inc(exp_done, 1)

            def head_out(H):
                nc.scalar.activation(flat(q_o[:, bass.ds(H - 1, 1), :]), bank[6][:], ACT.Copy)

            def head_squares(H):
                act.wait_ge(sq_ready, H - 1)
                nc.scalar.activation(sq[:], bank[6][:], ACT.Square).then_inc(o_done, 1)

            def turned_hi(t, H):
                act.wait_ge(p_turned, H * 4 + (t + 1))
                nc.scalar.activation(pt_hi[:, :, t * P:(t + 1) * P], bank[TURN_BANK[t]][:].rearrange("p (c n) -> p c n", c=NT), ACT.Copy).then_inc(pt_hi_done, 1)

            def attend(cur, nxt, after, first=False):
                H = cur[2]
                act.wait_ge(pv_done, H)
                if cur[0]:
                    stage_values(cur[1])
                elif not first:
                    head_out(H)
                turned_hi(0, H)
                turned_hi(1, H)
                if not first:
                    if cur[0]:
                        head_out(H)
                    head_squares(H)
                turned_hi(2, H)
                if nxt:
                    exp(nxt[0], 0, nxt[2])
                turned_hi(3, H)
                if nxt:
                    exp(nxt[0], 1, nxt[2])
                    exp(nxt[0], 2, nxt[2])
                if after:
                    stage_q(*after)
                if nxt:
                    exp(nxt[0], NT - 1, nxt[2])
                if after and after[0]:
                    stage_k(after[1])

            A = lambda h: (0, h, h)
            B = lambda h: (1, h, h + HEADS)
            for t in range(NT):
                exp(0, t, 0)
            stage_q(*A(1))
            attend(A(0), A(1), A(2), first=True)
            with act.Fori(1, HEADS - 2) as h:
                attend(A(h), A(h + 1), A(h + 2))
            attend(A(HEADS - 2), A(HEADS - 1), B(0))
            attend(A(HEADS - 1), B(0), B(1))
            with act.Fori(0, HEADS - 2) as h:
                attend(B(h), B(h + 1), B(h + 2))
            attend(B(HEADS - 2), B(HEADS - 1), None)
            attend(B(HEADS - 1), None, None)
            act.wait_ge(pv_done, 2 * HEADS)
            head_out(2 * HEADS)
            head_squares(2 * HEADS)

            act.wait_ge(s_done, 4 * 2 * HEADS)
            act.wait_ge(pt_done, 4 * 2 * HEADS)
            for k in range(KD):
                if k == KD - 1:
                    act.wait_ge(o_done, 2 * HEADS)
                nc.scalar.activation(o_hi[:, k, :], q_o[:, k, :], ACT.Copy, scale=gains[:, 3 * KD + k:3 * KD + k + 1]).then_inc(o_hi_done, 1)
            act.wait_ge(r_var, 1)
            nc.scalar.activation(stat_s[:, 0:2, :], stat_v[:, 0:2, :], ACT.Sqrt).then_inc(r_sqrt, 1)

            def a_part(n):
                act.wait_ge(r_ready, 1)
                if isinstance(n, int):
                    act.wait_ge(w_used, OUT_W + OUT_W_N * n + 4)
                else:
                    act.wait_ge(w_used, n * OUT_W_N + (OUT_W + 4))
                act.wait_ge(z_done, n * 4)
                for t in range(NT):
                    nc.scalar.activation(part[:, t, :], bank[t][:], ACT.Copy, scale=r_out[:, 0, t:t + 1]).then_inc(a_out, 1)

            def square(n, t):
                act.wait_ge(z_done, n * 4 + (t + 1))
                dst = row_sq[:, t, bass.ds(n, 1)]
                nc.scalar.activation(part[:, t, :], part[:, t, :], ACT.Square, accum_out=dst).then_inc(row_done, 1)

            with act.Fori(0, NB - 1) as n:
                out_his(n, range(4, 8))
                a_part(n)
                for j in range(4):
                    split_hi(At(OUT_RAW + OUT_RAW_N + 3 * j, n, OUT_RAW_N), At(OUT_W + OUT_W_N + j, n, OUT_W_N))
                for t in range(NT):
                    square(n, t)
            out_his(NB - 1, range(4, 8))
            a_part(NB - 1)

            def root(count, t, c):
                act.wait_ge(x1_var, count)
                nc.scalar.activation(stat_s[:, t, c:c + 1], stat_v[:, t, c:c + 1], ACT.Sqrt).then_inc(x1_sqrt, 1)

            for t in range(NT):
                square(NB - 1, t)
                root(max(2 * t, 1), t, 0)
                if t == NT - 2:
                    act.wait_ge(gm_reduced, 1)
                    for n in range(NB):
                        nc.scalar.activation(gm_acc[:, n * COLS:(n + 1) * COLS], bank[n][:], ACT.Copy).then_inc(gm_copied, 1)
                if t == NT - 1:
                    split_hi(*at_mlp(0, 0))
                if t:
                    root(2 * t + 1, t - 1, 1)
                act.wait_ge(x1_ready, t + 1)
                act.dma_start(x1_d[t], x_res[:, t, :]).then_inc(x1_saved, 16)
                nc.scalar.activation(z_tok[:, t, :], x_res[:, t, :], ACT.Square, accum_out=stat[:, t, 1:2]).then_inc(x1_sq, 1)
            root(2 * NT, NT - 1, 1)
            for k in range(KD):
                if k % 2 == 0:
                    src, g, b = bank[k if k < 8 else 4 + k % 4][:], gsc_m[:, k:k + 1], shf_m[:, k:k + 1]
                    act.wait_ge(xn_turned, k + 1)
                    if k >= 4:
                        act.wait_ge(h2_ready, k - 3)
                    nc.scalar.activation(h2_f32[k % 4][:], src, ACT.Identity, scale=g, bias=b)
                    nc.scalar.activation(h2_hi[:, k, :], src, ACT.Identity, scale=g, bias=b).then_inc(h2_hi_done, 1)
                else:
                    act.wait_ge(h2_mid, k // 2 + 1)
                    nc.scalar.activation(h2_hi[:, k, :], h2_f32[k % 4][:], ACT.Copy).then_inc(h2_hi_done, 1)
                for j in FIRST_AFTER.get(k, ()):
                    split_hi(*at_mlp(0, j))

            def relu_square(g, f):
                n0 = f * 4
                def relu(c):
                    nc.scalar.activation(tmp_u[c % 2][:], sets[f][c][:], ACT.Relu).then_inc(relu_done, 1)
                def square_hi(c):
                    act.wait_ge(y_done, g * FCH + (n0 + c + 1))
                    nc.scalar.activation(y_hi[:, n0 + c, :], tmp_y[c % 2][:], ACT.Copy).then_inc(y_hi_done, 1)
                relu(0)
                relu(1)
                for c in range(4):
                    square_hi(c)
                    if c + 2 < 4:
                        relu(c + 2)

            def mlp_group(g, first=False, last=False):
                for j in range(FIRST_SPLIT if first else 0, MLP_N):
                    r, w = at_mlp(g, j)
                    split_hi(r, w)
                    if j == UNITS_D + 3:
                        act.wait_ge(w_used, w.count(1, 1 - 4))
                        act.wait_ge(y_ready, g * FCH)
                        relu_square(g, 0)
                    if j == UP_UNITS + 3:
                        act.wait_ge(w_used, w.count(1, 1 - 4))
                        relu_square(g, 1)
                    if last and j > UP_UNITS + 3 and (j - UP_UNITS) % DN_U == DN_U - 1:
                        y_squares((j - UP_UNITS) // DN_U - 1)

            def y_squares(n):
                for t in range(NT):
                    act.wait_ge(mlp_free, LAST_ADDS + 4 * n + t + 1)
                    act.wait_ge(y_sq, 4 * n + t)
                    nc.scalar.activation(sq_junk[:], y_acc[:, t, n * COLS:(n + 1) * COLS], ACT.Square,
                                         accum_out=row_sq[:, t, n:n + 1]).then_inc(y_sq, 1)

            act.wait_ge(x1_saved, 16 * NT)
            mlp_group(0, first=True)
            with act.Fori(1, GROUPS - 1) as g:
                mlp_group(g)
            mlp_group(GROUPS - 1, last=True)
            y_squares(NB - 1)
            act.wait_ge(y_var, 1)
            nc.scalar.activation(stat_s[:, :, 2:3], stat_v[:, :, 2:3], ACT.Sqrt).then_inc(y_sqrt, 1)

        @block.vector
        def _(dve):
            own = Chain(dve, dve_own)
            tt, ts, stt = nc.vector.tensor_tensor, nc.vector.tensor_scalar, nc.vector.scalar_tensor_tensor

            def split_lo(r, w, pairs=None):
                dve.wait_ge(hi_ready, w.count(1, 1))
                for dst, src, high in (pairs or [(lo[w.slot()][:], raw[r.slot()][:], hi[w.slot()][:])]):
                    ins = tt(dst, src, high.bitcast(F32), ALU.subtract)
                ins.then_inc(raw_used, 1)

            def modulate(at, j, acc):
                wait_raw(dve, at)
                for q in range(QROWS):
                    k = QROWS * j + q
                    w = raw[at.slot()][:, q, :]
                    if k == 0:
                        ins = ts(acc, w, silu_c[:, 0:1], None, ALU.mult)
                    else:
                        ins = stt(acc, w, silu_c[:, k:k + 1], acc, ALU.mult, ALU.add)
                    if q == QROWS - 1:
                        ins.then_inc(raw_used, 1)
                        dve.wait_ge(raw_used, at.count(1, 1))
                    else:
                        own.step(ins)

            for n, dst in ((0, gains), (1, bias)):
                dve.wait_ge(vec_turned, n + 1)
                width = 3 * KD + 2 * HEADS + KR if n == 0 else 6 * KD
                nc.vector.tensor_copy(dst[:], bank[4 + n][:, 0:width]).then_inc(vec_ready, 1)
            dve.wait_ge(exp_c, 1)
            own.step(ts(silu_t[:], silu_t[:], 1.0, None, ALU.add))
            own.step(nc.vector.reciprocal(silu_t[:], silu_t[:]))
            own.step(tt(silu_c[:], gains[:, 0:KD], silu_t[:], ALU.mult))

            pairs = 0

            def modulate_pairs(cb, g, between):
                nonlocal pairs
                acc = start_acc[2 * (cb % 2) + g]
                for j in range(UNITS_D):
                    at = At(start_mod(cb, g, j))
                    wait_raw(dve, at)
                    for q in range(QROWS):
                        k, w = QROWS * j + q, raw[at.slot()][:, q, :]
                        if j == 0:
                            ins = ts(acc[:, q, :], w, silu_c[:, k:k + 1], None, ALU.mult)
                        else:
                            if q == 0:
                                dve.wait_ge(pair_own, pairs)
                            else:
                                dve.wait_ge(raw_used, at.const)
                            ins = stt(acc[:, q, :], w, silu_c[:, k:k + 1], acc[:, q, :], ALU.mult, ALU.add)
                        if q == 0:
                            ins.then_inc(pair_own, 1)
                            pairs += 1
                        else:
                            ins.then_inc(raw_used, 1)
                    if j == UNITS_D - 1:
                        dve.wait_ge(pair_own, pairs)
                        dve.wait_ge(raw_used, at.const + 1)
                        dve.sem_inc(mod_summed, 1)
                    between(j)

            def columns(cb):
                dve.wait_ge(mod_reduced, cb + 1)
                s = cb % 2
                own.step(tt(gsc_a[:, s, :], bank[5][:, 0:4], bias[:, KD + 4 * cb:KD + 4 * cb + 4], ALU.add))
                tt(shf_a[:, s, :], bank[5][:, 4:8], bias[:, 4 * cb:4 * cb + 4], ALU.add).then_inc(mod_read, 1)
                stt(gsc_a[:, s, :], gsc_a[:, s, :], 1.0, gains[:, KD + 4 * cb:KD + 4 * cb + 4], ALU.add, ALU.mult).then_inc(cols_ready, 1)

            def start_w_lo(cb, j):
                at, w = At(start_w(cb, j)), At(START_W * cb + j)
                if j < 2:
                    split_lo(at, w)
                else:
                    four = lambda t: t[:].rearrange("p q n -> p (q n)")[:, 0:4 * P].rearrange("p (k m e) -> p k m e", k=4, m=2)
                    src = raw[at.slot()][:].rearrange("p q n -> p (q n)")[:, 0:4 * ROPE_B].rearrange("p (k e) -> p k e", k=4)
                    split_lo(at, w, [(four(lo[w.slot()])[:, :, m, :], src, four(hi[w.slot()])[:, :, m, :]) for m in range(2)])

            def norm_x(j):
                if j == 2:
                    dve.wait_ge(x_sq, NT)
                    ts(stat_v[:, :, 0:1], stat[:, :, 0:1], 1.0 / D, EPS, ALU.mult, ALU.add).then_inc(x_var, 1)
                if j == 3:
                    dve.wait_ge(x_sqrt, 1)
                    own.step(nc.vector.reciprocal(rstd[:, :, 0:1], stat_s[:, :, 0:1]))
                    for t in range(NT):
                        ts(x_tok[:, t, :], x_tok[:, t, :], rstd[:, t, 0:1], None, ALU.mult).then_inc(x_normed, 1)

            def h_between(cb):
                return lambda j: columns(cb - 1) if j == 3 else None

            def w_between(cb):
                return lambda j: start_w_lo(cb - 1, START_W_AFTER[j]) if j in START_W_AFTER else None

            for cb in range(NB):
                modulate_pairs(cb, 0, h_between(cb) if cb else lambda j: None)
                modulate_pairs(cb, 1, w_between(cb) if cb else norm_x)
            start_w_lo(NB - 1, 0)
            columns(NB - 1)
            for j in range(1, 3):
                start_w_lo(NB - 1, j)

            def fold(g):
                own.step(tt(tab_g[:, 0], tab_a[:, 0], g[:].unsqueeze(1).broadcast_to([P, NT, P]), ALU.mult))
                swap = lambda x, s: x.rearrange("p (r s e) -> p r s e", r=2, s=2)[:, :, s, :]
                for s in range(2):
                    own.step(tt(tab_g[:, 1].rearrange("p t (r s e) -> p t r s e", r=2, s=2)[:, :, :, s, :],
                                tab_a[:, 1].rearrange("p t (r s e) -> p t r s e", r=2, s=2)[:, :, :, s, :],
                                swap(g[:], 1 - s).unsqueeze(1).broadcast_to([P, NT, 2, 32]), ALU.mult))

            def rope(t, heads, table, width):
                e = width // 4
                x = tok[:, t, 0:heads * width].rearrange("p (h d) -> p h d", h=heads)
                ca = tmp[0][:, 0:heads * width].rearrange("p (h d) -> p h d", h=heads)
                cos = table[:, 0, t, :].unsqueeze(1).broadcast_to([P, heads, width])
                tt(ca, x, cos, ALU.mult)
                for s in range(2):
                    for r in range(2):
                        at, of = r * 2 * e + s * e, r * 2 * e + (1 - s) * e
                        sin = table[:, 1, t, at:at + e].unsqueeze(1).broadcast_to([P, heads, e])
                        ins = tt(tmp[1][:, 0:heads * width].rearrange("p (h d) -> p h d", h=heads)[:, :, at:at + e], x[:, :, of:of + e], sin, ALU.mult)
                own.step(ins)
                tt(tok[:, t, 0:heads * width], tmp[0][:, 0:heads * width], tmp[1][:, 0:heads * width], ALU.add).then_inc(tok_ready, 1)

            for b in range(1, PROJ_BLOCKS + 1):
                heads = {2: 2, 3: 4, 4: 4, 5: 8}.get(b)
                for j in range(UNITS_D):
                    r = PROJ_RAW + 2 * UNITS_D * (b - 1) + 2 * j
                    split_lo(At(r), At(PROJ_W + UNITS_D * (b - 1) + j))
                    if j == 0 and b >= 3:
                        g = b - 3
                        dve.wait_ge(mod_reduced, NB + g + 1)
                        nc.vector.tensor_copy(mod_m[:, 4 * g:4 * g + 4], sets[b % 2][0][:, 0:4]).then_inc(mod_read, 1)
                    modulate(At(r + 1), j, mod_acc[(b - 1) % 2][:])
                    if j == UNITS_D - 1:
                        dve.sem_inc(mod_summed, 1)
                    if b == 1:
                        if j == 3:
                            dve.wait_ge(c_sq, NT)
                            ts(stat_v[:, :, 0:1], stat[:, :, 0:1], 1.0 / RANK, EPS, ALU.mult, ALU.add).then_inc(var_ready, 1)
                        if j == 4:
                            dve.wait_ge(sqrt_ready, 1)
                            nc.vector.reciprocal(rstd[:, :, 0:1], stat_s[:, :, 0:1]).then_inc(rstd_ready, 1)
                        if j == 6:
                            dve.wait_ge(kr_turned, 1)
                            dve.wait_ge(tab_landed, 16 * 6)
                            own.step(tt(tmp[0][:], tmp[0][:], tab_t[:, 0], ALU.mult))
                            own.step(tt(tmp[1][:], bank[0][:], tab_t[:, 1], ALU.mult))
                            tt(tmp[0][:], tmp[0][:], tmp[1][:], ALU.add).then_inc(kr_sum, 1)
                        if j == 7:
                            dve.wait_ge(kr_hi_done, 1)
                            tt(kr_lo[0:64, 0, :], tmp[0][0:64, :], kr_hi[0:64, 0, :].bitcast(F32), ALU.subtract)
                            tt(kr_lo[64:128, 1, :], tmp[0][64:128, :], kr_hi[64:128, 1, :].bitcast(F32), ALU.subtract).then_inc(kr_ready, 1)
                            dve.wait_ge(kr_ready, 1)
                            fold(g_k)
                    elif heads:
                        if j == 3 and b <= 4:
                            for t in range(NT):
                                dve.wait_ge(copied, 4 * (b - 1) + t + 1)
                                n = heads * P
                                own.step(tt(tmp[t % 2][:, 0:n], tok[:, t, 0:n], tok[:, t, 0:n], ALU.mult))
                                own.step(nc.vector.tensor_reduce(stat[:, t, 0:heads], tmp[t % 2][:, 0:n].rearrange("p (h d) -> p h d", h=heads), AX.X, ALU.add))
                            ts(stat_v[:, :, 0:heads], stat[:, :, 0:heads], 1.0 / P, EPS, ALU.mult, ALU.add).then_inc(var_ready, 1)
                        if j == 4 and b <= 4:
                            dve.wait_ge(sqrt_ready, b)
                            own.step(nc.vector.reciprocal(rstd[:, :, 0:heads], stat_s[:, :, 0:heads]))
                            if b == 3:
                                fold(g_q)
                        if j >= 4:
                            t = j - 4
                            dve.wait_ge(copied, 4 * (b - 1) + t + 1)
                            if b <= 4:
                                x = tok[:, t, 0:heads * P].rearrange("p (h d) -> p h d", h=heads)
                                own.step(tt(x, x, rstd[:, t, 0:heads].unsqueeze(2).broadcast_to([P, heads, P]), ALU.mult))
                                rope(t, heads, tab_g, P)
                            else:
                                rope(t, heads, tab_b, ROPE_B)
                if b == 6:
                    for k in range(KR):
                        dve.wait_ge(c_hi_done, k + 1)
                        tt(c_lo[:, k, :], ckv[:, k, :], c_hi[:, k, :].bitcast(F32), ALU.subtract).then_inc(c_ready, 1)

            flat = lambda x: x.rearrange("p a n -> p (a n)")

            def stage_q(grp, h, H):
                dve.wait_ge(q_hi_done, H + 1)
                ins = tt(stage["q"][1][:], flat(q_o[:, bass.ds(h + grp * HEADS, 1), :]), stage["q"][0][:].bitcast(F32), ALU.subtract)
                if not grp:
                    ins.then_inc(qk_ready, 1)

            def stage_k(h):
                dve.wait_ge(k_hi_done, h + 1)
                tt(stage["qr"][1][:], flat(q_rot[:, bass.ds(h // 2, 1), :]), stage["qr"][0][:].bitcast(F32), ALU.subtract)
                tt(stage["k"][1][:], flat(k_nope[:, bass.ds(h, 1), :]), stage["k"][0][:].bitcast(F32), ALU.subtract).then_inc(qk_ready, 1)

            def values_lo(dst, g, n):
                dve.wait_ge(v_hi_done, n)
                cut = lambda x: x.rearrange("p (c e) -> p c e", c=NT)
                tt(cut(dst[1][:]), v_gqa[:, :, g, :], cut(dst[0][:].bitcast(F32)), ALU.subtract).then_inc(v_ready, 1)

            for j in range(KV_UNITS):
                split_lo(At(KV_RAW + 3 * j), At(KV_W + j))
                if j == 5:
                    dve.wait_ge(kg_hi_done, 1)
                    tt(kg_lo[:], k_gqa[:], kg_hi[:].bitcast(F32), ALU.subtract).then_inc(kg_ready, 1)
                if j == 6:
                    stage_q(0, 0, 0)
                    values_lo(stage["v"], 0, 1)
                for m in range(2):
                    g, jj = divmod(2 * j + m, UNITS_D)
                    if jj == 0 and g == 0:
                        dve.wait_ge(mod_reduced, NB + 5)
                        nc.vector.tensor_copy(mod_m[:, 16:20], sets[1][0][:, 0:4]).then_inc(mod_read, 1)
                    modulate(At(KV_RAW + 3 * j + 1 + m), jj, mod_acc[(0, 2)[g]][:])
                    if jj == UNITS_D - 1:
                        dve.sem_inc(mod_summed, 1)

            def modulate_out(n, j, at=None):
                at = at or at_out(n, j)[0]
                for m in range(2):
                    if j < 4:
                        acc = ga_acc[:, bass.ds(n & 1, 1), :].rearrange("p a n -> p (a n)") if not isinstance(n, int) else ga_acc[:, n & 1, :]
                    else:
                        acc = gm_acc[:, bass.ds(n * COLS, COLS)]
                    modulate(at.plus(1 + m), 2 * (j % 4) + m, acc)
                if j == 3:
                    dve.sem_inc(ga_summed, 1)

            def out_units(n, js):
                for j in js:
                    split_lo(*at_out(n, j))
                    modulate_out(n, j)

            def next_out_units(n):
                for j in range(4):
                    r = At(OUT_RAW + OUT_RAW_N + 3 * j, n, OUT_RAW_N)
                    split_lo(r, At(OUT_W + OUT_W_N + j, n, OUT_W_N))
                    if j == 2:
                        combine(n)
                    modulate_out(n + 1, j, r)

            values_lo(vg1, 1, 2)
            out_units(0, range(2))
            dve.wait_ge(mod_reduced, NB + 8)
            own.step(nc.vector.tensor_copy(mod_m[:, 20:32], bank[7][:, 0:12]))
            dve.sem_inc(mod_read, 1)
            out_units(0, range(2, 3))

            def stage_values(h, H):
                dve.wait_ge(v_hi_done, H - (HEADS - 3))
                src = v_lat[:, :, bass.ds(h, 1), :]
                cut = lambda x: x.rearrange("p (c e) -> p c e", c=NT)
                tt(cut(stage["v"][1][:]), src.rearrange("p t a e -> p t (a e)"), cut(stage["v"][0][:].bitcast(F32)), ALU.subtract).then_inc(v_ready, 1)

            def row_max(grp, t, H):
                dve.wait_ge(s_done, H * 4 + (t + 1))
                own.step(nc.vector.reduce_max(top[:, t:t + 1], bank[t][:], AX.X))
                ts(nbias[:, t:t + 1], top[:, t:t + 1], -(SCALE_B if grp else SCALE_A), None, ALU.mult).then_inc(nb_ready, 1)

            def invert(t, H):
                dve.wait_ge(exp_done, H * 4 + (t + 1))
                nc.vector.reciprocal(rtotal[:, t:t + 1], total[:, t:t + 1]).then_inc(rt_ready, 1)

            def turned_lo(t, H):
                dve.wait_ge(pt_hi_done, H * 4 + (t + 1))
                tt(pt_lo[:, :, t * P:(t + 1) * P], bank[TURN_BANK[t]][:].rearrange("p (c n) -> p c n", c=NT),
                   pt_hi[:, :, t * P:(t + 1) * P].bitcast(F32), ALU.subtract).then_inc(pt_done, 1)

            def attend(cur, nxt, after):
                H = cur[2]
                if cur[0]:
                    stage_values(cur[1], H)
                turned_lo(0, H)
                if nxt:
                    row_max(nxt[0], 0, nxt[2])
                turned_lo(1, H)
                turned_lo(2, H)
                if nxt:
                    row_max(nxt[0], 1, nxt[2])
                    invert(0, nxt[2])
                turned_lo(3, H)
                if nxt:
                    for t in (2, 3):
                        row_max(nxt[0], t, nxt[2])
                        invert(t - 1, nxt[2])
                if after and after[0]:
                    stage_q(*after)
                if nxt:
                    invert(NT - 1, nxt[2])
                if after and not after[0]:
                    stage_q(*after)
                if after and after[0]:
                    stage_k(after[1])

            A = lambda h: (0, h, h)
            B = lambda h: (1, h, h + HEADS)
            split_lo(*at_out(0, 3))
            for t in range(NT):
                row_max(0, t, 0)
                if t:
                    invert(t - 1, 0)
            invert(NT - 1, 0)
            stage_q(*A(1))
            modulate_out(0, 3)
            attend(A(0), A(1), A(2))
            with dve.Fori(1, HEADS - 2) as h:
                own.enter(h - 1, NT)
                attend(A(h), A(h + 1), A(h + 2))
            own.leave(HEADS - 3)
            attend(A(HEADS - 2), A(HEADS - 1), B(0))
            attend(A(HEADS - 1), B(0), B(1))
            with dve.Fori(0, HEADS - 2) as h:
                own.enter(h, NT)
                attend(B(h), B(h + 1), B(h + 2))
            own.leave(HEADS - 2)
            attend(B(HEADS - 2), B(HEADS - 1), None)
            attend(B(HEADS - 1), None, None)

            own.step(tt(gsc_m[:], mod_m[:, 0:KD], bias[:, SC_M // P:SC_M // P + KD], ALU.add))
            own.step(stt(gsc_m[:], gsc_m[:], 1.0, gains[:, 2 * KD:3 * KD], ALU.add, ALU.mult))
            tt(shf_m[:], mod_m[:, KD:2 * KD], bias[:, SH_M // P:SH_M // P + KD], ALU.add)

            for k in range(KD):
                dve.wait_ge(o_hi_done, k + 1)
                stt(o_lo[:, k, :], q_o[:, k, :], gains[:, 3 * KD + k:3 * KD + k + 1], o_hi[:, k, :].bitcast(F32), ALU.mult, ALU.subtract).then_inc(o_ready, 1)
            dve.wait_ge(sq_reduced, 1)
            own.step(ts(stat_v[:, 0:2, :], bank[7][:, 16:24].rearrange("p (g t) -> p g t", g=2), 1.0 / (HEADS * P), EPS, ALU.mult, ALU.add))
            dve.sem_inc(r_var, 1)
            dve.wait_ge(r_sqrt, 1)
            nc.vector.reciprocal(r_out[:], stat_s[:, 0:2, :]).then_inc(r_ready, 1)
            dve.wait_ge(r_ready, 1)

            def combine(n):
                dve.wait_ge(ga_reduced, n + 1)
                dve.wait_ge(rows_landed, n * 32 + 32)
                own.step(tt(comb[:], bank[0][:], rows[:, 0, :], ALU.add))
                tt(comb[:], comb[:], rows[:, 1, :], ALU.mult).then_inc(comb_ready, 1)
                dve.wait_ge(comb_ready, n + 1)

            def sum_tile(n, t):
                dve.wait_ge(a_out, n * 4 + (t + 1))
                stt(part[:, t, :], bank[4 + t][:], r_out[:, 1, t:t + 1], part[:, t, :], ALU.mult, ALU.add).then_inc(b_sum, 1)

            def gate_tile(n, t):
                dve.wait_ge(b_sum, n * 4 + (t + 1))
                tt(z_tok[:, t, bass.ds(n * COLS, COLS)], part[:, t, :], comb[:], ALU.mult).then_inc(z_done, 1)

            def b_part(n):
                dve.wait_ge(w_used, n * OUT_W_N + (OUT_W + OUT_W_N))
                for t in range(NT):
                    sum_tile(n, t)
                for t in range(NT):
                    gate_tile(n, t)

            with dve.Fori(0, NB - 1) as n:
                own.enter(n, 8 + 8 + 1)
                out_units(n, range(4, 8))
                next_out_units(n)
                b_part(n)
            own.leave(NB - 1)
            out_units(NB - 1, range(4, 8))
            combine(NB - 1)

            def diagonal(t):
                dve.wait_ge(x1_sq, t + 1)
                ts(stat_v[:, t, 1:2], stat[:, t, 1:2], 1.0 / D, EPS, ALU.mult, ALU.add).then_inc(x1_var, 1)
                dve.wait_ge(x1_sqrt, min(2 * t + 3, 2 * NT))
                own.step(nc.vector.reciprocal(rstd[:, t, 1:2], stat_s[:, t, 1:2]))
                ts(diag[:, t, :], ident[:], rstd[:, t, 1:2], None, ALU.mult).then_inc(xn_ready, 1)

            def residual(t):
                dve.wait_ge(row_done, (NB - 1) * 4 + t + 1)
                own.step(nc.vector.tensor_reduce(stat[:, t, 0:1], row_sq[:, t, :], AX.X, ALU.add))
                ts(stat_v[:, t, 0:1], stat[:, t, 0:1], 1.0 / D, EPS, ALU.mult, ALU.add).then_inc(x1_var, 1)
                dve.wait_ge(x1_sqrt, max(2 * t, 1))
                own.step(nc.vector.reciprocal(rstd[:, t, 0:1], stat_s[:, t, 0:1]))
                dve.wait_ge(res_landed, 16 * (t + 1))
                stt(x_res[:, t, :], z_tok[:, t, :], rstd[:, t, 0:1], x_res[:, t, :], ALU.mult, ALU.add).then_inc(x1_ready, 1)

            for t in range(NT):
                if t < NT - 1:
                    dve.wait_ge(b_tile, t + 1)
                else:
                    dve.wait_ge(w_used, MLP_W)
                sum_tile(NB - 1, t)
                gate_tile(NB - 1, t)
                residual(t)
                if t:
                    diagonal(t - 1)
            split_lo(*at_mlp(0, 0))
            diagonal(NT - 1)
            for k in range(KD):
                if k % 2 == 0:
                    dve.wait_ge(xn_turned, k + 2)
                    k1 = k + 1
                    ts(h2_f32[k1 % 4][:], bank[k1 if k1 < 8 else 4 + k1 % 4][:], gsc_m[:, k1:k1 + 1], shf_m[:, k1:k1 + 1],
                       ALU.mult, ALU.add).then_inc(h2_mid, 1)
                else:
                    dve.wait_ge(h2_mid, k // 2 + 1)
                dve.wait_ge(h2_hi_done, k + 1)
                tt(h2_lo[:, k, :], h2_f32[k % 4][:], h2_hi[:, k, :].bitcast(F32), ALU.subtract).then_inc(h2_ready, 1)
                for j in FIRST_AFTER.get(k, ()):
                    split_lo(*at_mlp(0, j))

            dve.sem_inc(mlp_free, 4)

            def squares(g, f):
                n0 = 4 * f
                for c in range(4):
                    dve.wait_ge(relu_done, g * FCH + (n0 + c + 1))
                    stt(tmp_y[c % 2][:], sets[f][c][:], 0.0, tmp_u[c % 2][:], ALU.max, ALU.mult).then_inc(y_done, 1)
                    dve.wait_ge(y_hi_done, g * FCH + (n0 + c + 1))
                    tt(y_lo[:, n0 + c, :], tmp_y[c % 2][:], y_hi[:, n0 + c, :].bitcast(F32), ALU.subtract).then_inc(y_ready, 1)
                    dve.wait_ge(y_ready, g * FCH + (n0 + c + 1))
                dve.sem_inc(mlp_free, 4)

            def down_add(n):
                for t in range(NT):
                    dst = y_acc[:, t, n * COLS:(n + 1) * COLS]
                    tt(dst, sets[n % 2][t][:], dst, ALU.add).then_inc(mlp_free, 1)

            def gate(n):
                cols = slice(n * COLS, (n + 1) * COLS)
                for t in range(NT):
                    dve.wait_ge(mlp_free, LAST_ADDS + 4 * n + t + 1)
                    tt(z_out[:, t, cols], y_acc[:, t, cols], gm_acc[:, cols], ALU.mult).then_inc(z_ready, 1)

            def mlp_group(g, first=False, last=False):
                for j in range(FIRST_SPLIT if first else 0, MLP_N):
                    r, w = at_mlp(g, j)
                    split_lo(r, w)
                    if j == 3:
                        dve.wait_ge(w_used, w.count(1, 1 - 4))
                        down_add(NB - 1)
                    if j == UNITS_D + 3:
                        squares(g, 0)
                    if j == UP_UNITS + 3:
                        squares(g, 1)
                        if first:
                            dve.wait_ge(y_zero, 1)
                    if j > UP_UNITS + 3 and (j - UP_UNITS) % DN_U == DN_U - 1:
                        n = (j - UP_UNITS) // DN_U - 1
                        dve.wait_ge(w_used, w.count(1, 1 - 4))
                        down_add(n)
                        if last:
                            if n == 0:
                                dve.wait_ge(comb_m_ready, 1)
                            gate(n)

            mlp_group(0, first=True)
            with dve.Fori(1, GROUPS - 1) as g:
                mlp_group(g)
            mlp_group(GROUPS - 1, last=True)
            dve.wait_ge(w_used, MLP_W + MLP_N * GROUPS)
            down_add(NB - 1)
            gate(NB - 1)

            dve.wait_ge(y_sq, NB * NT)
            own.step(nc.vector.tensor_reduce(stat[:, :, 2:3], row_sq[:], AX.X, ALU.add))
            ts(stat_v[:, :, 2:3], stat[:, :, 2:3], 1.0 / D, EPS, ALU.mult, ALU.add).then_inc(y_var, 1)
            dve.wait_ge(y_sqrt, 1)
            own.step(nc.vector.reciprocal(rstd[:, :, 2:3], stat_s[:, :, 2:3]))
            dve.wait_ge(z_ready, NB * NT)
            dve.wait_ge(x1_landed, 16 * NT)
            for t in range(NT):
                for half in range(2):
                    cols = slice(half * D // 2, (half + 1) * D // 2)
                    stt(x1_back[:, t, cols], z_out[:, t, cols], rstd[:, t, 2:3], x1_back[:, t, cols], ALU.mult, ALU.add).then_inc(out_ready, 1)

        @block.tensor
        def _(pe):
            mm = nc.tensor.matmul

            def unit_tokens(w, acc, act_hi, act_lo, k0, first, last):
                s = w.slot()
                for t in range(NT):
                    for q in range(QROWS):
                        k = k0 + q
                        xh, xl = act_hi[:, k, t * P:(t + 1) * P], act_lo[:, k, t * P:(t + 1) * P]
                        mm(acc[t][:], xh, hi[s][:, q, :], start=first and q == 0, stop=False)
                        mm(acc[t][:], xh, lo[s][:, q, :], start=False, stop=False)
                        ins = mm(acc[t][:], xl, hi[s][:, q, :], start=False, stop=last and q == QROWS - 1)
                ins.then_inc(w_used, 1)

            def unit_columns(w, acc, act_hi, act_lo, k0, first, last):
                s = w.slot()
                for n in range(4):
                    for q in range(QROWS):
                        k = k0 + q
                        wh, wl = hi[s][:, q, n * P:(n + 1) * P], lo[s][:, q, n * P:(n + 1) * P]
                        mm(acc[n][:], wh, act_hi[:, k, :], start=first and q == 0, stop=False)
                        mm(acc[n][:], wh, act_lo[:, k, :], start=False, stop=False)
                        ins = mm(acc[n][:], wl, act_hi[:, k, :], start=False, stop=last and q == QROWS - 1)
                ins.then_inc(w_used, 1)

            pe.wait_ge(const_landed, 16)
            pe.wait_ge(vec_landed, 16 * 7)
            width = 3 * KD + 2 * HEADS + KR
            nc.tensor.transpose(bank[4][:, 0:width], vec_rows[0:width, 0, :], ident[0:width, 0:width]).then_inc(vec_turned, 1)
            nc.tensor.transpose(bank[5][:, 0:6 * KD], vec_rows[0:6 * KD, 1, :], ident[0:6 * KD, 0:6 * KD]).then_inc(vec_turned, 1)
            pe.wait_ge(x_normed, NT)
            for k in range(KD):
                if k >= 4:
                    pe.wait_ge(x_t_ready, k - 3)
                for t in range(NT):
                    ins = nc.tensor.transpose(bank[k % 4][:, t * P:(t + 1) * P], x_tok[:, t, k * P:(k + 1) * P], ident[:])
                ins.then_inc(x_turned, 1)
            pe.wait_ge(ones_ready, 1)
            pe.wait_ge(vec_ready, 2)

            def start_products(cb):
                w = START_W * cb
                for j in range(2):
                    pe.wait_ge(h_ready, 4 * cb + 2 * j + 2)
                    pe.wait_ge(raw_used, start_w(cb, j) + 1)
                    unit_tokens(At(w + j), sets[0], h_hi, h_lo, 4 * cb + 2 * j, cb == 0 and j == 0, cb == NB - 1 and j == 1)
                pe.wait_ge(raw_used, start_w(cb, 2) + 1)
                s = At(w + 2).slot()
                for k in range(4):
                    wh, wl = (x[s][:].rearrange("p q n -> p (q n)")[:, k * P:(k + 1) * P] for x in (hi, lo))
                    xh, xl = h_hi[:, 4 * cb + k, :], h_lo[:, 4 * cb + k, :]
                    mm(bank[4][:], wh, xh, start=cb == 0 and k == 0, stop=False)
                    mm(bank[4][:], wh, xl, start=False, stop=False)
                    ins = mm(bank[4][:], wl, xh, start=False, stop=cb == NB - 1 and k == 3)
                ins.then_inc(w_used, 1)

            def reduce_start(cb, g):
                pe.wait_ge(mod_summed, 2 * cb + g + 1)
                if cb and g == 0:
                    pe.wait_ge(mod_read, cb)
                for j in range(4):
                    for q in range(2):
                        ins = mm(bank[5][:, 4 * g + j:4 * g + j + 1], start_acc[2 * (cb % 2) + g][:, q, j * P:(j + 1) * P],
                                 ones[:, 0:1], start=q == 0, stop=q == 1)
                if g:
                    ins.then_inc(mod_reduced, 1)

            for cb in range(NB):
                reduce_start(cb, 0)
                if cb == 1:
                    pe.wait_ge(x_t_ready, KD)
                if 0 < cb < NB - 1:
                    start_products(cb - 1)
                reduce_start(cb, 1)
            start_products(NB - 2)
            start_products(NB - 1)

            def turn(b):
                if b == 0:
                    pe.wait_ge(copied, 4)
                    pe.wait_ge(kr_sum, 1)
                else:
                    pe.wait_ge(tok_ready, 4 * b)
                for n in range(TURNS[b]):
                    for t in range(NT):
                        ins = nc.tensor.transpose(sets[b % 2][n][:, t * P:(t + 1) * P], tok[:, t, n * P:(n + 1) * P], ident[:])
                    ins.then_inc(turned, 1)

            for b in range(1, PROJ_BLOCKS + 1):
                for j in range(UNITS_D):
                    r, w = PROJ_RAW + 2 * UNITS_D * (b - 1) + 2 * j, PROJ_W + UNITS_D * (b - 1) + j
                    pe.wait_ge(raw_used, r + 1)
                    if j == 0:
                        if b == 1:
                            pe.wait_ge(kr_copied, 1)
                            pe.wait_ge(mod_read, NB)
                        else:
                            pe.wait_ge(turned_out, TURNS_SUM[b - 1])
                            pe.wait_ge(copied, 4 * (b - 1))
                            if b >= 4:
                                pe.wait_ge(mod_read, NB + b - 2)
                    unit = unit_tokens if TOKENS_OUT[b] else unit_columns
                    unit(At(w), sets[b % 2], h_hi, h_lo, QROWS * j, j == 0, j == UNITS_D - 1)
                    if j == 4 and b == 1:
                        pe.wait_ge(tab_landed, 16 * 6)
                        pe.wait_ge(c_sq, 4)
                        pe.wait_ge(copied, 4)
                        mm(bank[0][:], rot[:], tmp[0][:], start=True, stop=True).then_inc(kr_turned, 1)
                    if j == 4 and b >= 2:
                        pe.wait_ge(mod_summed, 2 * NB + b - 1)
                        pe.wait_ge(copied, 4 * b)
                        for n in range(4):
                            ins = mm(sets[(b - 1) % 2][0][:, n:n + 1], mod_acc[(b - 2) % 2][:, n * P:(n + 1) * P], ones[:, 0:1], start=True, stop=True)
                        ins.then_inc(mod_reduced, 1)
                    if j == 6 and b <= 5:
                        if b >= 2:
                            pe.wait_ge(mod_read, NB + b - 1)
                        turn(b - 1)

            for i, b in enumerate((7, 8, 9, 10)):
                pe.wait_ge(copied, 4 * (b - 1))
                if b == 7:
                    pe.wait_ge(mod_read, NB + 5)
                    pe.wait_ge(c_ready, KR)
                for j in range(2):
                    pe.wait_ge(raw_used, KV_RAW + 3 * (2 * i + j) + 1)
                    unit = unit_columns if b < 9 else unit_tokens
                    unit(At(KV_W + 2 * i + j), sets[b % 2], c_hi, c_lo, 2 * j, j == 0, j == 1)
            pe.wait_ge(mod_summed, 2 * NB + 8)
            pe.wait_ge(copied, 4 * 10)
            for g, acc in ((5, 1), (6, 0), (7, 2)):
                for n in range(4):
                    c = 4 * (g - 5) + n
                    ins = mm(bank[7][:, c:c + 1], mod_acc[acc][:, n * P:(n + 1) * P], ones[:, 0:1], start=True, stop=True)
                ins.then_inc(mod_reduced, 1)
            pe.wait_ge(copied, 4 * 11)
            pe.wait_ge(kr_ready, 1)
            pe.wait_ge(kg_ready, 1)

            def scores(grp, h, H, t):
                if t == 0:
                    pe.wait_ge(qk_ready, H + 1)
                qh, ql = stage["q"]
                if grp:
                    kh, kl = (x[:] for x in stage["k"])
                else:
                    kh, kl = (x[:, bass.ds(h // 4, 1), :].rearrange("p a n -> p (a n)") for x in (kg_hi, kg_lo))
                cut = lambda x: x[:, t * P:(t + 1) * P]
                mm(bank[t][:], cut(qh), kh, start=True, stop=False)
                mm(bank[t][:], cut(qh), kl, start=False, stop=False)
                ins = mm(bank[t][:], cut(ql), kh, start=False, stop=not grp)
                if grp:
                    rh, rl = stage["qr"]
                    par = bass.ds(h & 1, 1) if not isinstance(h, int) else slice(h & 1, (h & 1) + 1)
                    krh, krl = (x[:, par, :].rearrange("p a n -> p (a n)") for x in (kr_hi, kr_lo))
                    mm(bank[t][:], cut(rh), krh, start=False, stop=False)
                    mm(bank[t][:], cut(rh), krl, start=False, stop=False)
                    ins = mm(bank[t][:], cut(rl), krh, start=False, stop=True)
                ins.then_inc(s_done, 1)

            def turn_probs(t, H):
                pe.wait_ge(p_ready, H * 4 + (t + 1))
                behind = {0: 0, 1: -2, 2: -1, 3: 1}[t]
                if not isinstance(H, int):
                    pe.wait_ge(pt_done, H * 4 + behind)
                elif H * 4 + behind > 0:
                    pe.wait_ge(pt_done, H * 4 + behind)
                for c in range(NT):
                    ins = nc.tensor.transpose(bank[TURN_BANK[t]][:, c * P:(c + 1) * P], prob[:, t, c * P:(c + 1) * P], ident[:])
                ins.then_inc(p_turned, 1)

            def attend(H, nxt, values, values_n):
                turn_probs(0, H)
                for t in range(1, NT):
                    turn_probs(t, H)
                    if nxt:
                        scores(*nxt, t - 1)
                if nxt:
                    scores(*nxt, NT - 1)
                pe.wait_ge(pt_done, H * 4 + 4)
                pe.wait_ge(v_ready, values_n)
                pe.wait_ge(o_done, H)
                vh, vl = values
                for c in range(NT):
                    v = slice(c * P, (c + 1) * P)
                    mm(bank[6][:], vh[:, v], pt_hi[:, c, :], start=c == 0, stop=False)
                    mm(bank[6][:], vh[:, v], pt_lo[:, c, :], start=False, stop=False)
                    ins = mm(bank[6][:], vl[:, v], pt_hi[:, c, :], start=False, stop=c == NT - 1)
                ins.then_inc(pv_done, 1)

            for t in range(NT):
                scores(0, 0, 0, t)
            vg0 = stage["v"]
            attend(0, (0, 1, 1), vg0, 1)
            with pe.Fori(1, HEADS // 2) as h:
                attend(h, (0, h + 1, h + 1), vg0, 1)
            with pe.Fori(HEADS // 2, HEADS - 1) as h:
                attend(h, (0, h + 1, h + 1), vg1, 2)
            attend(HEADS - 1, (1, 0, HEADS), vg1, 2)
            with pe.Fori(0, HEADS - 1) as h:
                attend(h + HEADS, (1, h + 1, h + (HEADS + 1)), stage["v"], h + 3)
            attend(2 * HEADS - 1, None, stage["v"], HEADS + 2)

            pe.wait_ge(sq_ready, 2 * HEADS - 1)
            pe.wait_ge(pt_done, 4 * 2 * HEADS)
            for g in range(2):
                for t in range(NT):
                    c = 16 + 4 * g + t
                    tile = slice(t * P, (t + 1) * P)
                    ins = mm(bank[7][:, c:c + 1], sq_sum[:, g, tile], ones[:, 0:1], start=True, stop=g == 0)
                    if g:
                        pe.wait_ge(o_done, 2 * HEADS)
                        ins = mm(bank[7][:, c:c + 1], sq[:, tile], ones[:, 0:1], start=False, stop=True)
            ins.then_inc(sq_reduced, 1)

            def wait_out(n, j):
                pe.wait_ge(raw_used, at_out(n, j)[0].count(1, 1))
                pe.wait_ge(o_ready, 2 * j + 2)
                if j == 0:
                    pe.wait_ge(comb_ready, n)
                if j == 4:
                    pe.wait_ge(z_done, n * 4)
                    pe.wait_ge(r_ready, 1)

            def spread_ga(n):
                pe.wait_ge(a_out, n * 4 + 4)
                pe.wait_ge(ga_summed, n + 1)
                src = ga_acc[:, bass.ds(n & 1, 1), :].rearrange("p a n -> p (a n)") if not isinstance(n, int) else ga_acc[:, n & 1, :]
                mm(bank[0][:], ones[:], src, start=True, stop=True).then_inc(ga_reduced, 1)

            with pe.Fori(0, NB - 1) as n:
                for j in range(UNITS_D):
                    wait_out(n, j)
                    unit_tokens(at_out(n, j)[1], sets[j // 4], o_hi, o_lo, QROWS * j, j % 4 == 0, j % 4 == 3)
                    if j == 6:
                        spread_ga(n)
            for j in range(4):
                wait_out(NB - 1, j)
                unit_tokens(at_out(NB - 1, j)[1], sets[0], o_hi, o_lo, QROWS * j, j == 0, j == 3)
            for t in range(NT):
                for j in range(4, 8):
                    if t == 0:
                        wait_out(NB - 1, j)
                    s = at_out(NB - 1, j)[1].slot()
                    for q in range(QROWS):
                        k = QROWS * j + q
                        xh, xl = o_hi[:, k, t * P:(t + 1) * P], o_lo[:, k, t * P:(t + 1) * P]
                        mm(bank[4 + t][:], xh, hi[s][:, q, :], start=k == KD // 2, stop=False)
                        mm(bank[4 + t][:], xh, lo[s][:, q, :], start=False, stop=False)
                        ins = mm(bank[4 + t][:], xl, hi[s][:, q, :], start=False, stop=k == KD - 1)
                    if t == NT - 1:
                        ins.then_inc(w_used, 1)
                    elif j == 7:
                        ins.then_inc(b_tile, 1)
                if t == 0:
                    spread_ga(NB - 1)
                if t == 2:
                    pe.wait_ge(raw_used, MLP_RAW)
                    pe.wait_ge(comb_ready, NB)
                    for n in range(NB):
                        ins = mm(bank[n][:], ones[:], gm_acc[:, n * COLS:(n + 1) * COLS], start=True, stop=True)
                    ins.then_inc(gm_reduced, 1)
            pe.wait_ge(gm_copied, NB)

            def turn_x1(k, t, out_bank):
                return mm(out_bank[:, t * P:(t + 1) * P], x_res[:, t, k * P:(k + 1) * P], diag[:, t, :], start=True, stop=True)

            for t in range(NT):
                pe.wait_ge(xn_ready, t + 1)
                for k in range(8):
                    if t == 0 and k == 4:
                        pe.wait_ge(z_done, 4 * NB)
                    ins = turn_x1(k, t, bank[k])
                    if t == NT - 1:
                        ins.then_inc(xn_turned, 1)

            def up_block(g, f, before=lambda j: None):
                for j in range(UNITS_D):
                    r, w = at_mlp(g, f * UNITS_D + j)
                    before(j)
                    pe.wait_ge(raw_used, r.count(1, 1))
                    if j == 0 and not (isinstance(g, int) and f == 0):
                        pe.wait_ge(mlp_free, g * 24 + 4 * f)
                    unit_columns(w, sets[f], h2_hi, h2_lo, QROWS * j, j == 0, j == UNITS_D - 1)

            def down_blocks(g):
                for n in range(NB):
                    for j in range(DN_U):
                        r, w = at_mlp(g, UP_UNITS + n * DN_U + j)
                        pe.wait_ge(raw_used, r.count(1, 1))
                        if n == 0:
                            pe.wait_ge(y_ready, g * FCH + 2 * j + 2)
                        if j == 0:
                            pe.wait_ge(mlp_free, g * 24 + 4 * (n + 2))
                        unit_tokens(w, sets[n % 2], y_hi, y_lo, QROWS * j, j == 0, j == DN_U - 1)

            def before_first(j):
                if j in (2, 4):
                    pe.wait_ge(h2_ready, 4 + 2 * j)
                    for k in range(4 + 2 * j, 8 + 2 * j):
                        for t in range(NT):
                            ins = turn_x1(k, t, bank[4 + k % 4])
                        ins.then_inc(xn_turned, 1)
                pe.wait_ge(h2_ready, max(4, 2 * j + 2))

            up_block(0, 0, before_first)
            up_block(0, 1)
            down_blocks(0)
            with pe.Fori(1, GROUPS) as g:
                up_block(g, 0)
                up_block(g, 1)
                down_blocks(g)

        @block.gpsimd
        def _(pool):
            own = Chain(pool, pool_own)
            tt = nc.gpsimd.tensor_tensor
            nc.gpsimd.memset(ones[:], 1.0).then_inc(ones_ready, 1)
            pool.wait_ge(ones_ready, 1)
            own.step(nc.gpsimd.memset(kr_hi[64:128, 0, :].bitcast(F32), 0.0))
            own.step(nc.gpsimd.memset(kr_hi[0:64, 1, :].bitcast(F32), 0.0))
            own.step(nc.gpsimd.memset(kr_lo[64:128, 0, :].bitcast(F32), 0.0))
            own.step(nc.gpsimd.memset(kr_lo[0:64, 1, :].bitcast(F32), 0.0))

            for k in range(KD):
                pool.wait_ge(h_hi_ready, k + 1)
                tt(h_lo[:, k, :], h_f32[k % 4][:], h_hi[:, k, :].bitcast(F32), ALU.subtract).then_inc(h_ready, 1)

            def normalise(H):
                for t in range(NT):
                    pool.wait_ge(rt_ready, H * 4 + (t + 1))
                    tt(prob[:, t, :], prob[:, t, :], rtotal[:, t:t + 1].broadcast_to([P, T]), ALU.mult).then_inc(p_ready, 1)

            def add_squares(H, grp):
                pool.wait_ge(o_done, H + 1)
                pool.wait_ge(sq_ready, H)
                tt(sq_sum[:, grp, :], sq_sum[:, grp, :], sq[:], ALU.add).then_inc(sq_ready, 1)

            pool.wait_ge(c_ready, KR)
            own.step(nc.gpsimd.memset(sq_sum[:], 0.0))
            normalise(0)
            normalise(1)
            with pool.Fori(1, HEADS + 1) as h:
                normalise(h + 1)
                add_squares(h - 1, 0)
            with pool.Fori(HEADS + 1, 2 * HEADS - 1) as h:
                normalise(h + 1)
                add_squares(h - 1, 1)
            add_squares(2 * HEADS - 2, 1)
            pool.wait_ge(sq_reduced, 1)
            for t in range(NT):
                pool.dma_start(x_res[:, t, :], x_d[t]).then_inc(res_landed, 16)
            for n in range(NB):
                if n:
                    pool.wait_ge(comb_ready, n)
                pool.dma_start(rows[:, 0, :], b_rows[:, GT_A + n * COLS:GT_A + (n + 1) * COLS].partition_broadcast(P)[:, 0, :]).then_inc(rows_landed, 16)
                pool.dma_start(rows[:, 1, :], a["g_post_attn"][:, n * COLS:(n + 1) * COLS].partition_broadcast(P)[:, 0, :]).then_inc(rows_landed, 16)
            pool.wait_ge(x1_sq, NT)
            nc.gpsimd.memset(y_acc[:], 0.0).then_inc(y_zero, 1)
            for n in range(NB):
                if n == 0:
                    pool.wait_ge(comb_ready, NB)
                pool.dma_start(rows[:, 0, :], b_rows[:, GT_M + n * COLS:GT_M + (n + 1) * COLS].partition_broadcast(P)[:, 0, :]).then_inc(rows_landed, 16)
                pool.dma_start(rows[:, 1, :], a["g_post_mlp"][:, n * COLS:(n + 1) * COLS].partition_broadcast(P)[:, 0, :]).then_inc(rows_landed, 16)
                pool.wait_ge(rows_landed, 32 * (NB + n + 1))
                pool.wait_ge(gm_copied, NB)
                dst = gm_acc[:, n * COLS:(n + 1) * COLS]
                own.step(tt(dst, dst, rows[:, 0, :], ALU.add))
                own.step(tt(dst, dst, rows[:, 1, :], ALU.mult))
            pool.sem_inc(comb_m_ready, 1)


def kernel(**inputs):
    import concourse.bacc as bacc
    from concourse.bass_utils import run_bass_kernel_spmd

    nc = bacc.Bacc("TRN2", target_bir_lowering=False, num_devices=1)
    arrays = {name: np.ascontiguousarray(v) for name, v in inputs.items()}
    arrays.update(tables())
    aps = {name: nc.dram_tensor("in_" + name, v.shape, F32, kind="ExternalInput").ap() for name, v in arrays.items()}
    out = nc.dram_tensor("out", (1, T, D), F32, kind="ExternalOutput").ap()
    x1_dram = nc.dram_tensor("x1_dram", (T, D), F32, kind="Internal").ap()
    build(nc, aps, out, x1_dram)
    r = run_bass_kernel_spmd(nc, [{"in_" + name: v for name, v in arrays.items()}], core_ids=[0])
    return r.results[0]["out"]


def tables():
    f = np.float32
    row, col = (np.arange(T) // 64).astype(f), (np.arange(T) % 64).astype(f)

    def angles(dim):
        half = dim // 2
        inv = np.power(f(10000.0), -np.arange(0, half, 2, dtype=f) / f(half)).astype(f)
        r, c = row[:, None] * inv[None], col[:, None] * inv[None]
        ang = np.concatenate([r, r, c, c], axis=-1).astype(f)
        sign = np.tile(np.repeat(np.array([-1, 1], f), dim // 4), 2)
        return np.stack([np.cos(ang), np.sin(ang) * sign]).astype(f)

    rot = np.zeros((P, P), f)
    for i in range(P):
        rot[i ^ (ROPE_B // 4), i] = 1.0
    tok_major = lambda t: np.ascontiguousarray(t.reshape(2, NT, P, -1).transpose(2, 0, 1, 3))
    b = angles(ROPE_B)
    tab_t = np.concatenate([b.transpose(2, 0, 1)] * 2, axis=0)
    return {"ident": np.eye(P, dtype=f), "rot": rot, "tab_a": tok_major(angles(P)), "tab_b": tok_major(b),
            "tab_t": np.ascontiguousarray(tab_t)}
```
